# Optimizing a Trainium2 kernel written in Bass

```python
import math
import jax
import jax.numpy as jnp
from jax import lax
import numpy as np

D_MODEL = 1024
BATCH = 1
SEQ = 1024
DEPTH = 2

GRID_W = 64
CTX_LEN = 256
N_EVEN = (DEPTH + 1) // 2
N_ODD = DEPTH // 2
EPS = 1e-6
CONV_W = 3

GLA_HEADS = 4
GLA_DK = 64
GLA_DV = 128
GLA_RANK = 16
GLA_TAU = 16.0
GLA_CHUNK = 64
GLA_QK = GLA_HEADS * GLA_DK
GLA_V = GLA_HEADS * GLA_DV

HY_WIDTH = 512
HY_EMB = 33
HY_BANDS = (HY_EMB - 1) // 2
HY_HIDDEN = 64
HY_FAST_DECAY = 0.3
HY_SLOW_DECAY = 1.5
HY_TARGET = 1e-2

EV_SPLIT = (GLA_QK, 2 * GLA_QK, 2 * GLA_QK + GLA_V, 2 * GLA_QK + 2 * GLA_V,
            2 * GLA_QK + 2 * GLA_V + GLA_RANK, 2 * GLA_QK + 2 * GLA_V + 2 * GLA_RANK)
EV_IN = 2 * GLA_QK + 2 * GLA_V + 2 * GLA_RANK + 3 * HY_WIDTH
EV_MIX = GLA_V + HY_WIDTH

SC_WIDTH = D_MODEL

N_GROUPS = 4
EXP_PER_GROUP = 8
N_EXPERTS = N_GROUPS * EXP_PER_GROUP
TOP_K = 2
D_EXPERT = 512
MOE_BLOCK = 128

kernel_name = 'hybrid_gla_hyena_shortconv_hmoe_dit'

def rmsnorm(x, g):
    xf = x.astype(jnp.float32)
    y = xf * lax.rsqrt(jnp.mean(xf * xf, axis=-1, keepdims=True) + EPS)
    return (y * g.astype(jnp.float32)).astype(x.dtype)

def modulate(x, shift, scale):
    return x * (1 + scale) + shift

def dwconv3(x, w, b=None):
    xp = jnp.pad(x, ((0, 0), (1, 1), (0, 0)))
    y = w[0] * xp[:, :-2] + w[1] * xp[:, 1:-1] + w[2] * xp[:, 2:]
    return y if b is None else y + b

def flip(a):
    return jnp.flip(a, axis=1)

def to_col_major(h):
    B, S, D = h.shape
    rows = S // GRID_W
    return h.reshape(B, rows, GRID_W, D).transpose(0, 2, 1, 3).reshape(B, S, D)

def to_row_major(h):
    B, S, D = h.shape
    rows = S // GRID_W
    return h.reshape(B, GRID_W, rows, D).transpose(0, 2, 1, 3).reshape(B, S, D)

def gla_chunked(q, k, v, g, s0):
    B, L, H, dk = q.shape
    dv = v.shape[-1]
    C = GLA_CHUNK
    n = L // C
    f32 = jnp.float32
    q = q.astype(f32).reshape(B, n, C, H, dk)
    k = k.astype(f32).reshape(B, n, C, H, dk)
    v = v.astype(f32).reshape(B, n, C, H, dv)
    b = jnp.cumsum(g.astype(f32).reshape(B, n, C, H, dk), axis=2)
    b_last = b[:, :, -1]
    qd = q * jnp.exp(b)
    kd = k * jnp.exp(-b)
    kr = k * jnp.exp(b_last[:, :, None] - b)
    mask = jnp.tril(jnp.ones((C, C), dtype=bool))
    a = jnp.where(mask, jnp.einsum('bnthd,bnshd->bnhts', qd, kd), 0.0)
    o_intra = jnp.einsum('bnhts,bnshe->bnthe', a, v)
    ds = jnp.einsum('bnshd,bnshe->bnhde', kr, v)
    decay = jnp.exp(b_last)

    def step(s, inp):
        d, dsn = inp
        return d[..., None] * s + dsn, s

    s_final, s_before = lax.scan(step, s0, (jnp.moveaxis(decay, 1, 0), jnp.moveaxis(ds, 1, 0)))
    s_before = jnp.moveaxis(s_before, 0, 1)
    o_inter = jnp.einsum('bnthd,bnhde->bnthe', qd, s_before)
    return (o_intra + o_inter).reshape(B, L, H, dv), s_final

def gla_split(p, wa_f, ba_f, wa_b, ba_b):
    B, L, _ = p.shape
    q, k, v, g, rf, rb, hy = jnp.split(p, EV_SPLIT, axis=-1)
    q = q.reshape(B, L, GLA_HEADS, GLA_DK) * GLA_DK ** -0.5
    k = k.reshape(B, L, GLA_HEADS, GLA_DK)
    v = v.reshape(B, L, GLA_HEADS, GLA_DV)
    gf = (jax.nn.log_sigmoid((rf @ wa_f + ba_f).astype(jnp.float32)) / GLA_TAU).reshape(B, L, GLA_HEADS, GLA_DK)
    gb = (jax.nn.log_sigmoid((rb @ wa_b + ba_b).astype(jnp.float32)) / GLA_TAU).reshape(B, L, GLA_HEADS, GLA_DK)
    return q, k, v, g, gf, gb, hy

def gla_readout(o, g, gain):
    B, L = o.shape[:2]
    o = o * lax.rsqrt(jnp.mean(o * o, axis=-1, keepdims=True) + EPS) * gain.astype(jnp.float32)
    return o.reshape(B, L, GLA_V).astype(g.dtype) * jax.nn.silu(g)

def hyena_filters(L, w1, b1, f1, w2, b2, f2, w3):
    f32 = jnp.float32
    t = jnp.linspace(0.0, 1.0, L, dtype=f32)[:, None]
    pos = jnp.arange(L, dtype=f32)[:, None]
    bands = jnp.linspace(1e-4, HY_BANDS - 1, HY_BANDS, dtype=f32)[None]
    ang = (2.0 * math.pi / L) * pos * bands
    z = jnp.concatenate([t, jnp.cos(ang), jnp.sin(ang)], axis=-1)
    hh = jnp.sin(f1 * (z @ w1 + b1))
    hh = jnp.sin(f2 * (hh @ w2 + b2))
    hh = (hh @ w3).astype(f32)
    max_decay = math.log(HY_TARGET) / HY_FAST_DECAY
    min_decay = math.log(HY_TARGET) / HY_SLOW_DECAY
    deltas = jnp.linspace(min_decay, max_decay, HY_WIDTH, dtype=f32)
    window = jnp.exp(-t * jnp.abs(deltas)[None])
    hh = hh.reshape(L, 2, HY_WIDTH) * window[:, None]
    return hh[:, 0], hh[:, 1]

def bidir_fftconv(u, h_fwd, h_bwd, skip):
    L = u.shape[1]
    n = 2 * L
    uf = u.astype(jnp.float32)
    U = jnp.fft.rfft(uf, n=n, axis=1)
    K = jnp.fft.rfft(h_fwd, n=n, axis=0) + jnp.conj(jnp.fft.rfft(h_bwd, n=n, axis=0))
    y = jnp.fft.irfft(U * K[None], n=n, axis=1)[:, :L]
    return (y + uf * skip.astype(jnp.float32)).astype(u.dtype)

def hyena_mix(p, filt, conv_w, conv_b, skip):
    pc = dwconv3(p, conv_w, conv_b)
    x0, x1, v = jnp.split(pc, 3, axis=-1)
    return x0 * bidir_fftconv(v * x1, filt[0], filt[1], skip)

def even_mixer(u, uc, w_in, w_out, wa_f, ba_f, wa_b, ba_b, gla_gain,
               conv_w, conv_b, w1, b1, f1, w2, b2, f2, w3, skip, ctx_out):
    ql, kl, vl, gl, gfl, gbl, hl = gla_split(u @ w_in, wa_f, ba_f, wa_b, ba_b)
    qc, kc, vc, gc, gfc, gbc, hc = gla_split(uc @ w_in, wa_f, ba_f, wa_b, ba_b)
    s0 = jnp.zeros((u.shape[0], GLA_HEADS, GLA_DK, GLA_DV), jnp.float32)
    oc_f, sc_f = gla_chunked(qc, kc, vc, gfc, s0)
    oc_b, sc_b = gla_chunked(flip(qc), flip(kc), flip(vc), flip(gbc), s0)
    ol_f, _ = gla_chunked(ql, kl, vl, gfl, sc_f)
    ol_b, _ = gla_chunked(flip(ql), flip(kl), flip(vl), flip(gbl), sc_b)
    hw = (w1, b1, f1, w2, b2, f2, w3)
    yl = jnp.concatenate([gla_readout(ol_f + flip(ol_b), gl, gla_gain),
                          hyena_mix(hl, hyena_filters(u.shape[1], *hw), conv_w, conv_b, skip)], axis=-1) @ w_out
    yc = None
    if ctx_out:
        yc = jnp.concatenate([gla_readout(oc_f + flip(oc_b), gc, gla_gain),
                              hyena_mix(hc, hyena_filters(uc.shape[1], *hw), conv_w, conv_b, skip)], axis=-1) @ w_out
    return yl, yc

def shortconv_mixer(u, w_in, conv_w, w_out):
    bg, cg, xin = jnp.split(u @ w_in, 3, axis=-1)
    return (bg * dwconv3(cg * xin, conv_w)) @ w_out

def grouped_experts(xt, expert, gate, w1, w3, w2):
    T, D = xt.shape
    M = T * TOP_K
    flat_e = expert.reshape(M)
    flat_t = jnp.repeat(jnp.arange(T, dtype=jnp.int32), TOP_K)
    flat_g = gate.reshape(M)
    order = jnp.argsort(flat_e)
    se = flat_e[order]
    counts = jnp.bincount(flat_e, length=N_EXPERTS)
    padded = (counts + MOE_BLOCK - 1) // MOE_BLOCK * MOE_BLOCK
    start = jnp.cumsum(counts) - counts
    pend = jnp.cumsum(padded)
    pstart = pend - padded
    dest = pstart[se] + jnp.arange(M, dtype=jnp.int32) - start[se]
    n_blocks = -(-(M + N_EXPERTS * (MOE_BLOCK - 1)) // MOE_BLOCK)
    P = n_blocks * MOE_BLOCK
    slot_t = jnp.full((P,), T, jnp.int32).at[dest].set(flat_t[order])
    slot_g = jnp.zeros((P,), gate.dtype).at[dest].set(flat_g[order])
    blk_e = jnp.minimum(jnp.searchsorted(pend, jnp.arange(n_blocks, dtype=jnp.int32) * MOE_BLOCK, side='right'),
                        N_EXPERTS - 1)
    x_pad = jnp.concatenate([xt, jnp.zeros((1, D), xt.dtype)], axis=0)

    def run_block(args):
        tok, e = args
        xb = x_pad[tok]
        return (jax.nn.silu(xb @ w1[e]) * (xb @ w3[e])) @ w2[e]

    yb = lax.map(run_block, (slot_t.reshape(n_blocks, MOE_BLOCK), blk_e))
    y = yb.reshape(P, D) * slot_g[:, None]
    return jax.ops.segment_sum(y, slot_t, num_segments=T + 1)[:T]

def hier_moe(xt, w_grp, b_grp, w_exp, b_exp, w1, w3, w2):
    T = xt.shape[0]
    lg = (xt @ w_grp + b_grp).astype(jnp.float32)
    p_grp = jax.nn.softmax(lg, axis=-1)
    p_g, grp = lax.top_k(p_grp, 1)
    le = (xt @ w_exp + b_exp).astype(jnp.float32).reshape(T, N_GROUPS, EXP_PER_GROUP)
    le = jnp.take_along_axis(le, grp[:, :, None], axis=1)[:, 0]
    top_p, top_i = lax.top_k(jax.nn.softmax(le, axis=-1), TOP_K)
    gate = p_g * top_p / jnp.sum(top_p, axis=-1, keepdims=True)
    expert = grp * EXP_PER_GROUP + top_i
    return grouped_experts(xt, expert, gate.astype(xt.dtype), w1, w3, w2)

def setup_inputs(seed: int = 0) -> dict:
    key = jax.random.key(seed)
    ks = iter(jax.random.split(key, 48))
    D = D_MODEL

    def nrm(shape, scale):
        return scale * jax.random.normal(next(ks), shape, jnp.float32)

    return {
        'x': nrm((BATCH, SEQ, D), 1.0),
        'c': nrm((BATCH, D), 1.0),
        'ctx': nrm((BATCH, CTX_LEN, D), 1.0),
        'c_ctx': nrm((D,), 1.0),
        'mod_w': nrm((DEPTH, D, 6 * D), 0.5 * D ** -0.5),
        'mod_b': nrm((DEPTH, 6 * D), 0.02),
        'norm_mix': 1.0 + nrm((DEPTH, D), 0.02),
        'norm_ffn': 1.0 + nrm((DEPTH, D), 0.02),
        'norm_final': 1.0 + nrm((D,), 0.02),
        'ev_w_in': nrm((N_EVEN, D, EV_IN), D ** -0.5),
        'ev_w_out': nrm((N_EVEN, EV_MIX, D), EV_MIX ** -0.5),
        'gla_wa_f': nrm((N_EVEN, GLA_RANK, GLA_QK), GLA_RANK ** -0.5),
        'gla_ba_f': nrm((N_EVEN, GLA_QK), 0.1),
        'gla_wa_b': nrm((N_EVEN, GLA_RANK, GLA_QK), GLA_RANK ** -0.5),
        'gla_ba_b': nrm((N_EVEN, GLA_QK), 0.1),
        'gla_norm': 1.0 + nrm((N_EVEN, GLA_DV), 0.02),
        'hy_conv_w': nrm((N_EVEN, CONV_W, 3 * HY_WIDTH), CONV_W ** -0.5),
        'hy_conv_b': nrm((N_EVEN, 3 * HY_WIDTH), 0.02),
        'hy_w1': nrm((N_EVEN, HY_EMB, HY_HIDDEN), HY_EMB ** -0.5),
        'hy_b1': nrm((N_EVEN, HY_HIDDEN), 0.1),
        'hy_f1': 1.0 + nrm((N_EVEN, HY_HIDDEN), 0.02),
        'hy_w2': nrm((N_EVEN, HY_HIDDEN, HY_HIDDEN), HY_HIDDEN ** -0.5),
        'hy_b2': nrm((N_EVEN, HY_HIDDEN), 0.1),
        'hy_f2': 1.0 + nrm((N_EVEN, HY_HIDDEN), 0.02),
        'hy_w3': nrm((N_EVEN, HY_HIDDEN, 2 * HY_WIDTH), 0.02),
        'hy_skip': nrm((N_EVEN, HY_WIDTH), 0.5),
        'od_w_in': nrm((N_ODD, D, 3 * SC_WIDTH), D ** -0.5),
        'od_conv_w': nrm((N_ODD, CONV_W, SC_WIDTH), CONV_W ** -0.5),
        'od_w_out': nrm((N_ODD, SC_WIDTH, D), SC_WIDTH ** -0.5),
        'rt_w_grp': nrm((DEPTH, D, N_GROUPS), D ** -0.5),
        'rt_b_grp': nrm((DEPTH, N_GROUPS), 0.01),
        'rt_w_exp': nrm((DEPTH, D, N_EXPERTS), D ** -0.5),
        'rt_b_exp': nrm((DEPTH, N_EXPERTS), 0.01),
        'ex_w1': nrm((DEPTH, N_EXPERTS, D, D_EXPERT), D ** -0.5),
        'ex_w3': nrm((DEPTH, N_EXPERTS, D, D_EXPERT), D ** -0.5),
        'ex_w2': nrm((DEPTH, N_EXPERTS, D_EXPERT, D), D_EXPERT ** -0.5),
    }

def reference(x, c, ctx, c_ctx, mod_w, mod_b, norm_mix, norm_ffn, norm_final,
              ev_w_in, ev_w_out, gla_wa_f, gla_ba_f, gla_wa_b, gla_ba_b, gla_norm,
              hy_conv_w, hy_conv_b, hy_w1, hy_b1, hy_f1, hy_w2, hy_b2, hy_f2, hy_w3, hy_skip,
              od_w_in, od_conv_w, od_w_out,
              rt_w_grp, rt_b_grp, rt_w_exp, rt_b_exp, ex_w1, ex_w3, ex_w2):
    B, S, D = x.shape
    Lc = ctx.shape[1]
    h, hc = x, ctx
    s_lat = jax.nn.silu(c)
    s_ctx = jax.nn.silu(c_ctx)
    for l in range(DEPTH):
        i = l // 2
        even = l % 2 == 0
        ctx_out = l < DEPTH - 1
        col_major = i % 2 == 1
        m_lat = jnp.split((s_lat @ mod_w[l] + mod_b[l])[:, None, :], 6, axis=-1)
        m_ctx = jnp.split(s_ctx @ mod_w[l] + mod_b[l], 6, axis=-1)
        u = modulate(rmsnorm(h, norm_mix[l]), m_lat[0], m_lat[1])
        if col_major:
            u = to_col_major(u)
        uc = modulate(rmsnorm(hc, norm_mix[l]), m_ctx[0], m_ctx[1]) if (even or ctx_out) else None
        if even:
            y, yc = even_mixer(u, uc, ev_w_in[i], ev_w_out[i], gla_wa_f[i], gla_ba_f[i], gla_wa_b[i], gla_ba_b[i],
                               gla_norm[i], hy_conv_w[i], hy_conv_b[i], hy_w1[i], hy_b1[i], hy_f1[i],
                               hy_w2[i], hy_b2[i], hy_f2[i], hy_w3[i], hy_skip[i], ctx_out)
        else:
            y = shortconv_mixer(u, od_w_in[i], od_conv_w[i], od_w_out[i])
            yc = shortconv_mixer(uc, od_w_in[i], od_conv_w[i], od_w_out[i]) if ctx_out else None
        if col_major:
            y = to_row_major(y)
        h = h + m_lat[2] * y
        v = modulate(rmsnorm(h, norm_ffn[l]), m_lat[3], m_lat[4]).reshape(B * S, D)
        if ctx_out:
            hc = hc + m_ctx[2] * yc
            vc = modulate(rmsnorm(hc, norm_ffn[l]), m_ctx[3], m_ctx[4]).reshape(B * Lc, D)
            f = hier_moe(jnp.concatenate([vc, v], axis=0), rt_w_grp[l], rt_b_grp[l], rt_w_exp[l], rt_b_exp[l],
                         ex_w1[l], ex_w3[l], ex_w2[l])
            hc = hc + m_ctx[5] * f[:B * Lc].reshape(B, Lc, D)
            f = f[B * Lc:]
        else:
            f = hier_moe(v, rt_w_grp[l], rt_b_grp[l], rt_w_exp[l], rt_b_exp[l], ex_w1[l], ex_w3[l], ex_w2[l])
        h = h + m_lat[5] * f.reshape(B, S, D)
    return rmsnorm(h, norm_final)


_drawn_inputs = setup_inputs


def setup_inputs(seed=0):
    import zlib

    import numpy as np

    out = dict(_drawn_inputs(seed))
    spreads = {}
    factors = {'ctx': 4.051,
     'c_ctx': 5.818,
     'norm_ffn': 3.221,
     'norm_final': 3.009,
     'gla_ba_f': 5.323,
     'gla_ba_b': 4.598,
     'gla_norm': 8.0,
     'hy_conv_b': 2.839,
     'hy_f1': 6.34,
     'hy_f2': 5.797,
     'rt_b_grp': 8.0,
     'rt_b_exp': 6.59}
    for name, (base, spread) in spreads.items():
        noise = np.random.default_rng([zlib.crc32(name.encode()), seed]).standard_normal(out[name].shape)
        drawn = base * np.exp(spread * noise) if base else spread * noise
        out[name] = jnp.asarray(drawn.astype(out[name].dtype))
    for name, factor in factors.items():
        out[name] = (out[name] * factor).astype(out[name].dtype)
    return out
```

```python
from contextlib import ExitStack

import concourse.bass as bass
import numpy as np
from concourse import mybir

F32 = mybir.dt.float32
I32 = mybir.dt.int32
ALU = mybir.AluOpType
ACT = mybir.ActivationFunctionType
AX = mybir.AxisListType

P = 128
D = 1024
SEQ = 1024
CTX = 256
DEPTH = 2
EPS = 1e-6
KC = D // P
TT = SEQ // P
CT = CTX // P
TOK = SEQ + CTX
HEADS, DK, DV, RANK = 4, 64, 128, 16
TAU = 16.0
CH = 64
NCH = SEQ // CH
NCC = CTX // CH
QK, GV = HEADS * DK, HEADS * DV
HW = 512
HC = HW // P
EMB, HID = 33, 64
NG, EPG, NE, FE = 4, 8, 32, 512
FC = FE // P
HALF = 512
KT = HALF // P
ASSIGN = 2 * SEQ
NJ = SEQ // P
FAR = 8192.0
BIG = 1e30
MAGIC = 1.5 * 2.0 ** 23
TWO_PI_HI = 6.28125
TWO_PI_LO = 2 * np.pi - 6.28125
PI_F = 3.1415925

C_V = 2 * QK
C_G = C_V + GV
C_R = C_G + GV
C_HY = C_R + 2 * RANK

R_CW, R_CB, R_SKIP, R_GAIN, R_OD, R_BA, R_HY, N_ROWS = 0, 36, 48, 52, 53, 77, 81, 85
V_NMIX, V_NFFN, N_VEC = 12, 14, 16
K_ID, K_UT, K_IOTA, K_E64, K_J, K_TV, K_ONE, K_MASK, K_END = 0, 128, 256, 384, 416, 424, 432, 560, 816


def constants():
    cst = np.zeros((P, K_END), np.float32)
    p, c = np.arange(P)[:, None], np.arange(P)[None, :]
    cst[:, K_ID:K_ID + P] = p == c
    cst[:, K_UT:K_UT + P] = p < c
    cst[:, K_IOTA:K_IOTA + P] = c
    cst[:, K_E64:K_E64 + NE] = np.arange(NE) + 64
    cst[:, K_J:K_J + NJ] = np.arange(NJ)
    cst[:, K_TV:K_TV + TT] = 2 * (np.arange(TT)[None, :] * P + p)
    cst[:, K_ONE:K_ONE + P] = 1.0
    same = (p // CH) == (c // CH)
    mask = np.stack([same & (p <= c), same & (p >= c)], 1).astype(np.int32)
    cst[:, K_MASK:K_END] = mask.reshape(P, 2 * P).view(np.float32)

    t = np.linspace(0.0, 1.0, SEQ, dtype=np.float32)
    pos = np.arange(SEQ, dtype=np.float32)
    nb = (EMB - 1) // 2
    bands = np.linspace(1e-4, nb - 1, nb, dtype=np.float32)
    ang = np.float32(2.0 * np.pi / SEQ) * pos[:, None] * bands[None]
    z = np.concatenate([t[:, None], np.cos(ang), np.sin(ang)], -1).astype(np.float32)
    deltas = np.linspace(np.log(1e-2) / 1.5, np.log(1e-2) / 0.3, HW, dtype=np.float32)
    win = np.exp(-t[:, None] * np.abs(deltas)[None]).astype(np.float32)
    win = win.reshape(HALF // P, P, 2, HW).transpose(1, 2, 0, 3).reshape(P, 2 * KT * HW)

    k = np.arange(HALF)
    w = np.pi * (2 * k[None, :] + 1) * np.arange(SEQ)[:, None] / 2048.0
    cs = np.stack([np.cos(w), np.sin(w)])
    cs = cs.reshape(2, KT, P, 2, KT, P)
    fwd = cs.transpose(2, 4, 0, 3, 1, 5)
    inv = (cs / 512.0).transpose(5, 0, 3, 4, 1, 2)
    return {
        "cst": cst, "zT": np.ascontiguousarray(z.T), "win": win,
        "dft": np.ascontiguousarray(fwd.reshape(P, 8192).astype(np.float32)),
        "idft": np.ascontiguousarray(inv.reshape(P, 8192).astype(np.float32)),
    }


def build(nc, a, out, UPTO=99):
    with ExitStack() as ctx:
        def sb(name, shape, dt=F32):
            return ctx.enter_context(nc.sbuf_tensor(name, shape, dt))

        def sem(name):
            return ctx.enter_context(nc.semaphore(name))

        arena = sb("arena", [P, 48512])
        cst = sb("constants", [P, K_END])
        small_rows = sb("small_rows", [N_ROWS, P])
        cols = sb("cols", [P, N_ROWS])
        neg_ba = sb("neg_ba", [P, HEADS])
        vec_cols = sb("vec_cols", [P, KC, N_VEC])
        mod = sb("mod", [P, 6, KC, 2])
        gain_x = sb("gain_x", [P, 3, KC])
        gates = sb("gates", [P, 2, D])
        c_raw = sb("c_raw", [P, 2, KC])
        silu_c = sb("silu_c", [P, KC, 2])
        ss = sb("ss", [P, 16])
        rstd = sb("rstd", [P, 16])
        w_rank = sb("w_rank", [P, KC, 2 * RANK])
        w_gate_up = sb("w_gate_up", [2 * RANK, HEADS, P])
        decay = sb("decay", [P, NCH + NCC])
        w_hy1 = sb("w_hy1", [EMB, HID])
        w_hy2 = sb("w_hy2", [HID, HID])
        row_number = sb("row_number", [P, 2, TT])

        def at(off, *dims):
            n = int(np.prod(dims))
            v = arena[:, off:off + n]
            if len(dims) == 2:
                return v.rearrange("p (a b) -> p a b", a=dims[0])
            if len(dims) == 3:
                return v.rearrange("p (a b c) -> p a b c", a=dims[0], b=dims[1])
            if len(dims) == 4:
                return v.rearrange("p (a b c d) -> p a b c d", a=dims[0], b=dims[1], c=dims[2])
            return v

        ps = ctx.enter_context(nc.psum_tensor("ps", [P, 8, 512], F32))

        def bank(b):
            return ps[:, b, :]

        ident = cst[:, K_ID:K_ID + P]

        SLAB = 4096
        RING = 3
        U = at(12288, KC, SEQ)
        UC = at(20480, KC, CTX)
        MIX = at(22528, KC, SEQ)
        HEAD_V = at(26624, TT + CT, GV)
        Q, K, KD = at(31744, SEQ), at(32768, TOK), at(34048, SEQ)
        BB, T1 = at(35072, TOK), at(36352, TOK)
        KRT = at(37632, TT + CT, P)
        ST = at(38912, NCH, DV)
        SG = at(40960, SEQ)
        AT = at(41984, 2, 2, P)
        OT = at(42496, TT, DV)
        QP, KP = at(43520, SEQ), at(44544, TOK)
        RT = at(45824, TOK)[0:2 * RANK]
        SCAN1 = at(47104, TOK)
        SCTX = at(48384, DV)
        MROW = at(28672, 2, D)
        VEC = at(30720, D)[0:N_VEC]
        X0 = at(31744, TT + CT, D)
        VX = at(30720, HC, SEQ)
        VTM = at(34816, 2, KT, HW)
        X1C, VC_ = at(20480, SEQ), at(21504, SEQ)
        DFT = at(38912, KT, 2, 2, 4 * P)
        YF = at(38912, KT, 4, HW)
        IDFT = at(12288, 2, 2, KT * HALF)
        HSUM, HDIF = at(4096, 2 * KT, HW), at(8192, 2 * KT, HW)
        UK = at(0, 8, HW)
        ZT, W3H = at(12288, SEQ), at(13312, SEQ)
        ARG, TURNS, HH1, HH2 = at(14336, SEQ), at(15360, SEQ), at(16384, SEQ), at(12288, SEQ)
        WIN = at(17408, 2 * KT, HW)
        FTMP = at(21504, 2, HW)
        CTMP = at(20480, 4, HW)
        H = at(38912, TT, D)
        GTM = at(20480, KC, SEQ)
        BGT, CONVT = at(28672, 2, SEQ), at(30720, 2, SEQ)
        CX = at(32768, 2, SEQ)
        XG = at(24576, 2, D)
        XT = at(26624, 2, KC * P)
        YS = at(28672, 2, D)
        VTT = at(27648, 2, KC * P)
        HB, HT, SL = at(30720, FE), at(31232, FE), at(31744, FE)
        LG = at(32256, TT, NG + NE)
        ONE_HOT = [at(32544 + 256 * k, TT, NE) for k in range(2)]
        SUMOH = at(33056, TT * NE)
        POSM = at(33312, TT, NE)
        MSK = at(33568, TT, NE)
        LEX = at(33824, TT, NE)
        GRP = at(34080, 4, TT, NG)
        SC = at(34208, 16, TT)
        HOT = at(34336, 2, P)
        RHS = at(34592, 2, 2, NJ * NE)
        OV = at(35616, 2, 2, NE)
        JEQ = at(35744, 2, NJ)
        GATE_OF = at(35760, NJ * NE)
        SLOT_F = at(36016, NJ * NE)
        SLOT_ROW = at(36272, NJ * NE).bitcast(I32)
        SLOT_TOK = at(36528, NJ * NE).bitcast(I32)
        ACTIVE_F = at(36784, NJ, NE)
        ACTIVE = at(37040, NJ * NE).bitcast(I32)
        ANY_F, ANY = at(37296, 4), at(37300, 4).bitcast(I32)
        IDX_G = at(37304, 4).bitcast(I32)
        IDX_S = at(37308, 4).bitcast(I32)
        W_RT = at(37312, KC, NG + NE)
        B_RT = at(37600, NG + NE)
        CY = at(24576, 2, 2, D)
        GF = at(30720, D)

        rows_hn = nc.dram_tensor("normed_rows", (SEQ, D), F32, kind="Internal").ap()
        rows_y = nc.dram_tensor("expert_rows", (ASSIGN, D), F32, kind="Internal").ap()

        s_cst = sem("s_cst")
        s_rows = sem("s_rows")
        s_vec = sem("s_vec")
        s_cin = sem("s_cin")
        s_x = sem("s_x")
        s_xr = sem("s_xr")
        s_wr = sem("s_wr")
        slab_full = [sem(f"slab_full{n}") for n in range(RING)]
        silu_ready = sem("silu_ready")
        rows_T = sem("rows_T")
        cols_ready = sem("cols_ready")
        vec_T = sem("vec_T")
        mod_mm = sem("mod_mm")
        mod_row = sem("mod_row")
        mod_T = sem("mod_T")
        mod_bc = sem("mod_bc")
        mod_gate = sem("mod_gate")
        mod_ready = sem("mod_ready")
        act_step = sem("act_step")
        dve_step = sem("dve_step")
        pool_step = sem("pool_step")
        sq_done = sem("sq_done")
        ms_ready = sem("ms_ready")
        root_ready = sem("root_ready")
        xn_ready = sem("xn_ready")
        xn_T = sem("xn_T")
        u_ready = sem("u_ready")
        hn_out = [sem(f"hn_out{b}") for b in range(2)]
        v_mm = sem("v_mm")
        v_ready = sem("v_ready")
        r_mm = sem("r_mm")
        r_ready = sem("r_ready")
        gla_zero = sem("gla_zero")
        qk_mm = sem("qk_mm")
        qk_ready = sem("qk_ready")
        dup_act = sem("dup_act")
        dup_pool = sem("dup_pool")
        gx_mm = sem("gx_mm")
        gx_read = sem("gx_read")
        ln_ready = sem("ln_ready")
        cum_ready = sem("cum_ready")
        er_ready = sem("er_ready")
        eb_ready = sem("eb_ready")
        kr_ready = sem("kr_ready")
        qd_ready = sem("qd_ready")
        g_mm = sem("g_mm")
        sg_ready = sem("sg_ready")
        kr_T = sem("kr_T")
        krt_ready = sem("krt_ready")
        ds_mm = sem("ds_mm")
        state_ready = sem("state_ready")
        a_mm = sem("a_mm")
        at_ready = sem("at_ready")
        o_mm = sem("o_mm")
        o_copied = sem("o_copied")
        oss_ready = sem("oss_ready")
        oroot_ready = sem("oroot_ready")
        on_ready = sem("on_ready")
        o_T = sem("o_T")
        omix_ready = sem("omix_ready")
        dft_in = sem("dft_in")
        idft_in = sem("idft_in")
        flt_in = sem("flt_in")
        win_in = sem("win_in")
        hy_mm = sem("hy_mm")
        conv_done = sem("conv_done")
        vx_ready = sem("vx_ready")
        vx_T = sem("vx_T")
        vtm_ready = sem("vtm_ready")
        f_mm = sem("f_mm")
        f_arg = sem("f_arg")
        f_sin = sem("f_sin")
        h3_mm = sem("h3_mm")
        h3_copied = sem("h3_copied")
        filt_ready = sem("filt_ready")
        dft_mm = sem("dft_mm")
        uk_ready = sem("uk_ready")
        yf_dve = sem("yf_dve")
        yf_pool = sem("yf_pool")
        idft_mm = sem("idft_mm")
        hmix_ready = sem("hmix_ready")
        out_mm = sem("out_mm")
        h_ready = sem("h_ready")
        od_mm = sem("od_mm")
        bg_ready = sem("bg_ready")
        od_conv = sem("od_conv")
        rt_in = sem("rt_in")
        lg_mm = sem("lg_mm")
        lg_ready = sem("lg_ready")
        gexp_in = sem("gexp_in")
        gexp_out = sem("gexp_out")
        oh_ready = sem("oh_ready")
        pos_mm = sem("pos_mm")
        hot_ready = sem("hot_ready")
        tab_mm = sem("tab_mm")
        tab_ready = sem("tab_ready")
        w_full = [[sem(f"w_full{b}_{m}") for m in range(3)] for b in range(2)]
        x_full = [sem(f"x_full{b}") for b in range(2)]
        idx_ready = sem("idx_ready")
        x_T = [sem(f"x_T{b}") for b in range(2)]
        xt_ready = [sem(f"xt_ready{b}") for b in range(2)]
        up_mm = [sem(f"up_mm{b}") for b in range(2)]
        gate_mm = [sem(f"gate_mm{b}") for b in range(2)]
        sl_ready = [sem(f"sl_ready{b}") for b in range(2)]
        hb_ready = [sem(f"hb_ready{b}") for b in range(2)]
        hb_T = [sem(f"hb_T{b}") for b in range(2)]
        ht_ready = [sem(f"ht_ready{b}") for b in range(2)]
        y_mm = [sem(f"y_mm{b}") for b in range(2)]
        y_ready = [sem(f"y_ready{b}") for b in range(2)]
        y_out = [sem(f"y_out{b}") for b in range(2)]
        ov_w = [sem(f"ov_w{m}") for m in range(3)]
        ov_idx = sem("ov_idx")
        ov_x = sem("ov_x")
        ov_xT = sem("ov_xT")
        ov_xt = sem("ov_xt")
        ov_up = sem("ov_up")
        ov_gate = sem("ov_gate")
        ov_sl = sem("ov_sl")
        ov_hb = sem("ov_hb")
        ov_hT = sem("ov_hT")
        ov_ht = sem("ov_ht")
        ov_ymm = sem("ov_ymm")
        ov_y = sem("ov_y")
        ov_out = sem("ov_out")
        ov_left = sem("ov_left")
        cy_full = [sem(f"cy_full{b}") for b in range(2)]
        cy_used = sem("cy_used")
        gf_in = sem("gf_in")
        o_ready = sem("o_ready")
        s_out = [sem(f"s_out{b}") for b in range(2)]

        NMOD = 12
        NOV = (NJ - 1) * NE
        L0_V, L0_G, L0_QK, L0_HY, L0_OUT = NMOD, NMOD + 1, NMOD + 2, NMOD + 3, NMOD + 7
        L1_MOD = NMOD + 9
        L1_IN, L1_OUT = L1_MOD + NMOD, L1_MOD + NMOD + KC
        NORMS = [TT + CT, TT, TT, TT, TT]
        norm_base = [sum(NORMS[:n]) for n in range(len(NORMS) + 1)]

        def last_use(n):
            if n < NMOD:
                return mod_mm, n + 1
            if n == L0_V:
                return v_mm, TT + CT
            if n == L0_G:
                return g_mm, 2 * HEADS
            if n == L0_QK:
                return qk_mm, 5 * (HEADS // 2)
            if n < L0_OUT:
                return hy_mm, 6 * (n - L0_HY + 1)
            if n < L1_MOD:
                return out_mm, 2 * TT
            if n < L1_IN:
                return mod_mm, NMOD + n - L1_MOD + 1
            if n < L1_OUT:
                return od_mm, 6 * (n - L1_IN + 1)
            return out_mm, 4 * TT

        def ds_place(c):
            b = (0, 1, 2)[c // 8] if c % 2 == 0 else (3, 4, 7)[c // 8]
            return bank(b)[:, (c // 2 % 4) * P:(c // 2 % 4 + 1) * P]

        def slab(n, *dims):
            return at((n % RING) * SLAB, *dims)

        def w_slot(b, m, *dims):
            return at((3 * b + m) * SLAB, *dims)

        block = ctx.enter_context(nc.Block())

        @block.sync
        def _(sp):
            def load(n, dst, src):
                if n >= RING:
                    sp.wait_ge(*last_use(n - RING))
                sp.dma_start(dst, src).then_inc(slab_full[n % RING], 16)

            def modulation(l, first):
                for n in range(NMOD):
                    load(first + n, slab(first + n, KC, 512),
                         a["mod_w"][l, :, n * 512:(n + 1) * 512].rearrange("(p j) n -> p j n", j=KC))

            def rows_in():
                sp.dma_start(cst[:], a["cst"]).then_inc(s_cst, 16)
                sp.dma_start(c_raw[:, 0], a["c"].rearrange("o (p j) -> p (o j)", j=KC)).then_inc(s_cin, 16)
                sp.dma_start(c_raw[:, 1], a["c_ctx"].rearrange("(p j) -> p j", j=KC)).then_inc(s_cin, 16)

            def moe_weights(l):
                srcs = [a["ex_w1"], a["ex_w3"], a["ex_w2"]]

                def pair(i, first):
                    for b in range(2):
                        for m in range(3):
                            if not first:
                                used = (up_mm, gate_mm, y_mm)[m][b]
                                sp.wait_ge(used, (i + l * (NE // 2)) * (2 if m == 2 else 1))
                            sp.dma_start(
                                w_slot(b, m, SLAB),
                                srcs[m][l, i * 2 + b].rearrange("(p j) n -> p (j n)", p=P),
                            ).then_inc(w_full[b][m], 16)

                pair(0, l == 0)
                with sp.Fori(0, NE // 2 - 1) as i:
                    pair(i + 1, False)

            def moe_overflow(l):
                flag = sp.value_load(ANY[0:1, 0:1])
                with sp.If(flag > 0):
                    with sp.Fori(0, NJ - 1) as t:
                        with sp.Fori(0, NE) as e:
                            n = t * NE + e
                            act_flag = sp.value_load(ACTIVE[0:1, bass.ds(n + NE, 1)])
                            with sp.If(act_flag > 0):
                                sp.wait_ge(ov_x, (n + (l * NOV + 1)) * 16)
                                for m, src in enumerate([a["ex_w1"], a["ex_w3"], a["ex_w2"]]):
                                    sp.dma_start(
                                        w_slot(0, m, SLAB), src[l, e].rearrange("(p j) n -> p (j n)", p=P),
                                    ).then_inc(ov_w[m], 16)
                            with sp.Else():
                                for m in range(3):
                                    sp.sem_inc(ov_w[m], 16)
                with sp.Else():
                    for m in range(3):
                        sp.sem_inc(ov_w[m], 16 * NOV)
                sp.sem_inc(ov_left, 1)

            def combine(l):
                for b in range(2):
                    sp.wait_ge(y_out[b], 16 * (NE // 2) * (l + 1))
                sp.wait_ge(ov_left, 5 * (l + 1))
                for i in range(TT):
                    if i >= 2:
                        sp.wait_ge(cy_used, l * TT + i - 1)
                    sp.dma_start(
                        CY[:, i % 2], rows_y[i * 2 * P:(i + 1) * 2 * P].rearrange("(t k) d -> t k d", k=2)
                    ).then_inc(cy_full[i % 2], 16)

            rows_in()
            modulation(0, 0)
            if UPTO >= 2:
                load(L0_V, slab(L0_V, KC, GV), a["ev_w_in"][0, :, C_V:C_G].rearrange("(p j) n -> p j n", j=KC))
                load(L0_G, slab(L0_G, KC, GV), a["ev_w_in"][0, :, C_G:C_R].rearrange("(p j) n -> p j n", j=KC))
                load(L0_QK, slab(L0_QK, KC, 2 * QK), a["ev_w_in"][0, :, 0:C_V].rearrange("(p j) n -> p j n", j=KC))
            if UPTO >= 3:
                for c in range(HC):
                    n = L0_HY + c
                    sp.wait_ge(*last_use(n - RING))
                    for k in range(3):
                        sp.dma_start(
                            slab(n, 3, KC, P)[:, k],
                            a["ev_w_in"][0, :, C_HY + k * HW + c * P:C_HY + k * HW + (c + 1) * P].rearrange(
                                "(p j) n -> p j n", j=KC),
                        ).then_inc(slab_full[n % RING], 16)
                sp.wait_ge(omix_ready, 2 * HEADS)
                sp.dma_start(at(38912, 8192), a["dft"]).then_inc(dft_in, 16)
            if UPTO >= 4:
                sp.wait_ge(hy_mm, 6 * HC)
                sp.dma_start(w_hy1[:], a["hy_w1"][0]).then_inc(flt_in, 16)
                sp.dma_start(w_hy2[:], a["hy_w2"][0]).then_inc(flt_in, 16)
                sp.dma_start(ZT[0:EMB], a["zT"]).then_inc(flt_in, 16)
                sp.dma_start(W3H[0:HID], a["hy_w3"][0]).then_inc(flt_in, 16)
                sp.wait_ge(vtm_ready, 2 * HC)
                sp.dma_start(at(17408, 4096), a["win"]).then_inc(win_in, 16)
            if UPTO >= 5:
                sp.wait_ge(filt_ready, 2 * KT)
                sp.dma_start(at(12288, 8192), a["idft"]).then_inc(idft_in, 16)
            if UPTO >= 6:
                sp.wait_ge(dft_mm, 8 * KT)
                sp.wait_ge(uk_ready, 8 * KT)
                for n in range(2):
                    load(L0_OUT + n, slab(L0_OUT + n, KC, 512),
                         a["ev_w_out"][0, :, n * 512:(n + 1) * 512].rearrange("(j p) n -> p j n", p=P))
                sp.wait_ge(idft_mm, 2 * HC)
                sp.dma_start(H, a["x"][0].rearrange("(i p) d -> p i d", p=P)).then_inc(s_xr, 16)
            if UPTO >= 7:
                for l in range(DEPTH):
                    if l:
                        modulation(1, L1_MOD)
                        for c in range(KC):
                            n = L1_IN + c
                            sp.wait_ge(*last_use(n - RING))
                            for k in range(3):
                                sp.dma_start(
                                    slab(n, 3, KC, P)[:, k],
                                    a["od_w_in"][0, :, k * D + c * P:k * D + (c + 1) * P].rearrange(
                                        "(p j) n -> p j n", j=KC),
                                ).then_inc(slab_full[n % RING], 16)
                        for n in range(2):
                            load(L1_OUT + n, slab(L1_OUT + n, KC, 512),
                                 a["od_w_out"][0, :, n * 512:(n + 1) * 512].rearrange("(j p) n -> p j n", p=P))
                    sp.wait_ge(h_ready, 2 * TT * (l + 1))
                    moe_weights(l)
                    sp.wait_ge(y_mm[0], (l + 1) * NE)
                    sp.wait_ge(tab_ready, l + 1)
                    moe_overflow(l)
                    combine(l)
                sp.wait_ge(cy_used, 2 * TT)
                for i in range(TT):
                    sp.wait_ge(o_ready, i + 1)
                    sp.dma_start(out[0, i * P:(i + 1) * P, :], H[:, i, :]).then_inc(s_out[i % 2], 16)
                for b in range(2):
                    sp.wait_ge(s_out[b], 16 * TT // 2)

        @block.gpsimd
        def _(pool):
            def step(ins, n):
                ins.then_inc(pool_step, 1)
                pool.wait_ge(pool_step, n)

            nc.gpsimd.memset(small_rows[:], 0.0).then_inc(pool_step, 1)
            nc.gpsimd.memset(w_gate_up[:], 0.0).then_inc(pool_step, 1)
            pool.wait_ge(pool_step, 2)

            def row(dst, src):
                pool.dma_start(dst, src).then_inc(s_rows, 16)

            row(small_rows[R_CW:R_CB], a["hy_conv_w"][0].rearrange("w (c p) -> (w c) p", p=P))
            row(small_rows[R_CB:R_SKIP], a["hy_conv_b"][0].rearrange("(c p) -> c p", p=P))
            row(small_rows[R_SKIP:R_GAIN], a["hy_skip"][0].rearrange("(c p) -> c p", p=P))
            row(small_rows[R_GAIN:R_OD], a["gla_norm"])
            row(small_rows[R_OD:R_BA], a["od_conv_w"][0].rearrange("w (c p) -> (w c) p", p=P))
            row(small_rows[R_BA:R_HY, 0:DK], a["gla_ba_f"][0].rearrange("(h d) -> h d", d=DK))
            row(small_rows[R_BA:R_HY, DK:P], a["gla_ba_b"][0].rearrange("(h d) -> h d", d=DK))
            for n, name in enumerate(["hy_b1", "hy_f1", "hy_b2", "hy_f2"]):
                row(small_rows[R_HY + n:R_HY + n + 1, 0:HID], a[name])
            row(w_gate_up[0:RANK, :, 0:DK], a["gla_wa_f"][0].rearrange("r (h d) -> r h d", d=DK))
            row(w_gate_up[RANK:2 * RANK, :, DK:P], a["gla_wa_b"][0].rearrange("r (h d) -> r h d", d=DK))

            def vectors():
                pool.dma_start(VEC[0:V_NMIX], a["mod_b"].rearrange("l (s d) -> (l s) d", d=D)).then_inc(s_vec, 16)
                pool.dma_start(VEC[V_NMIX:V_NFFN], a["norm_mix"]).then_inc(s_vec, 16)
                pool.dma_start(VEC[V_NFFN:N_VEC], a["norm_ffn"]).then_inc(s_vec, 16)

            vectors()
            pool.dma_start(X0[:, 0:TT], a["x"][0].rearrange("(i p) d -> p i d", p=P)).then_inc(s_x, 16)
            pool.dma_start(X0[:, TT:], a["ctx"][0].rearrange("(i p) d -> p i d", p=P)).then_inc(s_x, 16)
            pool.dma_start(w_rank[:], a["ev_w_in"][0, :, C_R:C_HY].rearrange("(p j) n -> p j n", j=KC))\
                .then_inc(s_wr, 16)

            if UPTO >= 2:
                for h in range(HEADS):
                    pool.wait_ge(qk_ready, 5 * (h // 2 + 1))
                    if h:
                        pool.wait_ge(o_mm, TT * h)
                        pool.wait_ge(kr_ready, 3 * h)
                    hb = (h % 2) * DK
                    nc.gpsimd.tensor_copy(K[0:DK], KP[hb:hb + DK]).then_inc(dup_pool, 1)
                    nc.gpsimd.tensor_copy(K[DK:P], KP[hb:hb + DK]).then_inc(dup_pool, 1)

            if UPTO >= 5:
                base = 2
                for kt in range(KT):
                    pool.wait_ge(uk_ready, 8 * (kt + 1))
                    ua, ub, uc, ud, ka, kb, kc, kd = [UK[:, q] for q in range(8)]
                    t0, t1 = CTMP[:, 2], CTMP[:, 3]
                    for row_, terms, signs in ((1, ((ua, kb), (ub, ka), (uc, kd), (ud, kc)), (1, -1, -1)),
                                               (3, ((ua, kd), (ub, kc), (uc, kb), (ud, ka)), (1, 1, 1))):
                        base += 1
                        step(nc.gpsimd.tensor_tensor(t0, terms[0][0], terms[0][1], ALU.mult), base)
                        for q in range(3):
                            x, y = terms[q + 1]
                            base += 1
                            step(nc.gpsimd.tensor_tensor(t1, x, y, ALU.mult), base)
                            dst = YF[:, kt, row_] if q == 2 else t0
                            if q == 2:
                                nc.gpsimd.tensor_tensor(
                                    dst, t0, t1, ALU.add if signs[q] > 0 else ALU.subtract).then_inc(yf_pool, 1)
                                pool.wait_ge(yf_pool, 2 * kt + row_ // 2 + 1)
                            else:
                                base += 1
                                step(nc.gpsimd.tensor_tensor(
                                    dst, t0, t1, ALU.add if signs[q] > 0 else ALU.subtract), base)

            def router_in(l):
                pool.wait_ge(h_ready, 2 * TT * (l + 1))
                pool.dma_start(W_RT[:, :, 0:NG], a["rt_w_grp"][l].rearrange("(p j) g -> p j g", j=KC))\
                    .then_inc(rt_in, 16)
                pool.dma_start(W_RT[:, :, NG:], a["rt_w_exp"][l].rearrange("(p j) g -> p j g", j=KC))\
                    .then_inc(rt_in, 16)
                pool.dma_start(B_RT[0:1, 0:NG], a["rt_b_grp"][l:l + 1]).then_inc(rt_in, 16)
                pool.dma_start(B_RT[0:1, NG:], a["rt_b_exp"][l:l + 1]).then_inc(rt_in, 16)

            def gather(l, b, col, wait):
                nc.gpsimd.tensor_copy(IDX_G[:, b:b + 1], SLOT_TOK[:, col]).then_inc(idx_ready, 1)
                pool.wait_ge(idx_ready, wait)
                pool.sem_inc(pool_step, 1)
                pool.indirect_dma_start(
                    XG[:, b], None, rows_hn, bass.IndirectOffsetOnAxis(ap=IDX_G[:, b:b + 1], axis=0),
                    bounds_check=SEQ - 1, oob_is_err=False).then_inc(x_full[b], 16)

            def scatter(l, b, col, wait):
                nc.gpsimd.tensor_copy(IDX_S[:, b:b + 1], SLOT_ROW[:, col]).then_inc(idx_ready, 1)
                pool.wait_ge(idx_ready, wait)
                pool.sem_inc(pool_step, 1)
                pool.indirect_dma_start(
                    rows_y, bass.IndirectOffsetOnAxis(ap=IDX_S[:, b:b + 1], axis=0), YS[:, b], None,
                    bounds_check=ASSIGN - 1, oob_is_err=False).then_inc(y_out[b], 16)

            def experts(l):
                e0 = l * (NE // 2)
                c0 = l * 2 * NE
                for i in range(TT):
                    pool.wait_ge(xn_ready, norm_base[2 * l + 1] + i + 1)
                    pool.dma_start(rows_hn[i * P:(i + 1) * P], at(24576, 2, D)[:, i % 2]).then_inc(hn_out[i % 2], 16)
                for b in range(2):
                    pool.wait_ge(hn_out[b], 16 * (TT // 2) * (l + 1))
                pool.wait_ge(tab_ready, l + 1)
                for b in range(2):
                    gather(l, b, bass.ds(b, 1), c0 + b + 1)

                def pair(i, first):
                    for b in range(2):
                        pool.wait_ge(y_ready[b], (i + e0 + 1) * 2)
                        if not first:
                            pool.wait_ge(y_out[b], (i + e0) * 16)
                        scatter(l, b, bass.ds(i * 2 + b, 1), i * 4 + (c0 + 2 * b + 3))
                        pool.wait_ge(x_T[b], (i + e0 + 1) * 2)
                        pool.wait_ge(x_full[b], (i + e0 + 1) * 16)
                        gather(l, b, bass.ds(i * 2 + b + 2, 1), i * 4 + (c0 + 2 * b + 4))

                pair(0, l == 0)
                with pool.Fori(0, NE // 2 - 2) as i:
                    pair(i + 1, False)
                last = NE // 2 - 1
                for b in range(2):
                    pool.wait_ge(y_ready[b], (last + e0 + 1) * 2)
                    pool.wait_ge(y_out[b], (last + e0) * 16)
                    scatter(l, b, bass.ds(2 * last + b, 1), c0 + 4 * last + b + 3)
                for b in range(2):
                    pool.wait_ge(y_out[b], (last + e0 + 1) * 16)

            def overflow(l):
                flag = pool.value_load(ANY[0:1, 0:1])
                with pool.If(flag > 0):
                    with pool.Fori(0, NOV) as n:
                        act_flag = pool.value_load(ACTIVE[0:1, bass.ds(n + NE, 1)])
                        with pool.If(act_flag > 0):
                            nc.gpsimd.tensor_copy(IDX_G[:, 2:3], SLOT_TOK[:, bass.ds(n + NE, 1)]).then_inc(ov_idx, 1)
                            nc.gpsimd.tensor_copy(IDX_S[:, 2:3], SLOT_ROW[:, bass.ds(n + NE, 1)]).then_inc(ov_idx, 1)
                            pool.wait_ge(ov_idx, (n + (l * NOV + 1)) * 2)
                            pool.sem_inc(pool_step, 1)
                            pool.indirect_dma_start(
                                XG[:, 0], None, rows_hn,
                                bass.IndirectOffsetOnAxis(ap=IDX_G[:, 2:3], axis=0),
                                bounds_check=SEQ - 1, oob_is_err=False).then_inc(ov_x, 16)
                            pool.wait_ge(ov_y, n + (l * NOV + 1))
                            pool.sem_inc(pool_step, 1)
                            pool.indirect_dma_start(
                                rows_y, bass.IndirectOffsetOnAxis(ap=IDX_S[:, 2:3], axis=0), YS[:, 0], None,
                                bounds_check=ASSIGN - 1, oob_is_err=False).then_inc(ov_out, 16)
                            pool.wait_ge(ov_out, (n + (l * NOV + 1)) * 16)
                        with pool.Else():
                            pool.sem_inc(ov_idx, 2)
                            pool.sem_inc(ov_x, 16)
                            pool.sem_inc(ov_out, 16)
                with pool.Else():
                    pool.sem_inc(ov_idx, 2 * NOV)
                    pool.sem_inc(ov_x, 16 * NOV)
                    pool.sem_inc(ov_out, 16 * NOV)
                pool.sem_inc(ov_left, 1)

            if UPTO >= 7:
                for l in range(DEPTH):
                    if l:
                        pool.wait_ge(cy_used, TT)
                        vectors()
                    router_in(l)
                    experts(l)
                    overflow(l)
                pool.wait_ge(cy_used, 2 * TT)
                pool.dma_start(GF, a["norm_final"].partition_broadcast(P)).then_inc(gf_in, 16)

        @block.scalar
        def _(act):
            count = [0]

            def step(ins):
                count[0] += 1
                ins.then_inc(act_step, 1)

            def settle():
                act.wait_ge(act_step, count[0])

            def norm(n, src, junk):
                for i in range(NORMS[n]):
                    if n in (1, 3):
                        act.wait_ge(h_ready, 2 * TT * (n // 2) + 2 * (i + 1))
                    if n in (2, 4) and i == 0:
                        act.wait_ge(cy_used, TT * n // 2)
                    if i >= 2:
                        act.wait_ge(sq_done, norm_base[n] + i - 1)
                    nc.scalar.activation(junk[:, i % 2], src[:, i], ACT.Square, accum_out=ss[:, i:i + 1]).then_inc(sq_done, 1)
                act.wait_ge(ms_ready, n + 1)
                nc.scalar.activation(rstd[:, 0:NORMS[n]], rstd[:, 0:NORMS[n]], ACT.Sqrt).then_inc(root_ready, 1)

            act.wait_ge(s_cin, 32)
            nc.scalar.activation(silu_c[:].rearrange("p j r -> p r j"), c_raw[:], ACT.Silu).then_inc(silu_ready, 1)
            act.wait_ge(s_x, 32)
            norm(0, X0, at(12288, 2, D))

            def gla_head(h):
                if h % 2 == 0:
                    if h:
                        act.wait_ge(dup_act, 2 * h)
                        act.wait_ge(dup_pool, 2 * h)
                    for q in range(5):
                        act.wait_ge(qk_mm, 5 * (h // 2) + q + 1)
                        if q < 2:
                            ins = nc.scalar.activation(QP[:, q * 512:(q + 1) * 512], bank(q), ACT.Copy, scale=DK ** -0.5)
                        else:
                            n = 512 if q < 4 else CTX
                            ins = nc.scalar.activation(KP[:, (q - 2) * 512:(q - 2) * 512 + n], bank(q)[:, 0:n], ACT.Copy)
                        ins.then_inc(qk_ready, 1)
                act.wait_ge(qk_ready, 5 * (h // 2 + 1))
                if h:
                    act.wait_ge(o_mm, TT * h)
                hb = (h % 2) * DK
                nc.scalar.activation(Q[0:DK], QP[hb:hb + DK], ACT.Copy).then_inc(dup_act, 1)
                nc.scalar.activation(Q[DK:P], QP[hb:hb + DK], ACT.Copy).then_inc(dup_act, 1)
                act.wait_ge(gx_read, 6 * (h + 1))
                step(nc.scalar.activation(BB, BB, ACT.Exp, bias=neg_ba[:, h:h + 1]))
                settle()
                nc.scalar.activation(BB, BB, ACT.Ln, bias=1.0).then_inc(ln_ready, 1)
                act.wait_ge(cum_ready, 2 * (h + 1))
                nc.scalar.activation(T1, T1, ACT.Exp, scale=1.0 / TAU).then_inc(er_ready, 1)
                bv = BB.rearrange("p (c t) -> p c t", t=CH)
                nc.scalar.activation(decay[0:DK], bv[0:DK, :, CH - 1], ACT.Exp, scale=1.0 / TAU).then_inc(er_ready, 1)
                nc.scalar.activation(decay[DK:P], bv[DK:P, :, 0], ACT.Exp, scale=1.0 / TAU).then_inc(er_ready, 1)
                nc.scalar.activation(KD, BB[:, 0:SEQ], ACT.Exp, scale=-1.0 / TAU).then_inc(eb_ready, 1)
                act.wait_ge(er_ready, 3 * (h + 1))
                act.wait_ge(eb_ready, 2 * h + 1)
                nc.scalar.activation(BB[:, 0:SEQ], BB[:, 0:SEQ], ACT.Exp, scale=1.0 / TAU).then_inc(eb_ready, 1)
                for half in range(2):
                    act.wait_ge(g_mm, 2 * h + half + 1)
                    if h:
                        act.wait_ge(omix_ready, 2 * h)
                    nc.scalar.activation(SG[:, half * 512:(half + 1) * 512], bank(half), ACT.Silu).then_inc(sg_ready, 1)
                for q in range(3):
                    act.wait_ge(kr_T, 3 * h + q + 1)
                    n = 4 if q < 2 else 2
                    nc.scalar.activation(KRT[:, 4 * q:4 * q + n],
                                         bank(5 + q)[:, 0:n * P].rearrange("p (a b) -> p a b", b=P),
                                         ACT.Copy).then_inc(krt_ready, 1)
                for i in range(TT):
                    act.wait_ge(o_mm, TT * h + i + 1)
                    nc.scalar.activation(OT[:, i], bank((7, 0)[i % 2])[:, 0:P], ACT.Copy).then_inc(o_copied, 1)
                act.wait_ge(oss_ready, h + 1)
                nc.scalar.activation(rstd[:, 0:TT], rstd[:, 0:TT], ACT.Sqrt).then_inc(oroot_ready, 1)

            if UPTO >= 2:
                for i in range(TT + CT):
                    act.wait_ge(v_mm, i + 1)
                    nc.scalar.activation(HEAD_V[:, i], bank(i % 4), ACT.Copy).then_inc(v_ready, 1)
                for q in range(3):
                    act.wait_ge(r_mm, q + 1)
                    n = 512 if q < 2 else CTX
                    nc.scalar.activation(RT[:, q * 512:q * 512 + n], bank(4 + q)[0:2 * RANK, 0:n], ACT.Copy)\
                        .then_inc(r_ready, 1)
                for h in range(HEADS):
                    gla_head(h)

            if UPTO >= 3:
                for c in range(HC):
                    for par in range(2):
                        act.wait_ge(vx_T, 2 * c + par + 1)
                        nc.scalar.activation(
                            VTM[:, par, :, c * P:(c + 1) * P], bank(6 + par).rearrange("p (a b) -> p a b", b=P),
                            ACT.Copy).then_inc(vtm_ready, 1)
            if UPTO >= 4:
                for n, dst in ((0, HH1), (1, HH2)):
                    act.wait_ge(f_arg, n + 1)
                    nc.scalar.activation(dst[0:HID], ARG[0:HID], ACT.Sin).then_inc(f_sin, 1)
                for t in range(2 * KT):
                    act.wait_ge(h3_mm, 2 * t + 2)
                    if t:
                        act.wait_ge(filt_ready, t)
                    nc.scalar.activation(FTMP[:, 0], bank(2 * (t % 2) + 1), ACT.Copy).then_inc(h3_copied, 1)
            if UPTO >= 5:
                for kt in range(KT):
                    if kt:
                        act.wait_ge(yf_dve, 2 * kt)
                        act.wait_ge(yf_pool, 2 * kt)
                    for q in range(8):
                        act.wait_ge(dft_mm, 8 * kt + q + 1)
                        nc.scalar.activation(UK[:, q], bank(q), ACT.Copy).then_inc(uk_ready, 1)

            def od_gates():
                for c in range(KC):
                    act.wait_ge(od_mm, 6 * c + 2)
                    if c >= 2:
                        act.wait_ge(od_conv, c - 1)
                    nc.scalar.activation(BGT[:, c % 2], ps[:, 0:2, :].rearrange("p a b -> p (a b)"), ACT.Copy)\
                        .then_inc(bg_ready, 1)
                    act.wait_ge(od_mm, 6 * c + 4)
                    nc.scalar.activation(CONVT[:, c % 2], ps[:, 2:4, :].rearrange("p a b -> p (a b)"), ACT.Copy)\
                        .then_inc(bg_ready, 1)

            def routing(l):
                act.wait_ge(gexp_in, 2 * l + 1)
                nc.scalar.activation(GRP[:, 1], GRP[:, 1], ACT.Exp).then_inc(gexp_out, 1)
                act.wait_ge(gexp_in, 2 * l + 2)
                nc.scalar.activation(SC[:, 4], SC[:, 4], ACT.Exp).then_inc(gexp_out, 1)

            def experts(l):
                e0 = l * (NE // 2)
                with act.Fori(0, NE // 2) as i:
                    for b in range(2):
                        act.wait_ge(up_mm[b], i + e0 + 1)
                        nc.scalar.activation(SL, bank(2), ACT.Silu).then_inc(sl_ready[b], 1)
                        act.wait_ge(hb_T[b], i + e0 + 1)
                        nc.scalar.activation(HT, bank(4), ACT.Copy).then_inc(ht_ready[b], 1)

            def overflow(l):
                flag = act.value_load(ANY[0:1, 0:1])
                with act.If(flag > 0):
                    with act.Fori(0, NOV) as n:
                        act_flag = act.value_load(ACTIVE[0:1, bass.ds(n + NE, 1)])
                        with act.If(act_flag > 0):
                            act.wait_ge(ov_up, n + (l * NOV + 1))
                            nc.scalar.activation(SL, bank(2), ACT.Silu).then_inc(ov_sl, 1)
                            act.wait_ge(ov_hT, n + (l * NOV + 1))
                            nc.scalar.activation(HT, bank(4), ACT.Copy).then_inc(ov_ht, 1)
                        with act.Else():
                            act.sem_inc(ov_sl, 1)
                            act.sem_inc(ov_ht, 1)
                with act.Else():
                    act.sem_inc(ov_sl, NOV)
                    act.sem_inc(ov_ht, NOV)
                act.sem_inc(ov_left, 1)

            if UPTO >= 7:
                for l in range(DEPTH):
                    if l:
                        norm(2, H, at(32768, 2, D))
                        od_gates()
                    norm(2 * l + 1, H, at(30720, 2, D))
                    routing(l)
                    experts(l)
                    act.wait_ge(tab_ready, l + 1)
                    overflow(l)
                norm(4, H, at(32768, 2, D))

        @block.tensor
        def _(pe):
            def slab_in(n, loads=1):
                before = sum(3 if (L0_HY <= m < L0_OUT or L1_IN <= m < L1_OUT) else 1
                             for m in range(n % RING, n, RING))
                pe.wait_ge(slab_full[n % RING], 16 * (before + loads))

            def modulation(l, first):
                pe.wait_ge(s_vec, 48 * (l + 1))
                if l == 0:
                    pe.wait_ge(s_cst, 16)
                    pe.wait_ge(pool_step, 2)
                    pe.wait_ge(s_rows, 16 * 13)
                    nc.tensor.transpose(bank(5)[:, 0:N_ROWS], small_rows[:], ident[0:N_ROWS, 0:N_ROWS])\
                        .then_inc(rows_T, 1)
                    for j in range(KC):
                        ins = nc.tensor.transpose(bank(6)[:, j * N_VEC:(j + 1) * N_VEC], VEC[:, j::KC],
                                                  ident[0:N_VEC, 0:N_VEC])
                    ins.then_inc(vec_T, 1)
                pe.wait_ge(silu_ready, 1)

                def section(s):
                    pe.wait_ge(mod_row, l * NMOD + 2 * s + 2)
                    for j in range(KC):
                        ins = nc.tensor.transpose(bank(2)[:, (s * KC + j) * 2:(s * KC + j) * 2 + 2],
                                                  MROW[0:2, s % 2, j::KC], ident[0:2, 0:2])
                    ins.then_inc(mod_T, 1)
                    if s % 3 == 2:
                        g = s // 3
                        for half in range(2):
                            sl = slice(half * 512, (half + 1) * 512)
                            pe.wait_ge(mod_gate, 4 * l + 2 * g)
                            nc.tensor.matmul(bank(3 + half), ident[0:2, 0:1].to_broadcast([2, P]),
                                             MROW[0:2, s % 2, sl], start=True, stop=False)
                            r = l * 6 + s
                            nc.tensor.matmul(bank(3 + half), ident[0:N_VEC, r:r + 1].to_broadcast([N_VEC, P]),
                                             VEC[:, sl], start=False, stop=True).then_inc(mod_bc, 1)

                for n in range(NMOD):
                    slab_in(first + n)
                    if n >= 2:
                        pe.wait_ge(mod_row, l * NMOD + n - 1)
                    w = slab(first + n, KC, 512)
                    for j in range(KC):
                        ins = nc.tensor.matmul(bank(n % 2)[0:2], silu_c[:, j], w[:, j], start=j == 0, stop=j == KC - 1)
                    ins.then_inc(mod_mm, 1)
                    if n >= 2 and n % 2 == 0:
                        section(n // 2 - 1)
                section(5)

            def transposes(n, i, xn):
                pe.wait_ge(xn_ready, norm_base[n] + i + 1)
                if i >= 2:
                    pe.wait_ge(u_ready, norm_base[n] + i - 1)
                for j in range(KC):
                    ins = nc.tensor.transpose(bank(4 * (i % 2) + j // 4)[:, (j % 4) * P:(j % 4 + 1) * P],
                                              xn[:, i % 2, j * P:(j + 1) * P], ident)
                ins.then_inc(xn_T, 1)

            modulation(0, 0)
            for i in range(TT + CT):
                if i == 0:
                    pe.wait_ge(mod_ready, 1)
                transposes(0, i, at(41984, 2, D))

            def u_cols(i, j):
                return U[:, j, i * P:(i + 1) * P] if i < TT else UC[:, j, (i - TT) * P:(i - TT + 1) * P]

            def u_part(q, j):
                return U[:, j, q * 512:(q + 1) * 512] if q < 2 else UC[:, j]

            def gla_projections():
                slab_in(L0_V)
                w = slab(L0_V, KC, GV)
                for i in range(TT + CT):
                    if i == 0:
                        pe.wait_ge(u_ready, TT + CT)
                    if i >= 4:
                        pe.wait_ge(v_ready, i - 3)
                    for j in range(KC):
                        ins = nc.tensor.matmul(bank(i % 4), u_cols(i, j), w[:, j], start=j == 0, stop=j == KC - 1)
                    ins.then_inc(v_mm, 1)
                pe.wait_ge(s_wr, 16)
                for q in range(3):
                    n = 512 if q < 2 else CTX
                    for j in range(KC):
                        ins = nc.tensor.matmul(bank(4 + q)[0:2 * RANK, 0:n], w_rank[:, j], u_part(q, j),
                                               start=j == 0, stop=j == KC - 1)
                    ins.then_inc(r_mm, 1)

            def gla_head(h):
                wqk = slab(L0_QK, KC, 2 * QK)
                if h % 2 == 0:
                    slab_in(L0_QK)
                    if h == 0:
                        pe.wait_ge(v_ready, TT + CT)
                        pe.wait_ge(r_ready, 3)
                    else:
                        pe.wait_ge(omix_ready, 2 * h)
                        pe.wait_ge(o_copied, TT * h)
                        pe.wait_ge(state_ready, h)
                    for q in range(5):
                        part = q if q < 2 else q - 2
                        n = 512 if part < 2 else CTX
                        c0 = (0 if q < 2 else QK) + (h // 2) * P
                        for j in range(KC):
                            ins = nc.tensor.matmul(bank(q)[:, 0:n], wqk[:, j, c0:c0 + P], u_part(part, j),
                                                   start=j == 0, stop=j == KC - 1)
                        ins.then_inc(qk_mm, 1)
                if h:
                    pe.wait_ge(at_ready, TT * h)
                    pe.wait_ge(o_copied, TT * h)
                for q in range(3):
                    n = 512 if q < 2 else CTX
                    nc.tensor.matmul(bank(5 + q)[:, 0:n], w_gate_up[:, h], RT[:, q * 512:q * 512 + n],
                                     start=True, stop=True).then_inc(gx_mm, 1)
                slab_in(L0_G)
                pe.wait_ge(qk_ready, 5 * (h // 2 + 1))
                if h:
                    pe.wait_ge(omix_ready, 2 * h)
                wg = slab(L0_G, KC, GV)
                for half in range(2):
                    for j in range(KC):
                        ins = nc.tensor.matmul(bank(half), wg[:, j, h * DV:(h + 1) * DV], u_part(half, j),
                                               start=j == 0, stop=j == KC - 1)
                    ins.then_inc(g_mm, 1)
                pe.wait_ge(gx_read, 6 * (h + 1))
                pe.wait_ge(kr_ready, 3 * h + 1)
                for q in range(3):
                    for i in range(4 * q, min(4 * q + 4, TT + CT)):
                        ins = nc.tensor.transpose(bank(5 + q)[:, (i % 4) * P:(i % 4 + 1) * P],
                                                  T1[:, i * P:(i + 1) * P], ident)
                    ins.then_inc(kr_T, 1)
                pe.wait_ge(krt_ready, 3 * (h + 1))
                pe.wait_ge(sg_ready, 2 * (h + 1))
                for c in range(NCH + NCC):
                    r = slice((c % 2) * CH, (c % 2 + 1) * CH)
                    ins = nc.tensor.matmul(ds_place(c), KRT[r, c // 2],
                                           HEAD_V[r, c // 2, h * DV:(h + 1) * DV], start=True, stop=True)
                ins.then_inc(ds_mm, 1)

                def scores(i):
                    cols_ = slice(i * P, (i + 1) * P)
                    for d in range(2):
                        r = slice(d * DK, (d + 1) * DK)
                        ins = nc.tensor.matmul(bank((5, 1)[i % 2] + d)[:, 0:P], KD[r, cols_], Q[r, cols_],
                                               start=True, stop=True)
                    ins.then_inc(a_mm, 1)

                pe.wait_ge(qd_ready, h + 1)
                scores(0)
                pe.wait_ge(state_ready, h + 1)
                scores(1)
                for i in range(TT):
                    if i >= 2:
                        pe.wait_ge(o_copied, TT * h + i - 1)
                    pe.wait_ge(at_ready, TT * h + i + 1)
                    o = bank((7, 0)[i % 2])[:, 0:P]
                    v = HEAD_V[:, i, h * DV:(h + 1) * DV]
                    nc.tensor.matmul(o, AT[:, i % 2, 0], v, start=True, stop=False, skip_group_check=True)
                    nc.tensor.matmul(o, AT[:, i % 2, 1], v, start=False, stop=False, skip_group_check=True)
                    for c in range(2):
                        rows = slice(c * CH, (c + 1) * CH)
                        t0 = (2 * i + c) * CH
                        ins = nc.tensor.matmul(o[rows], Q[:, t0:t0 + CH], ST[:, 2 * i + c], start=False, stop=c == 1,
                                               skip_group_check=True)
                    ins.then_inc(o_mm, 1)
                    if i + 2 < TT:
                        scores(i + 2)
                pe.wait_ge(on_ready, h + 1)
                for half in range(2):
                    for i in range(4 * half, 4 * half + 4):
                        ins = nc.tensor.transpose(bank(3 + half)[:, (i % 4) * P:(i % 4 + 1) * P], OT[:, i], ident)
                    ins.then_inc(o_T, 1)

            if UPTO >= 2:
                gla_projections()
                for h in range(HEADS):
                    gla_head(h)

            def hyena_projection():
                pe.wait_ge(omix_ready, 2 * HEADS)
                for c in range(HC):
                    slab_in(L0_HY + c, 3)
                    w = slab(L0_HY + c, 3, KC, P)
                    for k in range(3):
                        if c:
                            pe.wait_ge(conv_done, 3 * (c - 1) + k + 1)
                        for half in range(2):
                            for j in range(KC):
                                ins = nc.tensor.matmul(bank(2 * k + half), w[:, k, j], u_part(half, j),
                                                       start=j == 0, stop=j == KC - 1)
                            ins.then_inc(hy_mm, 1)
                    if c:
                        hyena_transposes(c - 1)
                hyena_transposes(HC - 1)

            def hyena_transposes(c):
                pe.wait_ge(vx_ready, c + 1)
                for par in range(2):
                    if c:
                        pe.wait_ge(vtm_ready, 2 * (c - 1) + par + 1)
                    for tc in range(KT):
                        ins = nc.tensor.transpose(bank(6 + par)[:, tc * P:(tc + 1) * P],
                                                  VX[:, c, par + 2 * tc * P:par + 2 * (tc + 1) * P - 1:2], ident)
                    ins.then_inc(vx_T, 1)

            if UPTO >= 3:
                hyena_projection()

            def hyena_filters():
                pe.wait_ge(flt_in, 64)
                pe.wait_ge(vtm_ready, 2 * HC)
                pe.wait_ge(conv_done, 3 * HC)
                for half in range(2):
                    nc.tensor.matmul(bank(half)[0:HID], w_hy1[:], ZT[0:EMB, half * 512:(half + 1) * 512],
                                     start=True, stop=True).then_inc(f_mm, 1)
                pe.wait_ge(f_sin, 1)
                for half in range(2):
                    nc.tensor.matmul(bank(2 + half)[0:HID], w_hy2[:], HH1[0:HID, half * 512:(half + 1) * 512],
                                     start=True, stop=True).then_inc(f_mm, 1)
                pe.wait_ge(f_sin, 2)
                for t in range(2 * KT):
                    par, tc = t // KT, t % KT
                    if t >= 2:
                        pe.wait_ge(filt_ready, t - 1)
                    for k in range(2):
                        nc.tensor.matmul(bank(2 * (t % 2) + k),
                                         HH2[0:HID, par + 2 * tc * P:par + 2 * (tc + 1) * P - 1:2],
                                         W3H[0:HID, k * HW:(k + 1) * HW], start=True, stop=True).then_inc(h3_mm, 1)

            if UPTO >= 4:
                hyena_filters()

            def transform():
                pe.wait_ge(dft_in, 16)
                pe.wait_ge(filt_ready, 2 * KT)
                for kt in range(KT):
                    for q in range(8):
                        fn, par = (q % 4) // 2, q % 2
                        if kt:
                            pe.wait_ge(uk_ready, 8 * (kt - 1) + q + 1)
                        for tc in range(KT):
                            rhs = VTM[:, par, tc] if q < 4 else (HSUM, HDIF)[fn][:, par * KT + tc]
                            ins = nc.tensor.matmul(bank(q), DFT[:, kt, fn, par, tc * P:(tc + 1) * P], rhs,
                                                   start=tc == 0, stop=tc == KT - 1)
                        ins.then_inc(dft_mm, 1)

            def inverse():
                pe.wait_ge(idft_in, 16)
                pe.wait_ge(uk_ready, 8 * KT)
                pe.wait_ge(yf_dve, 2 * KT)
                pe.wait_ge(yf_pool, 2 * KT)
                for c in range(HC):
                    for par in range(2):
                        for fn in range(2):
                            for kt in range(KT):
                                ins = nc.tensor.matmul(
                                    bank(2 * (c % 4) + par), YF[:, kt, 2 * fn + par, c * P:(c + 1) * P],
                                    IDFT[:, fn, par, kt * HALF:(kt + 1) * HALF],
                                    start=fn == 0 and kt == 0, stop=fn == 1 and kt == KT - 1)
                        ins.then_inc(idft_mm, 1)

            if UPTO >= 5:
                transform()
                inverse()

            def projection_out(l, first, mixed):
                for i in range(TT):
                    for half in range(2):
                        n = 2 * i + half
                        if i == 0:
                            slab_in(first + half)
                        if n >= 4:
                            pe.wait_ge(h_ready, 2 * TT * l + n - 3)
                        for j in range(KC):
                            ins = nc.tensor.matmul(bank(n % 4), mixed[:, j, i * P:(i + 1) * P],
                                                   slab(first + half, KC, 512)[:, j],
                                                   start=j == 0, stop=j == KC - 1)
                        ins.then_inc(out_mm, 1)

            if UPTO >= 6:
                pe.wait_ge(hmix_ready, 2 * HC)
                projection_out(0, L0_OUT, MIX)

            def router(l):
                n = 2 * l + 1
                pe.wait_ge(rt_in, 64 * (l + 1))
                pe.wait_ge(h_ready, 2 * TT * (l + 1))

                def logits(i):
                    pe.wait_ge(u_ready, norm_base[n] + i + 1)
                    if i >= 2:
                        pe.wait_ge(lg_ready, l * TT + i - 1)
                    lg = bank(2 + 4 * (i % 2))[:, 0:NG + NE]
                    for j in range(KC):
                        nc.tensor.matmul(lg, VTT[:, i % 2, j * P:(j + 1) * P], W_RT[:, j], start=j == 0, stop=False)
                    nc.tensor.matmul(lg, cst[0:1, K_ONE:K_ONE + P], B_RT[0:1], start=False, stop=True)\
                        .then_inc(lg_mm, 1)

                for i in range(TT):
                    transposes(n, i, at(24576, 2, D))
                    if i:
                        logits(i - 1)
                logits(TT - 1)

            def slots(l):
                pe.wait_ge(oh_ready, l + 1)
                ones = cst[:, K_ONE:K_ONE + P]
                pe.wait_ge(lg_ready, (l + 1) * TT)
                nc.tensor.matmul(bank(0)[:, 0:TT * NE], cst[:, K_UT:K_UT + P], SUMOH, start=True, stop=False,
                                 skip_group_check=True)
                for d in range(1, TT):
                    ins = nc.tensor.matmul(bank(0)[:, d * NE:TT * NE], ones, SUMOH[:, 0:(TT - d) * NE],
                                           start=False, stop=d == TT - 1, skip_group_check=True)
                ins.then_inc(pos_mm, 1)
                for i in range(TT):
                    ins = nc.tensor.matmul(bank(1)[:, 0:NE], ones, SUMOH[:, i * NE:(i + 1) * NE],
                                           start=i == 0, stop=i == TT - 1)
                ins.then_inc(pos_mm, 1)
                for n in range(2 * TT):
                    pe.wait_ge(hot_ready, 2 * TT * l + n + 1)
                    ins = nc.tensor.matmul(bank(3), HOT[:, n % 2], RHS[:, n % 2].rearrange("p a b -> p (a b)"),
                                           start=n == 0, stop=n == 2 * TT - 1)
                    ins.then_inc(tab_mm, 1)

            def experts(l):
                e0 = l * (NE // 2)

                def turn(b, i):
                    pe.wait_ge(x_full[b], (i + e0 + 1) * 16)
                    for j in range(KC):
                        ins = nc.tensor.transpose(bank(j // 4)[:, (j % 4) * P:(j % 4 + 1) * P],
                                                  XG[:, b, j * P:(j + 1) * P], ident)
                        if j % 4 == 3:
                            ins.then_inc(x_T[b], 1)

                def expert(b, i, first, last):
                    x = XT[:, b].rearrange("p (j t) -> p j t", j=KC)
                    pe.wait_ge(xt_ready[b], (i + e0 + 1) * 2)
                    for m, done in ((0, up_mm), (1, gate_mm)):
                        pe.wait_ge(w_full[b][m], (i + e0 + 1) * 16)
                        w = w_slot(b, m, KC, FE)
                        for j in range(KC):
                            ins = nc.tensor.matmul(bank(2 + m), x[:, j], w[:, j], start=j == 0, stop=j == KC - 1)
                        ins.then_inc(done[b], 1)
                    if not last:
                        turn(1 - b, i + b)
                    pe.wait_ge(hb_ready[b], i + e0 + 1)
                    for j in range(FC):
                        ins = nc.tensor.transpose(bank(4)[:, j * P:(j + 1) * P], HB[:, j * P:(j + 1) * P], ident)
                    ins.then_inc(hb_T[b], 1)
                    pe.wait_ge(ht_ready[b], i + e0 + 1)
                    pe.wait_ge(w_full[b][2], (i + e0 + 1) * 16)
                    if b:
                        pe.wait_ge(y_ready[0], (i + e0 + 1) * 2)
                    elif not first:
                        pe.wait_ge(y_ready[1], (i + e0) * 2)
                    w = w_slot(b, 2, FC, D)
                    for half in range(2):
                        for j in range(FC):
                            ins = nc.tensor.matmul(bank(5 + half), HT[:, j * P:(j + 1) * P],
                                                   w[:, j, half * 512:(half + 1) * 512],
                                                   start=j == 0, stop=j == FC - 1)
                        ins.then_inc(y_mm[b], 1)

                pe.wait_ge(tab_ready, l + 1)
                turn(0, 0)
                for b in range(2):
                    expert(b, 0, l == 0, False)
                with pe.Fori(0, NE // 2 - 2) as i:
                    for b in range(2):
                        expert(b, i + 1, False, False)
                for b in range(2):
                    expert(b, NE // 2 - 1, False, b == 1)

            def overflow(l):
                flag = pe.value_load(ANY[0:1, 0:1])
                with pe.If(flag > 0):
                    with pe.Fori(0, NOV) as n:
                        act_flag = pe.value_load(ACTIVE[0:1, bass.ds(n + NE, 1)])
                        with pe.If(act_flag > 0):
                            pe.wait_ge(ov_x, (n + (l * NOV + 1)) * 16)
                            for j in range(KC):
                                ins = nc.tensor.transpose(bank(j // 4)[:, (j % 4) * P:(j % 4 + 1) * P],
                                                          XG[:, 0, j * P:(j + 1) * P], ident)
                            ins.then_inc(ov_xT, 1)
                            pe.wait_ge(ov_xt, n + (l * NOV + 1))
                            for m, done in ((0, ov_up), (1, ov_gate)):
                                pe.wait_ge(ov_w[m], (n + (l * NOV + 1)) * 16)
                                for j in range(KC):
                                    ins = nc.tensor.matmul(bank(2 + m), XT[:, 0, j * P:(j + 1) * P],
                                                           w_slot(0, m, KC, FE)[:, j],
                                                           start=j == 0, stop=j == KC - 1)
                                ins.then_inc(done, 1)
                            pe.wait_ge(ov_hb, n + (l * NOV + 1))
                            for j in range(FC):
                                ins = nc.tensor.transpose(bank(4)[:, j * P:(j + 1) * P], HB[:, j * P:(j + 1) * P],
                                                          ident)
                            ins.then_inc(ov_hT, 1)
                            pe.wait_ge(ov_ht, n + (l * NOV + 1))
                            pe.wait_ge(ov_w[2], (n + (l * NOV + 1)) * 16)
                            for half in range(2):
                                for j in range(FC):
                                    ins = nc.tensor.matmul(bank(5 + half), HT[:, j * P:(j + 1) * P],
                                                           w_slot(0, 2, FC, D)[:, j, half * 512:(half + 1) * 512],
                                                           start=j == 0, stop=j == FC - 1)
                            ins.then_inc(ov_ymm, 1)
                        with pe.Else():
                            for s in (ov_xT, ov_up, ov_gate, ov_hT, ov_ymm):
                                pe.sem_inc(s, 1)
                with pe.Else():
                    pe.sem_inc(ov_xT, NOV)
                    pe.sem_inc(ov_up, NOV)
                    pe.sem_inc(ov_gate, NOV)
                    pe.sem_inc(ov_hT, NOV)
                    pe.sem_inc(ov_ymm, NOV)
                pe.sem_inc(ov_left, 1)

            def shortconv():
                pe.wait_ge(h_ready, 2 * TT)
                for i in range(TT):
                    if i == 0:
                        pe.wait_ge(mod_ready, 2)
                    transposes(2, i, at(28672, 2, D))
                pe.wait_ge(u_ready, norm_base[2] + TT)
                for c in range(KC):
                    slab_in(L1_IN + c, 3)
                    w = slab(L1_IN + c, 3, KC, P)
                    for k in range(3):
                        if c:
                            if k < 2:
                                pe.wait_ge(bg_ready, 2 * (c - 1) + k + 1)
                            else:
                                pe.wait_ge(od_conv, c)
                        for half in range(2):
                            for j in range(KC):
                                ins = nc.tensor.matmul(bank(2 * k + half), w[:, k, j], u_part(half, j),
                                                       start=j == 0, stop=j == KC - 1)
                            ins.then_inc(od_mm, 1)
                pe.wait_ge(od_conv, KC)
                projection_out(1, L1_OUT, GTM)

            if UPTO >= 7:
                for l in range(DEPTH):
                    if l:
                        modulation(1, L1_MOD)
                        shortconv()
                    router(l)
                    slots(l)
                    experts(l)
                    overflow(l)

        @block.vector
        def _(dve):
            count = [0]

            def step(ins):
                count[0] += 1
                ins.then_inc(dve_step, 1)
                return count[0]

            def settle(n=None):
                dve.wait_ge(dve_step, count[0] if n is None else n)

            def link(ins):
                step(ins)
                settle()

            V = nc.vector

            def norm(n, src, xn, target, gain, shift):
                dve.wait_ge(sq_done, norm_base[n + 1])
                m = NORMS[n]
                V.tensor_scalar(rstd[:, 0:m], ss[:, 0:m], 1.0 / D, EPS, ALU.mult, ALU.add).then_inc(ms_ready, 1)
                dve.wait_ge(root_ready, n + 1)
                link(V.reciprocal(rstd[:, 0:m], rstd[:, 0:m]))

                def columns(i):
                    dve.wait_ge(xn_T, norm_base[n] + i + 1)
                    if n in (1, 3) and i >= 2:
                        dve.wait_ge(lg_mm, (n // 2) * TT + i - 1)
                    for j in range(KC):
                        ins = V.tensor_scalar(target(i, j), bank(4 * (i % 2) + j // 4)[:, (j % 4) * P:(j % 4 + 1) * P],
                                              gain(i, j), shift(i, j), ALU.mult, ALU.add)
                    ins.then_inc(u_ready, 1)
                    if n in (1, 3) and i:
                        logits(n // 2, i - 1)

                for i in range(m):
                    if i >= 2:
                        dve.wait_ge(xn_T, norm_base[n] + i - 1)
                        if n in (1, 3):
                            dve.wait_ge(hn_out[i % 2], 16 * ((n // 2) * (TT // 2) + i // 2))
                    V.tensor_scalar(xn[:, i % 2].rearrange("t (c p) -> t p c", p=P),
                                    src[:, i].rearrange("t (p c) -> t p c", c=KC),
                                    rstd[:, i:i + 1], None, ALU.mult).then_inc(xn_ready, 1)
                    if i:
                        columns(i - 1)
                columns(m - 1)
                if n in (1, 3):
                    logits(n // 2, m - 1)

            def logits(l, i):
                dve.wait_ge(lg_mm, l * TT + i + 1)
                V.tensor_copy(LG[:, i], bank(2 + 4 * (i % 2))[:, 0:NG + NE]).then_inc(lg_ready, 1)

            def modulation(l):
                if l == 0:
                    dve.wait_ge(rows_T, 1)
                    link(V.tensor_copy(cols[:], bank(5)[:, 0:N_ROWS]))
                    V.tensor_scalar(neg_ba[:], cols[:, R_BA:R_HY], -1.0, None, ALU.mult).then_inc(cols_ready, 1)
                    dve.wait_ge(vec_T, 1)
                    step(V.tensor_copy(vec_cols[:], bank(6)[:, 0:KC * N_VEC].rearrange("p (a b) -> p a b", b=N_VEC)))
                for n in range(NMOD):
                    dve.wait_ge(mod_mm, l * NMOD + n + 1)
                    s = n // 2
                    if s >= 2:
                        dve.wait_ge(mod_T, l * 6 + s - 1)
                    if s >= 4:
                        dve.wait_ge(mod_bc, 4 * l + 2)
                    V.tensor_copy(MROW[0:2, s % 2, (n % 2) * 512:(n % 2 + 1) * 512], bank(n % 2)[0:2])\
                        .then_inc(mod_row, 1)
                    if n == 8:
                        gates_out(l, 0)
                dve.wait_ge(mod_T, 6 * (l + 1))
                for s in range(6):
                    for r in range(2):
                        ps_col = bank(2)[:, s * KC * 2:(s + 1) * KC * 2].rearrange("p (j r) -> p j r", r=2)[:, :, r]
                        step(V.tensor_tensor(mod[:, s, :, r], ps_col, vec_cols[:, :, l * 6 + s], ALU.add))
                settle()
                for k, (s, r, v) in enumerate([(1, 0, V_NMIX), (1, 1, V_NMIX), (4, 0, V_NFFN)]):
                    step(V.scalar_tensor_tensor(out=gain_x[:, k], in0=mod[:, s, :, r], scalar=1.0,
                                                in1=vec_cols[:, :, v + l], op0=ALU.add, op1=ALU.mult))
                gates_out(l, 1)
                settle()
                dve.wait_ge(mod_gate, 4 * (l + 1))
                dve.sem_inc(mod_ready, 1)

            def gates_out(l, g):
                for half in range(2):
                    dve.wait_ge(mod_bc, 4 * l + 2 * g + half + 1)
                    V.tensor_copy(gates[:, g, half * 512:(half + 1) * 512], bank(3 + half)).then_inc(mod_gate, 1)

            dve.wait_ge(s_cst, 16)
            for k in range(2):
                step(V.tensor_scalar(row_number[:, k], cst[:, K_TV:K_TV + TT], float(k) - FAR, None, ALU.add))
            modulation(0)
            norm(0, X0, at(41984, 2, D),
                 lambda i, j: U[:, j, i * P:(i + 1) * P] if i < TT else UC[:, j, (i - TT) * P:(i - TT + 1) * P],
                 lambda i, j: gain_x[:, i // TT, j:j + 1],
                 lambda i, j: mod[:, 0, j, i // TT:i // TT + 1])

            def gla_head(h):
                for q in range(3):
                    n = 512 if q < 2 else CTX
                    cs = slice(q * 512, q * 512 + n)
                    dve.wait_ge(gx_mm, 3 * h + q + 1)
                    V.tensor_scalar(T1[:, cs], bank(5 + q)[:, 0:n], cols[:, R_BA + h:R_BA + h + 1], 0.0,
                                    ALU.add, ALU.min).then_inc(gx_read, 1)
                for q in range(3):
                    n = 512 if q < 2 else CTX
                    cs = slice(q * 512, q * 512 + n)
                    dve.wait_ge(gx_read, 6 * h + 3 + q)
                    V.scalar_tensor_tensor(out=BB[:, cs], in0=T1[:, cs], scalar=2.0, in1=bank(5 + q)[:, 0:n],
                                           op0=ALU.mult, op1=ALU.subtract).then_inc(gx_read, 1)
                dve.wait_ge(ln_ready, h + 1)
                link(V.tensor_tensor(T1, T1, BB, ALU.subtract))
                step(V.tensor_tensor_scan(BB[0:DK], SCAN1[0:DK], T1[0:DK], 0.0, ALU.mult, ALU.add))
                link(V.tensor_tensor_scan(BB[DK:P, TOK - 1::-1], SCAN1[DK:P], T1[DK:P, TOK - 1::-1], 0.0,
                                          ALU.mult, ALU.add))
                bv = BB.rearrange("p (c t) -> p c t", t=CH)
                tv = T1.rearrange("p (c t) -> p c t", t=CH)
                shape = [DK, NCH + NCC, CH]
                V.tensor_tensor(tv[0:DK], bv[0:DK, :, CH - 1:CH].to_broadcast(shape), bv[0:DK], ALU.subtract)\
                    .then_inc(cum_ready, 1)
                V.tensor_tensor(tv[DK:P], bv[DK:P, :, 0:1].to_broadcast(shape), bv[DK:P], ALU.subtract)\
                    .then_inc(cum_ready, 1)
                dve.wait_ge(er_ready, 3 * h + 1)
                dve.wait_ge(dup_pool, 2 * (h + 1))
                V.tensor_tensor(T1, K, T1, ALU.mult).then_inc(kr_ready, 1)
                dve.wait_ge(eb_ready, 2 * h + 1)
                V.tensor_tensor(KD, K[:, 0:SEQ], KD, ALU.mult).then_inc(kr_ready, 1)
                dve.wait_ge(eb_ready, 2 * h + 2)
                dve.wait_ge(dup_act, 2 * (h + 1))
                V.tensor_tensor(Q, Q, BB[:, 0:SEQ], ALU.mult).then_inc(kr_ready, 1)
                dve.wait_ge(kr_ready, 3 * (h + 1))
                dve.sem_inc(qd_ready, 1)

                dve.wait_ge(ds_mm, h + 1)
                dve.wait_ge(er_ready, 3 * (h + 1))

                def ds(c, r):
                    return ds_place(c)[r]

                fw, bw = slice(0, DK), slice(DK, P)
                order = {0: [NCH + n for n in range(NCC)] + list(range(NCH)),
                         1: [NCH + NCC - 1 - n for n in range(NCC)] + list(range(NCH - 1, -1, -1))}
                last = [0, 0]
                for n in range(NCC + NCH - 1):
                    for d, r in ((0, fw), (1, bw)):
                        c = order[d][n]
                        nxt = order[d][n + 1]
                        dst = (SCTX if n < NCC - 1 else ST[:, nxt])[r]
                        if n == 0:
                            last[d] = step(V.tensor_copy(dst, ds(c, r)))
                            continue
                        src = (SCTX if n < NCC else ST[:, c])[r]
                        settle(last[d])
                        last[d] = step(V.scalar_tensor_tensor(out=dst, in0=src, scalar=decay[r, c:c + 1],
                                                              in1=ds(c, r), op0=ALU.mult, op1=ALU.add))
                settle()
                dve.sem_inc(state_ready, 1)
                for i in range(TT):
                    dve.wait_ge(a_mm, TT * h + i + 1)
                    if h or i >= 2:
                        dve.wait_ge(o_mm, TT * h + i - 1)
                    V.copy_predicated(out=AT[:, i % 2],
                                      mask=cst[:, K_MASK:K_END].bitcast(I32).rearrange("p (a b) -> p a b", a=2),
                                      data=ps[:, (5, 1)[i % 2]:(5, 1)[i % 2] + 2, 0:P]).then_inc(at_ready, 1)
                dve.wait_ge(o_copied, TT * (h + 1))
                sq = BB[:, 0:SEQ].rearrange("p (a b) -> p a b", b=DV)
                link(V.tensor_tensor(sq, OT, OT, ALU.mult))
                link(V.tensor_reduce(ss[:, 0:TT], sq, AX.X, ALU.add))
                V.tensor_scalar(rstd[:, 0:TT], ss[:, 0:TT], 1.0 / DV, EPS, ALU.mult, ALU.add).then_inc(oss_ready, 1)
                dve.wait_ge(oroot_ready, h + 1)
                link(V.reciprocal(rstd[:, 0:TT], rstd[:, 0:TT]))
                V.tensor_tensor(OT, OT, rstd[:, 0:TT].unsqueeze(2).to_broadcast([P, TT, DV]), ALU.mult)\
                    .then_inc(on_ready, 1)
                for half in range(2):
                    dve.wait_ge(o_T, 2 * h + half + 1)
                    cs = slice(half * 512, (half + 1) * 512)
                    V.scalar_tensor_tensor(out=MIX[:, h, cs], in0=bank(3 + half), scalar=cols[:, R_GAIN:R_GAIN + 1],
                                           in1=SG[:, cs], op0=ALU.mult, op1=ALU.mult).then_inc(omix_ready, 1)

            if UPTO >= 2:
                dve.wait_ge(u_ready, TT + CT)
                step(V.memset(AT, 0.0))
                link(V.memset(SCAN1, 1.0))
                link(V.memset(SCAN1.rearrange("p (c t) -> p c t", t=CH)[:, :, 0:1], 0.0))
                for h in range(HEADS):
                    gla_head(h)

            def conv(dst, src, w0, bias):
                if bias is None:
                    link(V.tensor_scalar(dst, src, w0(1), None, ALU.mult))
                else:
                    link(V.tensor_scalar(dst, src, w0(1), bias, ALU.mult, ALU.add))
                link(V.scalar_tensor_tensor(out=dst[:, 1:], in0=src[:, 0:SEQ - 1], scalar=w0(0), in1=dst[:, 1:],
                                            op0=ALU.mult, op1=ALU.add))
                return V.scalar_tensor_tensor(out=dst[:, 0:SEQ - 1], in0=src[:, 1:], scalar=w0(2),
                                              in1=dst[:, 0:SEQ - 1], op0=ALU.mult, op1=ALU.add)

            if UPTO >= 3:
                for c in range(HC):
                    for k, dst in ((0, MIX[:, HC + c]), (1, X1C), (2, VC_)):
                        dve.wait_ge(hy_mm, 6 * c + 2 * k + 2)
                        src = ps[:, 2 * k:2 * k + 2, :].rearrange("p a b -> p (a b)")
                        r = R_CB + 4 * k + c
                        conv(dst, src, lambda w: cols[:, R_CW + 12 * w + 4 * k + c:R_CW + 12 * w + 4 * k + c + 1],
                             cols[:, r:r + 1]).then_inc(conv_done, 1)
                    dve.wait_ge(conv_done, 3 * (c + 1))
                    V.tensor_tensor(VX[:, c], VC_, X1C, ALU.mult).then_inc(vx_ready, 1)
            if UPTO >= 4:
                def sine_argument(first, b, f):
                    for half in range(2):
                        dve.wait_ge(f_mm, first + half + 1)
                        step(V.tensor_scalar(ARG[0:HID, half * 512:(half + 1) * 512], bank(first + half)[0:HID],
                                             cols[0:HID, b:b + 1], cols[0:HID, f:f + 1], ALU.add, ALU.mult))
                    settle()
                    ar, tu = ARG[0:HID], TURNS[0:HID]
                    link(V.tensor_scalar(tu, ar, 1.0 / (2 * np.pi), MAGIC, ALU.mult, ALU.add))
                    link(V.tensor_scalar(tu, tu, MAGIC, None, ALU.subtract))
                    link(V.scalar_tensor_tensor(out=ar, in0=tu, scalar=-TWO_PI_HI, in1=ar, op0=ALU.mult, op1=ALU.add))
                    link(V.scalar_tensor_tensor(out=ar, in0=tu, scalar=-TWO_PI_LO, in1=ar, op0=ALU.mult, op1=ALU.add))
                    V.tensor_scalar(ar, ar, PI_F, -PI_F, ALU.min, ALU.max).then_inc(f_arg, 1)

                sine_argument(0, R_HY, R_HY + 1)
                dve.wait_ge(f_sin, 1)
                sine_argument(2, R_HY + 2, R_HY + 3)
                dve.wait_ge(win_in, 16)
                for t in range(2 * KT):
                    dve.wait_ge(h3_copied, t + 1)
                    b = 2 * (t % 2)
                    step(V.tensor_tensor(HSUM[:, t], bank(b), FTMP[:, 0], ALU.add))
                    link(V.tensor_tensor(HDIF[:, t], bank(b), FTMP[:, 0], ALU.subtract))
                    step(V.tensor_tensor(HSUM[:, t], HSUM[:, t], WIN[:, t], ALU.mult))
                    link(V.tensor_tensor(HDIF[:, t], HDIF[:, t], WIN[:, t], ALU.mult))
                    dve.sem_inc(filt_ready, 1)
            if UPTO >= 5:
                for kt in range(KT):
                    dve.wait_ge(uk_ready, 8 * (kt + 1))
                    ua, ub, uc, ud, ka, kb, kc, kd = [UK[:, q] for q in range(8)]
                    t0, t1 = CTMP[:, 0], CTMP[:, 1]
                    for row_, terms, signs in ((0, ((ua, ka), (ub, kb), (uc, kc), (ud, kd)), (1, -1, -1)),
                                               (2, ((ua, kc), (ub, kd), (uc, ka), (ud, kb)), (1, 1, 1))):
                        step(V.tensor_tensor(t0, terms[0][0], terms[0][1], ALU.mult))
                        for q in range(3):
                            x, y = terms[q + 1]
                            link(V.tensor_tensor(t1, x, y, ALU.mult))
                            op = ALU.add if signs[q] > 0 else ALU.subtract
                            if q == 2:
                                V.tensor_tensor(YF[:, kt, row_], t0, t1, op).then_inc(yf_dve, 1)
                                dve.wait_ge(yf_dve, 2 * kt + row_ // 2 + 1)
                            else:
                                link(V.tensor_tensor(t0, t0, t1, op))
                for c in range(HC):
                    for par in range(2):
                        n = 2 * c + par
                        dve.wait_ge(idft_mm, n + 1)
                        sl = slice(par, SEQ - 1 + par, 2)
                        tmp = CTMP[:, n % 2]
                        if c:
                            dve.wait_ge(hmix_ready, n - 1)
                        link(V.scalar_tensor_tensor(out=tmp, in0=VX[:, c, sl],
                                                    scalar=cols[:, R_SKIP + c:R_SKIP + c + 1], in1=bank(n),
                                                    op0=ALU.mult, op1=ALU.add))
                        V.tensor_tensor(MIX[:, HC + c, sl], tmp, MIX[:, HC + c, sl], ALU.mult).then_inc(hmix_ready, 1)

            def residual(l, tmp):
                for n in range(2 * TT):
                    dve.wait_ge(out_mm, 2 * TT * l + n + 1)
                    cs = slice((n % 2) * 512, (n % 2 + 1) * 512)
                    link(V.tensor_tensor(tmp[:, n % 2], bank(n % 4), gates[:, 0, cs], ALU.mult))
                    V.tensor_tensor(H[:, n // 2, cs], H[:, n // 2, cs], tmp[:, n % 2], ALU.add).then_inc(h_ready, 1)

            if UPTO >= 6:
                dve.wait_ge(s_xr, 16)
                residual(0, CTMP)

            def first_of_largest(dst, values, top, iota, n, scratch):
                shape = [P, TT, n]
                link(V.tensor_tensor(scratch, values, top.unsqueeze(2).to_broadcast(shape), ALU.is_equal))
                link(V.scalar_tensor_tensor(out=scratch, in0=scratch, scalar=-64.0,
                                            in1=iota.unsqueeze(1).to_broadcast(shape), op0=ALU.mult, op1=ALU.add))
                link(V.tensor_reduce(SC[:, 15], scratch, AX.X, ALU.min))
                link(V.tensor_tensor(dst, scratch, SC[:, 15].unsqueeze(2).to_broadcast(shape), ALU.is_equal))

            def routing(l):
                dve.wait_ge(lg_ready, (l + 1) * TT)
                lg4, lge = LG[:, :, 0:NG], LG[:, :, NG:]
                e64 = cst[:, K_E64:K_E64 + NE]
                link(V.tensor_reduce(SC[:, 0], lg4, AX.X, ALU.max))
                V.tensor_tensor(GRP[:, 1], lg4, SC[:, 0].unsqueeze(2).to_broadcast([P, TT, NG]), ALU.subtract)\
                    .then_inc(gexp_in, 1)
                first_of_largest(GRP[:, 0], lg4, SC[:, 0], e64[:, 0:NG], NG, GRP[:, 2])
                link(V.tensor_scalar(GRP[:, 3], GRP[:, 0], BIG, -BIG, ALU.mult, ALU.add))
                link(V.tensor_tensor(LEX.rearrange("p t (g e) -> p t g e", g=NG),
                                     lge.rearrange("p t (g e) -> p t g e", g=NG),
                                     GRP[:, 3].unsqueeze(3).to_broadcast([P, TT, NG, EPG]), ALU.add))
                link(V.tensor_reduce(SC[:, 1], LEX, AX.X, ALU.max))
                first_of_largest(ONE_HOT[0], LEX, SC[:, 1], e64, NE, MSK)
                link(V.scalar_tensor_tensor(out=LEX, in0=ONE_HOT[0], scalar=-3.0 * BIG, in1=LEX,
                                            op0=ALU.mult, op1=ALU.add))
                link(V.tensor_reduce(SC[:, 2], LEX, AX.X, ALU.max))
                V.tensor_tensor(SC[:, 4], SC[:, 2], SC[:, 1], ALU.subtract).then_inc(gexp_in, 1)
                first_of_largest(ONE_HOT[1], LEX, SC[:, 2], e64, NE, MSK)
                link(V.tensor_tensor(SUMOH.rearrange("p (t e) -> p t e", e=NE), ONE_HOT[0], ONE_HOT[1], ALU.add))
                dve.sem_inc(oh_ready, 1)
                dve.wait_ge(gexp_out, 2 * (l + 1))
                link(V.tensor_reduce(SC[:, 3], GRP[:, 1], AX.X, ALU.add))
                link(V.tensor_scalar(SC[:, 5], SC[:, 4], 1.0, None, ALU.add))
                link(V.tensor_tensor(SC[:, 5], SC[:, 5], SC[:, 3], ALU.mult))
                link(V.reciprocal(SC[:, 6], SC[:, 5]))
                link(V.tensor_tensor(SC[:, 7], SC[:, 6], SC[:, 4], ALU.mult))
                dve.wait_ge(pos_mm, 2 * l + 1)
                link(V.tensor_copy(POSM, bank(0)[:, 0:TT * NE].rearrange("p (t e) -> p t e", e=NE)))
                for k in range(2):
                    link(V.tensor_tensor(MSK, ONE_HOT[k], POSM, ALU.mult))
                    link(V.tensor_reduce(SC[:, 8 + k], MSK, AX.X, ALU.add))
                    link(V.tensor_scalar(SC[:, 10 + k], SC[:, 8 + k], float(P), None, ALU.is_ge))
                    for j in range(2, NJ):
                        link(V.tensor_scalar(SC[:, 14], SC[:, 8 + k], float(P * j), None, ALU.is_ge))
                        link(V.tensor_tensor(SC[:, 10 + k], SC[:, 10 + k], SC[:, 14], ALU.add))
                    link(V.scalar_tensor_tensor(out=SC[:, 12 + k], in0=SC[:, 10 + k], scalar=-float(P),
                                                in1=SC[:, 8 + k], op0=ALU.mult, op1=ALU.add))
                dve.wait_ge(pos_mm, 2 * l + 2)
                for j in range(NJ):
                    step(V.tensor_scalar(ACTIVE_F[:, j], bank(1)[:, 0:NE], float(P * j), None, ALU.is_gt))
                settle()
                link(V.tensor_reduce(ANY_F[:, 0:1], ACTIVE_F[:, 1], AX.X, ALU.max))
                step(V.tensor_copy(ANY[:, 0:1], ANY_F[:, 0:1]))
                link(V.tensor_copy(ACTIVE, ACTIVE_F.rearrange("p a b -> p (a b)")))
                for n in range(2 * TT):
                    i, k = n // 2, n % 2
                    if l or n >= 2:
                        dve.wait_ge(tab_mm, 2 * TT * l + n - 1)
                    step(V.tensor_scalar(HOT[:, k], cst[:, K_IOTA:K_IOTA + P], SC[:, 12 + k, i:i + 1], None,
                                         ALU.is_equal))
                    step(V.tensor_scalar(JEQ[:, k], cst[:, K_J:K_J + NJ], SC[:, 10 + k, i:i + 1], None, ALU.is_equal))
                    step(V.tensor_scalar(OV[:, k, 0], ONE_HOT[k][:, i], row_number[:, k, i:i + 1], None, ALU.mult))
                    link(V.tensor_scalar(OV[:, k, 1], ONE_HOT[k][:, i], SC[:, 6 + k, i:i + 1], None, ALU.mult))
                    shape = [P, NJ, NE]
                    for m in range(2):
                        ins = V.tensor_tensor(RHS[:, k, m].rearrange("p (a b) -> p a b", b=NE),
                                              JEQ[:, k].unsqueeze(2).to_broadcast(shape),
                                              OV[:, k, m].unsqueeze(1).to_broadcast(shape), ALU.mult)
                        if m == 0:
                            step(ins)
                        else:
                            link(ins)
                    dve.sem_inc(hot_ready, 1)
                dve.wait_ge(tab_mm, 2 * TT * (l + 1))
                step(V.tensor_copy(GATE_OF, bank(3)[:, NJ * NE:2 * NJ * NE]))
                link(V.tensor_scalar(SLOT_F, bank(3)[:, 0:NJ * NE], FAR, None, ALU.add))
                link(V.tensor_copy(SLOT_ROW, SLOT_F))
                link(V.tensor_scalar(SLOT_TOK, SLOT_ROW, 1, None, ALU.logical_shift_right))
                dve.sem_inc(tab_ready, 1)

            def columns_of_x(b, done, halves):
                for j in range(KC):
                    ins = V.tensor_scalar(XT[:, b, j * P:(j + 1) * P],
                                          bank(j // 4)[:, (j % 4) * P:(j % 4 + 1) * P],
                                          gain_x[:, 2, j:j + 1], mod[:, 3, j, 0:1], ALU.mult, ALU.add)
                    if j % 4 == 3 and halves or j == KC - 1:
                        ins.then_inc(done, 1)

            def experts(l):
                e0 = l * (NE // 2)

                def x_cols(b, i):
                    dve.wait_ge(x_T[b], (i + e0 + 1) * 2)
                    columns_of_x(b, xt_ready[b], True)

                def expert(b, i, first, last):
                    dve.wait_ge(sl_ready[b], i + e0 + 1)
                    dve.wait_ge(gate_mm[b], i + e0 + 1)
                    V.tensor_tensor(HB.rearrange("t (c p) -> t p c", p=P), SL.rearrange("t (p c) -> t p c", c=FC),
                                    bank(3).rearrange("t (p c) -> t p c", c=FC), ALU.mult).then_inc(hb_ready[b], 1)
                    if not last:
                        x_cols(1 - b, i + b)
                    if not first:
                        dve.wait_ge(y_out[b], (i + e0) * 16)
                    for half in range(2):
                        cs = slice(half * 512, (half + 1) * 512)
                        dve.wait_ge(y_mm[b], (i + e0) * 2 + half + 1)
                        V.scalar_tensor_tensor(out=YS[:, b, cs], in0=bank(5 + half),
                                               scalar=GATE_OF[:, bass.ds(i * 2 + b, 1)], in1=gates[:, 1, cs],
                                               op0=ALU.mult, op1=ALU.mult).then_inc(y_ready[b], 1)

                x_cols(0, 0)
                for b in range(2):
                    expert(b, 0, l == 0, False)
                with dve.Fori(0, NE // 2 - 2) as i:
                    for b in range(2):
                        expert(b, i + 1, False, False)
                for b in range(2):
                    expert(b, NE // 2 - 1, False, b == 1)

            def overflow(l):
                dve.wait_ge(tab_ready, l + 1)
                flag = dve.value_load(ANY[0:1, 0:1])
                with dve.If(flag > 0):
                    with dve.Fori(0, NOV) as n:
                        act_flag = dve.value_load(ACTIVE[0:1, bass.ds(n + NE, 1)])
                        with dve.If(act_flag > 0):
                            dve.wait_ge(ov_xT, n + (l * NOV + 1))
                            columns_of_x(0, ov_xt, False)
                            dve.wait_ge(ov_sl, n + (l * NOV + 1))
                            dve.wait_ge(ov_gate, n + (l * NOV + 1))
                            V.tensor_tensor(HB.rearrange("t (c p) -> t p c", p=P),
                                            SL.rearrange("t (p c) -> t p c", c=FC),
                                            bank(3).rearrange("t (p c) -> t p c", c=FC), ALU.mult).then_inc(ov_hb, 1)
                            dve.wait_ge(ov_ymm, n + (l * NOV + 1))
                            for half in range(2):
                                cs = slice(half * 512, (half + 1) * 512)
                                ins = V.scalar_tensor_tensor(
                                    out=YS[:, 0, cs], in0=bank(5 + half),
                                    scalar=GATE_OF[:, bass.ds(n + NE, 1)], in1=gates[:, 1, cs],
                                    op0=ALU.mult, op1=ALU.mult)
                            ins.then_inc(ov_y, 1)
                        with dve.Else():
                            for s in (ov_xt, ov_hb, ov_y):
                                dve.sem_inc(s, 1)
                with dve.Else():
                    dve.sem_inc(ov_xt, NOV)
                    dve.sem_inc(ov_hb, NOV)
                    dve.sem_inc(ov_y, NOV)
                dve.sem_inc(ov_left, 1)

            def router_norm(l):
                norm(2 * l + 1, H, at(24576, 2, D), lambda i, j: VTT[:, i % 2, j * P:(j + 1) * P],
                     lambda i, j: gain_x[:, 2, j:j + 1], lambda i, j: mod[:, 3, j, 0:1])

            def final():
                dve.wait_ge(sq_done, norm_base[5])
                V.tensor_scalar(rstd[:, 0:TT], ss[:, 0:TT], 1.0 / D, EPS, ALU.mult, ALU.add).then_inc(ms_ready, 1)
                dve.wait_ge(root_ready, 5)
                link(V.reciprocal(rstd[:, 0:TT], rstd[:, 0:TT]))
                dve.wait_ge(gf_in, 16)
                for i in range(TT):
                    V.scalar_tensor_tensor(out=H[:, i], in0=H[:, i], scalar=rstd[:, i:i + 1], in1=GF,
                                           op0=ALU.mult, op1=ALU.mult).then_inc(o_ready, 1)

            def combine(l):
                for i in range(TT):
                    dve.wait_ge(cy_full[i % 2], 16 * (l * TT // 2 + i // 2 + 1))
                    link(V.tensor_tensor(H[:, i], H[:, i], CY[:, i % 2, 0], ALU.add))
                    V.tensor_tensor(H[:, i], H[:, i], CY[:, i % 2, 1], ALU.add).then_inc(cy_used, 1)

            def shortconv():
                for c in range(KC):
                    cx = CX[:, c % 2]
                    dve.wait_ge(bg_ready, 2 * c + 2)
                    dve.wait_ge(od_mm, 6 * c + 6)
                    link(V.tensor_tensor(cx, CONVT[:, c % 2], ps[:, 4:6, :].rearrange("p a b -> p (a b)"), ALU.mult))
                    dst = GTM[:, c]
                    link(conv(dst, cx, lambda w: cols[:, R_OD + 8 * w + c:R_OD + 8 * w + c + 1], None))
                    V.tensor_tensor(dst, dst, BGT[:, c % 2], ALU.mult).then_inc(od_conv, 1)

            if UPTO >= 7:
                for l in range(DEPTH):
                    if l:
                        modulation(1)
                        norm(2, H, at(28672, 2, D), lambda i, j: U[:, j, i * P:(i + 1) * P],
                             lambda i, j: gain_x[:, 0, j:j + 1], lambda i, j: mod[:, 0, j, 0:1])
                        shortconv()
                        residual(1, at(28672, 4, 512))
                    router_norm(l)
                    routing(l)
                    experts(l)
                    overflow(l)
                    combine(l)
                final()


_INS = ['x', 'c', 'ctx', 'c_ctx', 'mod_w', 'mod_b', 'norm_mix', 'norm_ffn', 'norm_final', 'ev_w_in', 'ev_w_out',
        'gla_wa_f', 'gla_ba_f', 'gla_wa_b', 'gla_ba_b', 'gla_norm', 'hy_conv_w', 'hy_conv_b', 'hy_w1', 'hy_b1',
        'hy_f1', 'hy_w2', 'hy_b2', 'hy_f2', 'hy_w3', 'hy_skip', 'od_w_in', 'od_conv_w', 'od_w_out', 'rt_w_grp',
        'rt_b_grp', 'rt_w_exp', 'rt_b_exp', 'ex_w1', 'ex_w3', 'ex_w2']


def kernel(**inputs):
    import concourse.bacc as _bacc
    from concourse.bass_utils import run_bass_kernel_spmd as _run

    nc = _bacc.Bacc("TRN2", target_bir_lowering=False, num_devices=1)
    arrays, aps = {}, {}
    for name, value in [(n, inputs[n]) for n in _INS] + list(constants().items()):
        arr = np.ascontiguousarray(value)
        arrays[f"in_{name}_dram"] = arr
        aps[name] = nc.dram_tensor(f"in_{name}_dram", arr.shape, F32, kind="ExternalInput").ap()
    out = nc.dram_tensor("out_0_dram", (1, SEQ, D), F32, kind="ExternalOutput").ap()
    build(nc, aps, out)
    r = _run(nc, [arrays], core_ids=[0])
    return r.results[0]["out_0_dram"]
```

```python
from contextlib import ExitStack

import concourse.bass as bass
import numpy as np
from concourse import mybir

F32 = mybir.dt.float32
I32 = mybir.dt.int32
ALU = mybir.AluOpType
ACT = mybir.ActivationFunctionType
AX = mybir.AxisListType

P = 128
D = 1024
SEQ = 1024
CTX = 256
DEPTH = 2
EPS = 1e-6
KC = D // P
TT = SEQ // P
CT = CTX // P
TOK = SEQ + CTX
HEADS, DK, DV, RANK = 4, 64, 128, 16
TAU = 16.0
CH = 64
NCH = SEQ // CH
NCC = CTX // CH
QK, GV = HEADS * DK, HEADS * DV
HW = 512
HC = HW // P
EMB, HID = 33, 64
NG, EPG, NE, FE = 4, 8, 32, 512
FC = FE // P
HALF = 512
KT = HALF // P
ASSIGN = 2 * SEQ
NJ = SEQ // P
FAR = 8192.0
BIG = 1e30
MAGIC = 1.5 * 2.0 ** 23
TWO_PI_HI = 6.28125
TWO_PI_LO = 2 * np.pi - 6.28125
PI_F = 3.1415925

C_V = 2 * QK
C_G = C_V + GV
C_R = C_G + GV
C_HY = C_R + 2 * RANK

R_CW, R_CB, R_SKIP, R_GAIN, R_OD, R_BA, R_HY, N_ROWS = 0, 36, 48, 52, 53, 77, 81, 85
V_NMIX, V_NFFN, N_VEC = 12, 14, 16
K_ID, K_UT, K_IOTA, K_E64, K_J, K_TV, K_ONE, K_MASK, K_END = 0, 128, 256, 384, 416, 424, 432, 560, 816


def constants():
    cst = np.zeros((P, K_END), np.float32)
    p, c = np.arange(P)[:, None], np.arange(P)[None, :]
    cst[:, K_ID:K_ID + P] = p == c
    cst[:, K_UT:K_UT + P] = p < c
    cst[:, K_IOTA:K_IOTA + P] = c
    cst[:, K_E64:K_E64 + NE] = np.arange(NE) + 64
    cst[:, K_J:K_J + NJ] = np.arange(NJ)
    cst[:, K_TV:K_TV + TT] = 2 * (np.arange(TT)[None, :] * P + p)
    cst[:, K_ONE:K_ONE + P] = 1.0
    same = (p // CH) == (c // CH)
    mask = np.stack([same & (p <= c), same & (p >= c)], 1).astype(np.int32)
    cst[:, K_MASK:K_END] = mask.reshape(P, 2 * P).view(np.float32)

    t = np.linspace(0.0, 1.0, SEQ, dtype=np.float32)
    pos = np.arange(SEQ, dtype=np.float32)
    nb = (EMB - 1) // 2
    bands = np.linspace(1e-4, nb - 1, nb, dtype=np.float32)
    ang = np.float32(2.0 * np.pi / SEQ) * pos[:, None] * bands[None]
    z = np.concatenate([t[:, None], np.cos(ang), np.sin(ang)], -1).astype(np.float32)
    deltas = np.linspace(np.log(1e-2) / 1.5, np.log(1e-2) / 0.3, HW, dtype=np.float32)
    win = np.exp(-t[:, None] * np.abs(deltas)[None]).astype(np.float32)
    win = win.reshape(HALF // P, P, 2, HW).transpose(1, 2, 0, 3).reshape(P, 2 * KT * HW)

    k = np.arange(HALF)
    w = np.pi * (2 * k[None, :] + 1) * np.arange(SEQ)[:, None] / 2048.0
    cs = np.stack([np.cos(w), np.sin(w)])
    cs = cs.reshape(2, KT, P, 2, KT, P)
    fwd = cs.transpose(2, 4, 0, 3, 1, 5)
    inv = (cs / 512.0).transpose(5, 0, 3, 4, 1, 2)
    return {
        "cst": cst, "zT": np.ascontiguousarray(z.T), "win": win,
        "dft": np.ascontiguousarray(fwd.reshape(P, 8192).astype(np.float32)),
        "idft": np.ascontiguousarray(inv.reshape(P, 8192).astype(np.float32)),
    }


def build(nc, a, out):
    with ExitStack() as ctx:
        def sb(name, shape, dt=F32):
            return ctx.enter_context(nc.sbuf_tensor(name, shape, dt))

        def sem(name):
            return ctx.enter_context(nc.semaphore(name))

        arena = sb("arena", [P, 48512])
        cst = sb("constants", [P, K_END])
        small_rows = sb("small_rows", [N_ROWS, P])
        cols = sb("cols", [P, N_ROWS])
        neg_ba = sb("neg_ba", [P, HEADS])
        vec_cols = sb("vec_cols", [P, KC, N_VEC])
        mod = sb("mod", [P, DEPTH, 6, KC])
        mod_ctx = sb("mod_ctx", [P, 2, KC])
        gain_x = sb("gain_x", [P, 2 * DEPTH + 1, KC])
        gates = sb("gates", [P, 2, D])
        c_raw = sb("c_raw", [P, 2, KC])
        silu_c = sb("silu_c", [P, KC, 2])
        ss = sb("ss", [P, 16])
        rstd = sb("rstd", [P, 16])
        w_rank = sb("w_rank", [P, KC, 2 * RANK])
        w_gate_up = sb("w_gate_up", [2 * RANK, HEADS, P])
        decay = sb("decay", [P, NCH + NCC])
        w_hy1 = sb("w_hy1", [EMB, HID])
        w_hy2 = sb("w_hy2", [HID, HID])
        row_number = sb("row_number", [P, 2, TT])
        w_router = sb("w_router", [P, KC, NG + NE])
        b_router = sb("b_router", [1, NG + NE])

        def at(off, *dims):
            n = int(np.prod(dims))
            v = arena[:, off:off + n]
            if len(dims) == 2:
                return v.rearrange("p (a b) -> p a b", a=dims[0])
            if len(dims) == 3:
                return v.rearrange("p (a b c) -> p a b c", a=dims[0], b=dims[1])
            if len(dims) == 4:
                return v.rearrange("p (a b c d) -> p a b c d", a=dims[0], b=dims[1], c=dims[2])
            return v

        ps = ctx.enter_context(nc.psum_tensor("ps", [P, 8, 512], F32))

        def bank(b):
            return ps[:, b, :]

        ident = cst[:, K_ID:K_ID + P]

        SLAB = 4096
        NCY = 4
        RING = 3
        U = at(12288, KC, SEQ)
        UC = at(20480, KC, CTX)
        MIX = at(22528, KC, SEQ)
        HEAD_V = at(26624, TT + CT, GV)
        Q, K, KD = at(31744, SEQ), at(32768, TOK), at(34048, SEQ)
        BB, T1 = at(35072, TOK), at(36352, TOK)
        KRT = at(37632, TT + CT, P)
        ST = at(38912, NCH, DV)
        SG = at(40960, SEQ)
        AT = at(41984, 2, 2, P)
        OT = at(42496, TT, DV)
        QP, KP = at(43520, SEQ), at(44544, TOK)
        RT = at(45824, TOK)[0:2 * RANK]
        SCAN1 = at(47104, TOK)
        SCTX = at(48384, DV)
        MROW = at(28672, 2, D)
        VEC = at(30720, D)[0:N_VEC]
        M_SLABS = [at(n, KC, 512) for n in (22528, 31744, 35840)]
        ACC = at(39936, 2, D)
        X0 = at(31744, TT + CT, D)
        VX = at(30720, HC, SEQ)
        VTM = at(34816, 2, KT, HW)
        X1C, VC_ = at(20480, SEQ), at(21504, SEQ)
        DFT = at(38912, KT, 2, 2, 4 * P)
        YF = at(38912, KT, 4, HW)
        IDFT = at(12288, 2, 2, KT * HALF)
        HSUM, HDIF = at(4096, 2 * KT, HW), at(8192, 2 * KT, HW)
        UK = at(0, 8, HW)
        ZT, W3H = at(12288, SEQ), at(13312, SEQ)
        ARG, TURNS, HH1, HH2 = at(14336, SEQ), at(15360, SEQ), at(16384, SEQ), at(12288, SEQ)
        WIN = at(17408, 2 * KT, HW)
        FTMP = at(21504, 2, HW)
        CTMP = at(20480, 4, HW)
        H = at(38912, TT, D)
        GTM = at(20480, KC, SEQ)
        BGT, CONVT = at(28672, 2, SEQ), at(30720, 2, SEQ)
        CX = at(32768, 2, SEQ)
        XG = at(24576, 2, D)
        XT = at(26624, 2, KC * P)
        YS = at(28672, 2, D)
        VTT = at(27648, 2, KC * P)
        HT, SL = at(31232, FE), at(31744, FE)
        LG = at(32256, TT, NG + NE)
        ONE_HOT = [at(32544 + 256 * k, TT, NE) for k in range(2)]
        SUMOH = at(33056, TT * NE)
        POSM = at(33312, TT, NE)
        MSK = at(33568, TT, NE)
        LEX = at(33824, TT, NE)
        GRP = at(34080, 4, TT, NG)
        SC = at(34208, 16, TT)
        HOTS_OF = at(32544, 2 * TT * NE)
        POS2 = at(33568, 2 * TT * NE)
        HOT = at(34336, 2, P)
        RHS = at(34592, 2, 2, NJ * NE)
        HOT0, RHS0 = at(28672, 2 * TT, P), at(34592, 2 * TT, 2, NE)
        JEQ0, FIRST = at(37312, 2 * TT), at(37328, 2, 2 * TT)
        OV = at(35616, 2, 2, NE)
        JEQ = at(35744, 2, NJ)
        GATE_OF = at(35760, NJ * NE)
        SLOT_F = at(36016, NJ * NE)
        SLOT_ROW = at(36272, NJ * NE).bitcast(I32)
        SLOT_TOK = at(36528, NJ * NE).bitcast(I32)
        ACTIVE_F = at(36784, NJ, NE)
        ACTIVE = at(37040, NJ * NE).bitcast(I32)
        ANY_F, ANY = at(37296, 4), at(37300, 4).bitcast(I32)
        IDX_G = at(37304, 4).bitcast(I32)
        IDX_S = at(37308, 4).bitcast(I32)
        CY = at(24576, NCY, 2, D)
        GF = at(34816, D)

        rows_hn = nc.dram_tensor("normed_rows", (SEQ, D), F32, kind="Internal").ap()
        rows_y = nc.dram_tensor("expert_rows", (ASSIGN, D), F32, kind="Internal").ap()

        s_cst = sem("s_cst")
        s_rows = sem("s_rows")
        s_cin = sem("s_cin")
        s_x = sem("s_x")
        slab_full = [sem(f"slab_full{n}") for n in range(RING)]
        silu_ready = sem("silu_ready")
        rows_T = sem("rows_T")
        cols_ready = sem("cols_ready")
        vec_T = sem("vec_T")
        mod_mm = sem("mod_mm")
        mod_row = sem("mod_row")
        mod_T = sem("mod_T")
        mod_bc = sem("mod_bc")
        m_full = [sem(f"m_full{n}") for n in range(3)]
        m_used = sem("m_used")
        m_cols = sem("m_cols")
        m_ready = sem("m_ready")
        mod_gate = sem("mod_gate")
        mod_ready = sem("mod_ready")
        act_step = sem("act_step")
        dve_step = sem("dve_step")
        pool_step = sem("pool_step")
        sq_done = sem("sq_done")
        ms_ready = sem("ms_ready")
        root_ready = sem("root_ready")
        xn_ready = sem("xn_ready")
        xn_T = sem("xn_T")
        u_ready = sem("u_ready")
        u_act = sem("u_act")
        hn_out = [sem(f"hn_out{b}") for b in range(2)]
        v_mm = sem("v_mm")
        v_ready = sem("v_ready")
        r_mm = sem("r_mm")
        r_ready = sem("r_ready")
        gla_zero = sem("gla_zero")
        qk_mm = sem("qk_mm")
        qk_ready = sem("qk_ready")
        dup_act = sem("dup_act")
        dup_pool = sem("dup_pool")
        gx_mm = sem("gx_mm")
        gx_read = sem("gx_read")
        ln_ready = sem("ln_ready")
        cum_ready = sem("cum_ready")
        er_ready = sem("er_ready")
        eb_ready = sem("eb_ready")
        kr_ready = sem("kr_ready")
        qd_ready = sem("qd_ready")
        g_mm = sem("g_mm")
        sg_ready = sem("sg_ready")
        kr_T = sem("kr_T")
        krt_ready = sem("krt_ready")
        ds_mm = sem("ds_mm")
        state_ready = sem("state_ready")
        a_mm = sem("a_mm")
        at_ready = sem("at_ready")
        o_mm = sem("o_mm")
        o_copied = sem("o_copied")
        oss_ready = sem("oss_ready")
        oroot_ready = sem("oroot_ready")
        on_ready = sem("on_ready")
        o_T = sem("o_T")
        omix_ready = sem("omix_ready")
        tables_in = sem("tables_in")
        flt_in = sem("flt_in")
        hy_mm = sem("hy_mm")
        conv_done = sem("conv_done")
        vx_ready = sem("vx_ready")
        vx_T = sem("vx_T")
        vtm_ready = sem("vtm_ready")
        f_mm = sem("f_mm")
        f_arg = sem("f_arg")
        f_sin = sem("f_sin")
        h3_mm = sem("h3_mm")
        h3_copied = sem("h3_copied")
        filt_ready = sem("filt_ready")
        dft_mm = sem("dft_mm")
        uk_ready = sem("uk_ready")
        yf_dve = sem("yf_dve")
        yf_pool = sem("yf_pool")
        idft_mm = sem("idft_mm")
        hmix_ready = sem("hmix_ready")
        out_mm = sem("out_mm")
        h_ready = sem("h_ready")
        od_mm = sem("od_mm")
        bg_ready = sem("bg_ready")
        od_conv = sem("od_conv")
        small_in = sem("small_in")
        lg_mm = sem("lg_mm")
        lg_ready = sem("lg_ready")
        gexp_in = sem("gexp_in")
        gexp_out = sem("gexp_out")
        oh_ready = sem("oh_ready")
        pos_mm = sem("pos_mm")
        hot_ready = sem("hot_ready")
        tab_mm = sem("tab_mm")
        tab_ready = sem("tab_ready")
        w_full = [[sem(f"w_full{b}_{m}") for m in range(3)] for b in range(2)]
        x_full = [sem(f"x_full{b}") for b in range(2)]
        idx_ready = sem("idx_ready")
        x_T = [sem(f"x_T{b}") for b in range(2)]
        xt_ready = [sem(f"xt_ready{b}") for b in range(2)]
        up_mm = [sem(f"up_mm{b}") for b in range(2)]
        gate_mm = [sem(f"gate_mm{b}") for b in range(2)]
        sl_ready = [sem(f"sl_ready{b}") for b in range(2)]
        ht_ready = [sem(f"ht_ready{b}") for b in range(2)]
        y_mm = [sem(f"y_mm{b}") for b in range(2)]
        y_ready = [sem(f"y_ready{b}") for b in range(2)]
        y_out = [sem(f"y_out{b}") for b in range(2)]
        ov_w = [sem(f"ov_w{m}") for m in range(3)]
        ov_hot = sem("ov_hot")
        ov_tmm = sem("ov_tmm")
        ov_tab = sem("ov_tab")
        ov_idx = sem("ov_idx")
        ov_x = [sem(f"ov_x{n}") for n in range(DEPTH)]
        ov_xT = sem("ov_xT")
        ov_xt = sem("ov_xt")
        ov_up = sem("ov_up")
        ov_gate = sem("ov_gate")
        ov_sl = sem("ov_sl")
        ov_ht = sem("ov_ht")
        ov_ymm = sem("ov_ymm")
        ov_y = sem("ov_y")
        ov_out = [sem(f"ov_out{n}") for n in range(DEPTH)]
        ov_left = sem("ov_left")
        waited = sem("waited")
        cy_full = [sem(f"cy_full{b}") for b in range(NCY)]
        cy_used = sem("cy_used")
        o_ready = sem("o_ready")
        s_out = [sem(f"s_out{b}") for b in range(2)]

        NOV = (NJ - 1) * NE
        NMOD, L0_MOD = 4, 2
        L0_V, L0_G, L0_QK, L0_HY = [L0_MOD + NMOD + n for n in range(4)]
        L0_OUT = L0_HY + HC
        L1_IN = L0_OUT + 2
        L1_OUT = L1_IN + KC
        SECTIONS = [(0, s) for s in range(2, 6)] + [(1, s) for s in range(6)]
        NSEC = len(SECTIONS)
        SMALL0 = 16 * 5
        NORMS = [TT + CT, TT, TT, TT, TT]
        norm_base = [sum(NORMS[:n]) for n in range(len(NORMS) + 1)]

        def last_use(n):
            if n < L0_V:
                return mod_mm, n - L0_MOD + 1
            if n == L0_V:
                return v_mm, TT + CT
            if n == L0_G:
                return g_mm, 2 * HEADS
            if n == L0_QK:
                return qk_mm, 5 * (HEADS // 2)
            if n < L0_OUT:
                return hy_mm, 6 * (n - L0_HY + 1)
            if n < L1_IN:
                return out_mm, 2 * TT
            if n < L1_OUT:
                return od_mm, 6 * (n - L1_IN + 1)
            return out_mm, 4 * TT

        def ds_place(c):
            b = (0, 1, 2)[c // 8] if c % 2 == 0 else (3, 4, 7)[c // 8]
            return bank(b)[:, (c // 2 % 4) * P:(c // 2 % 4 + 1) * P]

        def slab(n, *dims):
            return at((n % RING) * SLAB, *dims)

        def w_slot(b, m, *dims):
            return at((3 * b + m) * SLAB, *dims)

        block = ctx.enter_context(nc.Block())

        @block.sync
        def _(sp):
            def load(n, dst, src):
                if n >= RING + L0_MOD:
                    sp.wait_ge(*last_use(n - RING))
                sp.dma_start(dst, src).then_inc(slab_full[n % RING], 16)

            def mod_slab(l, n):
                return a["mod_w"][l, :, n * 512:(n + 1) * 512].rearrange("(p j) n -> p j n", j=KC)

            def late_modulation(slabs):
                for m in slabs:
                    l, sec = SECTIONS[m // 2]
                    if m >= 3:
                        sp.wait_ge(m_used, m - 2)
                    elif m:
                        sp.wait_ge(xn_ready, 4 * m)
                    sp.dma_start(M_SLABS[m % 3], mod_slab(l, 2 * sec + m % 2)).then_inc(m_full[m % 3], 16)

            def rows_in():
                sp.dma_start(cst[:], a["cst"]).then_inc(s_cst, 16)
                sp.dma_start(c_raw[:, 0], a["c"].rearrange("o (p j) -> p (o j)", j=KC)).then_inc(s_cin, 16)
                sp.dma_start(c_raw[:, 1], a["c_ctx"].rearrange("(p j) -> p j", j=KC)).then_inc(s_cin, 16)

            def moe_weights(l):
                srcs = [a["ex_w1"], a["ex_w3"], a["ex_w2"]]

                def pair(i, first):
                    for b in range(2):
                        for m in range(3):
                            if not first:
                                used = (up_mm, gate_mm, y_mm)[m][b]
                                sp.wait_ge(used, (i + l * (NE // 2)) * (2 if m == 2 else 1))
                            sp.dma_start(
                                w_slot(b, m, SLAB),
                                srcs[m][l, i * 2 + b].rearrange("(p j) n -> p (j n)", p=P),
                            ).then_inc(w_full[b][m], 16)

                pair(0, l == 0)
                with sp.Fori(0, NE // 2 - 1) as i:
                    pair(i + 1, False)

            def moe_overflow(l):
                flag = sp.value_load(ANY[0:1, 0:1])
                with sp.If(flag > 0):
                    with sp.Fori(0, NJ - 1) as t:
                        with sp.Fori(0, NE) as e:
                            n = t * NE + e
                            act_flag = sp.value_load(ACTIVE[0:1, bass.ds(n + NE, 1)])
                            with sp.If(act_flag > 0):
                                sp.wait_ge(ov_x[l], (n + 1) * 16)
                                for m, src in enumerate([a["ex_w1"], a["ex_w3"], a["ex_w2"]]):
                                    sp.dma_start(
                                        w_slot(0, m, SLAB), src[l, e].rearrange("(p j) n -> p (j n)", p=P),
                                    ).then_inc(ov_w[m], 16)
                                for m in range(3):
                                    sp.wait_ge(ov_w[m], (n + (l * NOV + 1)) * 16)
                                sp.sem_inc(waited, 1)
                            with sp.Else():
                                for m in range(3):
                                    sp.sem_inc(ov_w[m], 16)
                with sp.Else():
                    for m in range(3):
                        sp.sem_inc(ov_w[m], 16 * NOV)
                sp.sem_inc(ov_left, 1)

            def combine(l):
                for b in range(2):
                    sp.wait_ge(y_out[b], 16 * (NE // 2) * (l + 1))
                sp.wait_ge(ov_left, 5 * (l + 1))
                for i in range(TT):
                    if i >= NCY:
                        sp.wait_ge(cy_used, l * TT + i - NCY + 1)
                    sp.dma_start(
                        CY[:, i % NCY], rows_y[i * 2 * P:(i + 1) * 2 * P].rearrange("(t k) d -> t k d", k=2)
                    ).then_inc(cy_full[i % NCY], 16)

            rows_in()
            for n in range(NMOD):
                load(L0_MOD + n, slab(L0_MOD + n, KC, 512), mod_slab(0, n))
            load(L0_V, slab(L0_V, KC, GV), a["ev_w_in"][0, :, C_V:C_G].rearrange("(p j) n -> p j n", j=KC))
            load(L0_G, slab(L0_G, KC, GV), a["ev_w_in"][0, :, C_G:C_R].rearrange("(p j) n -> p j n", j=KC))
            load(L0_QK, slab(L0_QK, KC, 2 * QK), a["ev_w_in"][0, :, 0:C_V].rearrange("(p j) n -> p j n", j=KC))
            late_modulation(range(2 * NSEC))
            for c in range(HC):
                n = L0_HY + c
                sp.wait_ge(*last_use(n - RING))
                for k in range(3):
                    sp.dma_start(
                        slab(n, 3, KC, P)[:, k],
                        a["ev_w_in"][0, :, C_HY + k * HW + c * P:C_HY + k * HW + (c + 1) * P].rearrange(
                            "(p j) n -> p j n", j=KC),
                    ).then_inc(slab_full[n % RING], 16)
            sp.wait_ge(omix_ready, 2 * HEADS)
            sp.dma_start(at(38912, 8192), a["dft"]).then_inc(tables_in, 16)
            sp.wait_ge(hy_mm, 6 * HC)
            sp.dma_start(w_hy1[:], a["hy_w1"][0]).then_inc(flt_in, 16)
            sp.dma_start(w_hy2[:], a["hy_w2"][0]).then_inc(flt_in, 16)
            sp.dma_start(ZT[0:EMB], a["zT"]).then_inc(flt_in, 16)
            sp.dma_start(W3H[0:HID], a["hy_w3"][0]).then_inc(flt_in, 16)
            sp.wait_ge(vtm_ready, 2 * HC)
            sp.wait_ge(tables_in, 16)
            sp.dma_start(at(17408, 4096), a["win"]).then_inc(tables_in, 16)
            sp.wait_ge(filt_ready, 2 * KT)
            sp.dma_start(at(12288, 8192), a["idft"]).then_inc(tables_in, 16)
            sp.wait_ge(dft_mm, 8 * KT)
            sp.wait_ge(uk_ready, 8 * KT)
            for n in range(2):
                load(L0_OUT + n, slab(L0_OUT + n, KC, 512),
                     a["ev_w_out"][0, :, n * 512:(n + 1) * 512].rearrange("(j p) n -> p j n", p=P))
            sp.wait_ge(idft_mm, 2 * HC)
            sp.dma_start(H, a["x"][0].rearrange("(i p) d -> p i d", p=P)).then_inc(tables_in, 16)
            for l in range(DEPTH):
                if l:
                    for c in range(KC):
                        n = L1_IN + c
                        sp.wait_ge(*last_use(n - RING))
                        for k in range(3):
                            sp.dma_start(
                                slab(n, 3, KC, P)[:, k],
                                a["od_w_in"][0, :, k * D + c * P:k * D + (c + 1) * P].rearrange(
                                    "(p j) n -> p j n", j=KC),
                            ).then_inc(slab_full[n % RING], 16)
                    for n in range(2):
                        load(L1_OUT + n, slab(L1_OUT + n, KC, 512),
                             a["od_w_out"][0, :, n * 512:(n + 1) * 512].rearrange("(j p) n -> p j n", p=P))
                sp.wait_ge(h_ready, 2 * TT * (l + 1))
                sp.wait_ge(xn_ready, norm_base[2 * l + 2])
                moe_weights(l)
                sp.wait_ge(y_mm[0], (l + 1) * NE)
                sp.wait_ge(tab_ready, l + 1)
                moe_overflow(l)
                combine(l)
            sp.wait_ge(cy_used, 2 * TT)
            for i in range(TT):
                sp.wait_ge(o_ready, i + 1)
                sp.dma_start(out[0, i * P:(i + 1) * P, :], H[:, i, :]).then_inc(s_out[i % 2], 16)
            for b in range(2):
                sp.wait_ge(s_out[b], 16 * TT // 2)

        @block.gpsimd
        def _(pool):
            def step(ins, n):
                ins.then_inc(pool_step, 1)
                pool.wait_ge(pool_step, n)

            nc.gpsimd.memset(small_rows[:], 0.0).then_inc(pool_step, 1)
            nc.gpsimd.memset(w_gate_up[:], 0.0).then_inc(pool_step, 1)
            pool.wait_ge(pool_step, 2)

            def row(dst, src):
                pool.dma_start(dst, src).then_inc(s_rows, 16)

            row(small_rows[R_CW:R_CB], a["hy_conv_w"][0].rearrange("w (c p) -> (w c) p", p=P))
            row(small_rows[R_CB:R_SKIP], a["hy_conv_b"][0].rearrange("(c p) -> c p", p=P))
            row(small_rows[R_SKIP:R_GAIN], a["hy_skip"][0].rearrange("(c p) -> c p", p=P))
            row(small_rows[R_GAIN:R_OD], a["gla_norm"])
            row(small_rows[R_OD:R_BA], a["od_conv_w"][0].rearrange("w (c p) -> (w c) p", p=P))
            row(small_rows[R_BA:R_HY, 0:DK], a["gla_ba_f"][0].rearrange("(h d) -> h d", d=DK))
            row(small_rows[R_BA:R_HY, DK:P], a["gla_ba_b"][0].rearrange("(h d) -> h d", d=DK))
            for n, name in enumerate(["hy_b1", "hy_f1", "hy_b2", "hy_f2"]):
                row(small_rows[R_HY + n:R_HY + n + 1, 0:HID], a[name])
            row(w_gate_up[0:RANK, :, 0:DK], a["gla_wa_f"][0].rearrange("r (h d) -> r h d", d=DK))
            row(w_gate_up[RANK:2 * RANK, :, DK:P], a["gla_wa_b"][0].rearrange("r (h d) -> r h d", d=DK))

            pool.dma_start(VEC[0:V_NMIX], a["mod_b"].rearrange("l (s d) -> (l s) d", d=D)).then_inc(s_rows, 16)
            pool.dma_start(VEC[V_NMIX:V_NFFN], a["norm_mix"]).then_inc(s_rows, 16)
            pool.dma_start(VEC[V_NFFN:N_VEC], a["norm_ffn"]).then_inc(s_rows, 16)
            pool.dma_start(X0[:, 0:TT], a["x"][0].rearrange("(i p) d -> p i d", p=P)).then_inc(s_x, 16)
            pool.dma_start(X0[:, TT:], a["ctx"][0].rearrange("(i p) d -> p i d", p=P)).then_inc(s_x, 16)
            pool.dma_start(w_rank[:], a["ev_w_in"][0, :, C_R:C_HY].rearrange("(p j) n -> p j n", j=KC))\
                .then_inc(small_in, 16)

            def router_in(l):
                if l:
                    pool.wait_ge(lg_mm, TT * l)
                pool.dma_start(w_router[:, :, 0:NG], a["rt_w_grp"][l].rearrange("(p j) g -> p j g", j=KC))\
                    .then_inc(small_in, 16)
                pool.dma_start(w_router[:, :, NG:], a["rt_w_exp"][l].rearrange("(p j) g -> p j g", j=KC))\
                    .then_inc(small_in, 16)
                pool.dma_start(b_router[0:1, 0:NG], a["rt_b_grp"][l:l + 1]).then_inc(small_in, 16)
                pool.dma_start(b_router[0:1, NG:], a["rt_b_exp"][l:l + 1]).then_inc(small_in, 16)

            router_in(0)

            for h in range(HEADS):
                pool.wait_ge(qk_ready, 5 * (h // 2 + 1))
                if h:
                    pool.wait_ge(o_mm, TT * h)
                    pool.wait_ge(kr_ready, 3 * h)
                else:
                    pool.wait_ge(m_used, 2 * NSEC)
                hb = (h % 2) * DK
                nc.gpsimd.tensor_copy(K[0:DK], KP[hb:hb + DK]).then_inc(dup_pool, 1)
                nc.gpsimd.tensor_copy(K[DK:P], KP[hb:hb + DK]).then_inc(dup_pool, 1)

            base = 2
            for kt in range(KT):
                pool.wait_ge(uk_ready, 8 * (kt + 1))
                ua, ub, uc, ud, ka, kb, kc, kd = [UK[:, q] for q in range(8)]
                t0, t1 = CTMP[:, 2], CTMP[:, 3]
                for row_, terms, signs in ((1, ((ua, kb), (ub, ka), (uc, kd), (ud, kc)), (1, -1, -1)),
                                           (3, ((ua, kd), (ub, kc), (uc, kb), (ud, ka)), (1, 1, 1))):
                    base += 1
                    step(nc.gpsimd.tensor_tensor(t0, terms[0][0], terms[0][1], ALU.mult), base)
                    for q in range(3):
                        x, y = terms[q + 1]
                        base += 1
                        step(nc.gpsimd.tensor_tensor(t1, x, y, ALU.mult), base)
                        dst = YF[:, kt, row_] if q == 2 else t0
                        if q == 2:
                            nc.gpsimd.tensor_tensor(
                                dst, t0, t1, ALU.add if signs[q] > 0 else ALU.subtract).then_inc(yf_pool, 1)
                            pool.wait_ge(yf_pool, 2 * kt + row_ // 2 + 1)
                        else:
                            base += 1
                            step(nc.gpsimd.tensor_tensor(
                                dst, t0, t1, ALU.add if signs[q] > 0 else ALU.subtract), base)

            def gather(l, b, col, wait):
                nc.gpsimd.tensor_copy(IDX_G[:, b:b + 1], SLOT_TOK[:, col]).then_inc(idx_ready, 1)
                pool.wait_ge(idx_ready, wait)
                pool.sem_inc(waited, 1)
                pool.indirect_dma_start(
                    XG[:, b], None, rows_hn, bass.IndirectOffsetOnAxis(ap=IDX_G[:, b:b + 1], axis=0),
                    bounds_check=SEQ - 1, oob_is_err=False).then_inc(x_full[b], 16)

            def scatter(l, b, col, wait):
                nc.gpsimd.tensor_copy(IDX_S[:, b:b + 1], SLOT_ROW[:, col]).then_inc(idx_ready, 1)
                pool.wait_ge(idx_ready, wait)
                pool.sem_inc(waited, 1)
                pool.indirect_dma_start(
                    rows_y, bass.IndirectOffsetOnAxis(ap=IDX_S[:, b:b + 1], axis=0), YS[:, b], None,
                    bounds_check=ASSIGN - 1, oob_is_err=False).then_inc(y_out[b], 16)

            def experts(l):
                e0 = l * (NE // 2)
                c0 = l * 2 * NE
                for i in range(TT):
                    pool.wait_ge(xn_ready, norm_base[2 * l + 1] + i + 1)
                    pool.dma_start(rows_hn[i * P:(i + 1) * P], at(24576, 2, D)[:, i % 2]).then_inc(hn_out[i % 2], 16)
                for b in range(2):
                    pool.wait_ge(hn_out[b], 16 * (TT // 2) * (l + 1))
                pool.wait_ge(tab_ready, l + 1)
                for b in range(2):
                    gather(l, b, bass.ds(b, 1), c0 + b + 1)

                def pair(i, first):
                    for b in range(2):
                        pool.wait_ge(y_ready[b], (i + e0 + 1) * 2)
                        if not first:
                            pool.wait_ge(y_out[b], (i + e0) * 16)
                        scatter(l, b, bass.ds(i * 2 + b, 1), i * 4 + (c0 + 2 * b + 3))
                        pool.wait_ge(x_T[b], (i + e0 + 1) * 2)
                        pool.wait_ge(x_full[b], (i + e0 + 1) * 16)
                        gather(l, b, bass.ds(i * 2 + b + 2, 1), i * 4 + (c0 + 2 * b + 4))

                pair(0, l == 0)
                with pool.Fori(0, NE // 2 - 2) as i:
                    pair(i + 1, False)
                last = NE // 2 - 1
                for b in range(2):
                    pool.wait_ge(y_ready[b], (last + e0 + 1) * 2)
                    pool.wait_ge(y_out[b], (last + e0) * 16)
                    scatter(l, b, bass.ds(2 * last + b, 1), c0 + 4 * last + b + 3)
                for b in range(2):
                    pool.wait_ge(y_out[b], (last + e0 + 1) * 16)

            def overflow(l):
                flag = pool.value_load(ANY[0:1, 0:1])
                with pool.If(flag > 0):
                    pool.wait_ge(ov_tab, l + 1)
                    with pool.Fori(0, NOV) as n:
                        nc.gpsimd.tensor_copy(IDX_G[:, 2:3], SLOT_TOK[:, bass.ds(n + NE, 1)]).then_inc(ov_idx, 1)
                        nc.gpsimd.tensor_copy(IDX_S[:, 2:3], SLOT_ROW[:, bass.ds(n + NE, 1)]).then_inc(ov_idx, 1)
                        pool.wait_ge(ov_idx, (n + (l * NOV + 1)) * 2)
                        pool.sem_inc(waited, 1)
                        pool.indirect_dma_start(
                            XG[:, 0], None, rows_hn,
                            bass.IndirectOffsetOnAxis(ap=IDX_G[:, 2:3], axis=0),
                            bounds_check=SEQ - 1, oob_is_err=False).then_inc(ov_x[l], 16)
                        pool.wait_ge(ov_y, n + (l * NOV + 1))
                        pool.sem_inc(waited, 1)
                        pool.indirect_dma_start(
                            rows_y, bass.IndirectOffsetOnAxis(ap=IDX_S[:, 2:3], axis=0), YS[:, 0], None,
                            bounds_check=ASSIGN - 1, oob_is_err=False).then_inc(ov_out[l], 16)
                        pool.wait_ge(ov_x[l], (n + 1) * 16)
                        pool.wait_ge(ov_out[l], (n + 1) * 16)
                with pool.Else():
                    pool.sem_inc(ov_idx, 2 * NOV)
                pool.sem_inc(ov_left, 1)

            for l in range(DEPTH):
                experts(l)
                overflow(l)
                if l + 1 < DEPTH:
                    router_in(l + 1)
            pool.wait_ge(ov_left, 5 * DEPTH)
            pool.dma_start(GF, a["norm_final"].partition_broadcast(P)).then_inc(small_in, 16)

        @block.scalar
        def _(act):
            count = [0]

            def step(ins):
                count[0] += 1
                ins.then_inc(act_step, 1)

            def settle():
                act.wait_ge(act_step, count[0])

            def norm(n, src, junk):
                for i in range(NORMS[n]):
                    if n in (1, 3):
                        act.wait_ge(h_ready, 2 * TT * (n // 2) + 2 * (i + 1))
                    if n in (2, 4):
                        act.wait_ge(cy_used, TT * (n // 2 - 1) + i + 1)
                    if i >= 2:
                        act.wait_ge(sq_done, norm_base[n] + i - 1)
                    nc.scalar.activation(junk[:, i % 2], src[:, i], ACT.Square, accum_out=ss[:, i:i + 1]).then_inc(sq_done, 1)
                act.wait_ge(ms_ready, n + 1)
                nc.scalar.activation(rstd[:, 0:NORMS[n]], rstd[:, 0:NORMS[n]], ACT.Sqrt).then_inc(root_ready, 1)

            def columns(n, target):
                l = n // 2
                for i in range(NORMS[n]):
                    act.wait_ge(xn_T, norm_base[n] + i + 1)
                    if n % 2 and i >= 2:
                        act.wait_ge(lg_mm, l * TT + i - 1)
                    if n % 2:
                        g, b = gain_x[:, n], mod[:, l, 3]
                    elif i < TT:
                        g, b = gain_x[:, n], mod[:, l, 0]
                    else:
                        g, b = gain_x[:, 2 * DEPTH], mod_ctx[:, 0]
                    for j in range(KC // 2, KC):
                        ins = nc.scalar.activation(
                            target(i, j), bank(4 * (i % 2) + 1)[:, (j - 4) * P:(j - 3) * P], ACT.Identity,
                            scale=g[:, j:j + 1], bias=b[:, j:j + 1])
                    ins.then_inc(u_act, 1)

            act.wait_ge(s_cin, 32)
            nc.scalar.activation(silu_c[:].rearrange("p j r -> p r j"), c_raw[:], ACT.Silu).then_inc(silu_ready, 1)
            act.wait_ge(s_x, 32)
            norm(0, X0, at(12288, 2, D))
            columns(0, lambda i, j: U[:, j, i * P:(i + 1) * P] if i < TT else UC[:, j, (i - TT) * P:(i - TT + 1) * P])

            def gla_head(h):
                if h % 2 == 0:
                    if h:
                        act.wait_ge(dup_act, 2 * h)
                        act.wait_ge(dup_pool, 2 * h)
                    for q in range(5):
                        act.wait_ge(qk_mm, 5 * (h // 2) + q + 1)
                        if q < 2:
                            ins = nc.scalar.activation(QP[:, q * 512:(q + 1) * 512], bank(q), ACT.Copy, scale=DK ** -0.5)
                        else:
                            n = 512 if q < 4 else CTX
                            ins = nc.scalar.activation(KP[:, (q - 2) * 512:(q - 2) * 512 + n], bank(q)[:, 0:n], ACT.Copy)
                        ins.then_inc(qk_ready, 1)
                act.wait_ge(qk_ready, 5 * (h // 2 + 1))
                if h:
                    act.wait_ge(o_mm, TT * h)
                else:
                    act.wait_ge(m_used, 2 * NSEC)
                hb = (h % 2) * DK
                nc.scalar.activation(Q[0:DK], QP[hb:hb + DK], ACT.Copy).then_inc(dup_act, 1)
                nc.scalar.activation(Q[DK:P], QP[hb:hb + DK], ACT.Copy).then_inc(dup_act, 1)
                act.wait_ge(gx_read, 6 * (h + 1))
                step(nc.scalar.activation(BB, BB, ACT.Exp, bias=neg_ba[:, h:h + 1]))
                settle()
                nc.scalar.activation(BB, BB, ACT.Ln, bias=1.0).then_inc(ln_ready, 1)
                act.wait_ge(cum_ready, 2 * (h + 1))
                nc.scalar.activation(T1, T1, ACT.Exp, scale=1.0 / TAU).then_inc(er_ready, 1)
                bv = BB.rearrange("p (c t) -> p c t", t=CH)
                nc.scalar.activation(decay[0:DK], bv[0:DK, :, CH - 1], ACT.Exp, scale=1.0 / TAU).then_inc(er_ready, 1)
                nc.scalar.activation(decay[DK:P], bv[DK:P, :, 0], ACT.Exp, scale=1.0 / TAU).then_inc(er_ready, 1)
                nc.scalar.activation(KD, BB[:, 0:SEQ], ACT.Exp, scale=-1.0 / TAU).then_inc(eb_ready, 1)
                act.wait_ge(er_ready, 3 * (h + 1))
                act.wait_ge(eb_ready, 2 * h + 1)
                nc.scalar.activation(BB[:, 0:SEQ], BB[:, 0:SEQ], ACT.Exp, scale=1.0 / TAU).then_inc(eb_ready, 1)
                for half in range(2):
                    act.wait_ge(g_mm, 2 * h + half + 1)
                    if h:
                        act.wait_ge(omix_ready, 2 * h)
                    nc.scalar.activation(SG[:, half * 512:(half + 1) * 512], bank(half), ACT.Silu).then_inc(sg_ready, 1)
                for q in range(3):
                    act.wait_ge(kr_T, 3 * h + q + 1)
                    n = 4 if q < 2 else 2
                    nc.scalar.activation(KRT[:, 4 * q:4 * q + n],
                                         bank(5 + q)[:, 0:n * P].rearrange("p (a b) -> p a b", b=P),
                                         ACT.Copy).then_inc(krt_ready, 1)
                for i in range(TT):
                    act.wait_ge(o_mm, TT * h + i + 1)
                    nc.scalar.activation(OT[:, i], bank((7, 0)[i % 2])[:, 0:P], ACT.Copy).then_inc(o_copied, 1)
                act.wait_ge(oss_ready, h + 1)
                nc.scalar.activation(rstd[:, 0:TT], rstd[:, 0:TT], ACT.Sqrt).then_inc(oroot_ready, 1)

            for i in range(TT + CT):
                act.wait_ge(v_mm, i + 1)
                nc.scalar.activation(HEAD_V[:, i], bank(i % 4), ACT.Copy).then_inc(v_ready, 1)
            for q in range(3):
                act.wait_ge(r_mm, q + 1)
                n = 512 if q < 2 else CTX
                nc.scalar.activation(RT[:, q * 512:q * 512 + n], bank(4 + q)[0:2 * RANK, 0:n], ACT.Copy)\
                    .then_inc(r_ready, 1)
            for h in range(HEADS):
                gla_head(h)

            for c in range(HC):
                for par in range(2):
                    act.wait_ge(vx_T, 2 * c + par + 1)
                    nc.scalar.activation(
                        VTM[:, par, :, c * P:(c + 1) * P], bank(6 + par).rearrange("p (a b) -> p a b", b=P),
                        ACT.Copy).then_inc(vtm_ready, 1)
            for n, dst in ((0, HH1), (1, HH2)):
                act.wait_ge(f_arg, n + 1)
                nc.scalar.activation(dst[0:HID], ARG[0:HID], ACT.Sin).then_inc(f_sin, 1)
            for t in range(2 * KT):
                act.wait_ge(h3_mm, 2 * t + 2)
                if t:
                    act.wait_ge(filt_ready, t)
                nc.scalar.activation(FTMP[:, 0], bank(2 * (t % 2) + 1), ACT.Copy).then_inc(h3_copied, 1)
            for kt in range(KT):
                if kt:
                    act.wait_ge(yf_dve, 2 * kt)
                    act.wait_ge(yf_pool, 2 * kt)
                for q in range(8):
                    act.wait_ge(dft_mm, 8 * kt + q + 1)
                    nc.scalar.activation(UK[:, q], bank((q + 4) % 8), ACT.Copy).then_inc(uk_ready, 1)

            def od_gates():
                for c in range(KC):
                    act.wait_ge(od_mm, 6 * c + 2)
                    if c >= 2:
                        act.wait_ge(od_conv, c - 1)
                    nc.scalar.activation(BGT[:, c % 2], ps[:, 0:2, :].rearrange("p a b -> p (a b)"), ACT.Copy)\
                        .then_inc(bg_ready, 1)
                    act.wait_ge(od_mm, 6 * c + 4)
                    nc.scalar.activation(CONVT[:, c % 2], ps[:, 2:4, :].rearrange("p a b -> p (a b)"), ACT.Copy)\
                        .then_inc(bg_ready, 1)

            def routing(l):
                act.wait_ge(gexp_in, 2 * l + 1)
                nc.scalar.activation(GRP[:, 1], GRP[:, 1], ACT.Exp).then_inc(gexp_out, 1)
                act.wait_ge(gexp_in, 2 * l + 2)
                nc.scalar.activation(SC[:, 4], SC[:, 4], ACT.Exp).then_inc(gexp_out, 1)

            def experts(l):
                e0 = l * (NE // 2)
                with act.Fori(0, NE // 2) as i:
                    for b in range(2):
                        act.wait_ge(up_mm[b], i + e0 + 1)
                        nc.scalar.activation(SL, bank(2), ACT.Silu).then_inc(sl_ready[b], 1)

            def overflow(l):
                flag = act.value_load(ANY[0:1, 0:1])
                with act.If(flag > 0):
                    with act.Fori(0, NOV) as n:
                        act_flag = act.value_load(ACTIVE[0:1, bass.ds(n + NE, 1)])
                        with act.If(act_flag > 0):
                            act.wait_ge(ov_up, n + (l * NOV + 1))
                            nc.scalar.activation(SL, bank(2), ACT.Silu).then_inc(ov_sl, 1)
                            act.wait_ge(ov_sl, n + (l * NOV + 1))
                            act.sem_inc(waited, 1)
                        with act.Else():
                            act.sem_inc(ov_sl, 1)
                with act.Else():
                    act.sem_inc(ov_sl, NOV)
                act.sem_inc(ov_left, 1)

            for l in range(DEPTH):
                if l:
                    norm(2, H, at(32768, 2, D))
                    columns(2, lambda i, j: U[:, j, i * P:(i + 1) * P])
                    od_gates()
                norm(2 * l + 1, H, at(30720, 2, D))
                columns(2 * l + 1, lambda i, j: VTT[:, i % 2, j * P:(j + 1) * P])
                routing(l)
                experts(l)
                act.wait_ge(tab_ready, l + 1)
                overflow(l)
            norm(4, H, at(32768, 2, D))

        @block.tensor
        def _(pe):
            def slab_in(n, loads=1):
                before = sum(3 if (L0_HY <= m < L0_OUT or L1_IN <= m < L1_OUT) else 1
                             for m in range(n % RING, n, RING) if m >= L0_MOD)
                pe.wait_ge(slab_full[n % RING], 16 * (before + loads))

            def modulation():
                pe.wait_ge(silu_ready, 1)
                for n in range(NMOD):
                    slab_in(L0_MOD + n)
                    if n >= 2:
                        pe.wait_ge(mod_row, n - 1)
                    w = slab(L0_MOD + n, KC, 512)
                    for j in range(KC):
                        ins = nc.tensor.matmul(bank(n % 2)[0:2], silu_c[:, j], w[:, j], start=j == 0, stop=j == KC - 1)
                    ins.then_inc(mod_mm, 1)
                pe.wait_ge(s_cst, 16)
                pe.wait_ge(pool_step, 2)
                pe.wait_ge(s_rows, 16 * (13 + 3))
                nc.tensor.transpose(bank(5)[:, 0:N_ROWS], small_rows[:], ident[0:N_ROWS, 0:N_ROWS])\
                    .then_inc(rows_T, 1)
                for j in range(KC):
                    ins = nc.tensor.transpose(bank(6)[:, j * N_VEC:(j + 1) * N_VEC], VEC[:, j::KC],
                                              ident[0:N_VEC, 0:N_VEC])
                ins.then_inc(vec_T, 1)
                for s in range(2):
                    pe.wait_ge(mod_row, 2 * s + 2)
                    for j in range(KC):
                        ins = nc.tensor.transpose(bank(2)[:, (s * KC + j) * 2:(s * KC + j) * 2 + 2],
                                                  MROW[0:2, s, j::KC], ident[0:2, 0:2])
                    ins.then_inc(mod_T, 1)

            def late_columns(g):
                pe.wait_ge(m_used, 2 * g + 2)
                if g:
                    pe.wait_ge(m_ready, g)
                for j in range(KC):
                    ins = nc.tensor.matmul(bank(7)[:, g * KC + j:g * KC + j + 1], ACC[:, g % 2, j::KC],
                                           cst[:, K_ONE:K_ONE + 1], start=True, stop=True)
                ins.then_inc(m_cols, 1)

            def gate_rows(l):
                pe.wait_ge(m_ready, NSEC)
                for g in range(2):
                    for half in range(2):
                        for j in range(KC):
                            ins = nc.tensor.matmul(bank((2, 3, 6, 7)[2 * g + half])[:, j::KC],
                                                   mod[:, l, 3 * g + 2, j:j + 1].to_broadcast([P, P]),
                                                   ident[:, half * 64:(half + 1) * 64], start=True, stop=True)
                        ins.then_inc(mod_bc, 1)

            def transposes(n, i, xn):
                pe.wait_ge(xn_ready, norm_base[n] + i + 1)
                if i >= 2:
                    pe.wait_ge(u_ready, norm_base[n] + i - 1)
                    pe.wait_ge(u_act, norm_base[n] + i - 1)
                for j in range(KC):
                    ins = nc.tensor.transpose(bank(4 * (i % 2) + j // 4)[:, (j % 4) * P:(j % 4 + 1) * P],
                                              xn[:, i % 2, j * P:(j + 1) * P], ident)
                ins.then_inc(xn_T, 1)

            modulation()
            for i in range(TT + CT):
                if i == 0:
                    pe.wait_ge(mod_ready, 1)
                transposes(0, i, at(41984, 2, D))

            def u_cols(i, j):
                return U[:, j, i * P:(i + 1) * P] if i < TT else UC[:, j, (i - TT) * P:(i - TT + 1) * P]

            def u_part(q, j):
                return U[:, j, q * 512:(q + 1) * 512] if q < 2 else UC[:, j]

            def gla_projections():
                slab_in(L0_V)
                w = slab(L0_V, KC, GV)
                for i in range(TT + CT):
                    if i == 0:
                        pe.wait_ge(u_ready, TT + CT)
                        pe.wait_ge(u_act, TT + CT)
                    if i >= 4:
                        pe.wait_ge(v_ready, i - 3)
                    for j in range(KC):
                        ins = nc.tensor.matmul(bank(i % 4), u_cols(i, j), w[:, j], start=j == 0, stop=j == KC - 1)
                    ins.then_inc(v_mm, 1)
                    if i in (2, 4, 6, 8):
                        late_columns(i // 2 - 1)
                pe.wait_ge(small_in, SMALL0)
                for q in range(3):
                    n = 512 if q < 2 else CTX
                    for j in range(KC):
                        ins = nc.tensor.matmul(bank(4 + q)[0:2 * RANK, 0:n], w_rank[:, j], u_part(q, j),
                                               start=j == 0, stop=j == KC - 1)
                    ins.then_inc(r_mm, 1)
                    if q == 1:
                        late_columns(4)

            def gla_head(h):
                wqk = slab(L0_QK, KC, 2 * QK)
                if h % 2 == 0:
                    slab_in(L0_QK)
                    if h == 0:
                        pe.wait_ge(v_ready, TT + CT)
                        pe.wait_ge(r_ready, 3)
                    else:
                        pe.wait_ge(omix_ready, 2 * h)
                        pe.wait_ge(o_copied, TT * h)
                        pe.wait_ge(state_ready, h)
                    for q in range(5):
                        part = q if q < 2 else q - 2
                        n = 512 if part < 2 else CTX
                        c0 = (0 if q < 2 else QK) + (h // 2) * P
                        for j in range(KC):
                            ins = nc.tensor.matmul(bank(q)[:, 0:n], wqk[:, j, c0:c0 + P], u_part(part, j),
                                                   start=j == 0, stop=j == KC - 1)
                        ins.then_inc(qk_mm, 1)
                        if h == 0 and q % 2 == 0:
                            late_columns(5 + q // 2)
                if h == 0:
                    for g in range(8, NSEC):
                        late_columns(g)
                    pe.wait_ge(m_ready, NSEC)
                if h:
                    pe.wait_ge(at_ready, TT * h)
                    pe.wait_ge(o_copied, TT * h)
                for q in range(3):
                    n = 512 if q < 2 else CTX
                    nc.tensor.matmul(bank(5 + q)[:, 0:n], w_gate_up[:, h], RT[:, q * 512:q * 512 + n],
                                     start=True, stop=True).then_inc(gx_mm, 1)
                slab_in(L0_G)
                pe.wait_ge(qk_ready, 5 * (h // 2 + 1))
                if h:
                    pe.wait_ge(omix_ready, 2 * h)
                wg = slab(L0_G, KC, GV)
                for half in range(2):
                    for j in range(KC):
                        ins = nc.tensor.matmul(bank(half), wg[:, j, h * DV:(h + 1) * DV], u_part(half, j),
                                               start=j == 0, stop=j == KC - 1)
                    ins.then_inc(g_mm, 1)
                pe.wait_ge(gx_read, 6 * (h + 1))
                pe.wait_ge(kr_ready, 3 * h + 1)
                for q in range(3):
                    for i in range(4 * q, min(4 * q + 4, TT + CT)):
                        ins = nc.tensor.transpose(bank(5 + q)[:, (i % 4) * P:(i % 4 + 1) * P],
                                                  T1[:, i * P:(i + 1) * P], ident)
                    ins.then_inc(kr_T, 1)
                pe.wait_ge(krt_ready, 3 * (h + 1))
                pe.wait_ge(sg_ready, 2 * (h + 1))
                for c in range(NCH + NCC):
                    r = slice((c % 2) * CH, (c % 2 + 1) * CH)
                    ins = nc.tensor.matmul(ds_place(c), KRT[r, c // 2],
                                           HEAD_V[r, c // 2, h * DV:(h + 1) * DV], start=True, stop=True)
                ins.then_inc(ds_mm, 1)

                def scores(i):
                    cols_ = slice(i * P, (i + 1) * P)
                    for d in range(2):
                        r = slice(d * DK, (d + 1) * DK)
                        ins = nc.tensor.matmul(bank((5, 1)[i % 2] + d)[:, 0:P], KD[r, cols_], Q[r, cols_],
                                               start=True, stop=True)
                    ins.then_inc(a_mm, 1)

                pe.wait_ge(qd_ready, h + 1)
                scores(0)
                pe.wait_ge(state_ready, h + 1)
                scores(1)
                for i in range(TT):
                    if i >= 2:
                        pe.wait_ge(o_copied, TT * h + i - 1)
                    pe.wait_ge(at_ready, TT * h + i + 1)
                    o = bank((7, 0)[i % 2])[:, 0:P]
                    v = HEAD_V[:, i, h * DV:(h + 1) * DV]
                    nc.tensor.matmul(o, AT[:, i % 2, 0], v, start=True, stop=False, skip_group_check=True)
                    nc.tensor.matmul(o, AT[:, i % 2, 1], v, start=False, stop=False, skip_group_check=True)
                    for c in range(2):
                        rows = slice(c * CH, (c + 1) * CH)
                        t0 = (2 * i + c) * CH
                        ins = nc.tensor.matmul(o[rows], Q[:, t0:t0 + CH], ST[:, 2 * i + c], start=False, stop=c == 1,
                                               skip_group_check=True)
                    ins.then_inc(o_mm, 1)
                    if i + 2 < TT:
                        scores(i + 2)
                pe.wait_ge(on_ready, h + 1)
                for half in range(2):
                    for i in range(4 * half, 4 * half + 4):
                        ins = nc.tensor.transpose(bank(3 + half)[:, (i % 4) * P:(i % 4 + 1) * P], OT[:, i], ident)
                    ins.then_inc(o_T, 1)

            gla_projections()
            for h in range(HEADS):
                gla_head(h)

            def hyena_projection():
                pe.wait_ge(omix_ready, 2 * HEADS)
                for c in range(HC):
                    slab_in(L0_HY + c, 3)
                    w = slab(L0_HY + c, 3, KC, P)
                    for k in range(3):
                        if c:
                            pe.wait_ge(conv_done, 3 * (c - 1) + k + 1)
                        for half in range(2):
                            for j in range(KC):
                                ins = nc.tensor.matmul(bank(2 * k + half), w[:, k, j], u_part(half, j),
                                                       start=j == 0, stop=j == KC - 1)
                            ins.then_inc(hy_mm, 1)
                    if c:
                        hyena_transposes(c - 1)
                hyena_transposes(HC - 1)

            def hyena_transposes(c):
                pe.wait_ge(vx_ready, c + 1)
                for par in range(2):
                    if c:
                        pe.wait_ge(vtm_ready, 2 * (c - 1) + par + 1)
                    for tc in range(KT):
                        ins = nc.tensor.transpose(bank(6 + par)[:, tc * P:(tc + 1) * P],
                                                  VX[:, c, par + 2 * tc * P:par + 2 * (tc + 1) * P - 1:2], ident)
                    ins.then_inc(vx_T, 1)

            hyena_projection()

            def spectrum(kt, q):
                fn, par = (q % 4) // 2, q % 2
                if kt:
                    pe.wait_ge(uk_ready, 8 * (kt - 1) + q + 1)
                for tc in range(KT):
                    rhs = VTM[:, par, tc] if q < 4 else (HSUM, HDIF)[fn][:, par * KT + tc]
                    ins = nc.tensor.matmul(bank((q + 4) % 8), DFT[:, kt, fn, par, tc * P:(tc + 1) * P], rhs,
                                           start=tc == 0, stop=tc == KT - 1)
                ins.then_inc(dft_mm, 1)

            def hyena_filters():
                pe.wait_ge(vtm_ready, 2 * HC)
                pe.wait_ge(conv_done, 3 * HC)
                gate_rows(0)
                pe.wait_ge(tables_in, 16)
                spectrum(0, 0)
                pe.wait_ge(flt_in, 64)
                for half in range(2):
                    nc.tensor.matmul(bank(half)[0:HID], w_hy1[:], ZT[0:EMB, half * 512:(half + 1) * 512],
                                     start=True, stop=True).then_inc(f_mm, 1)
                spectrum(0, 1)
                pe.wait_ge(mod_gate, 4)
                spectrum(0, 2)
                pe.wait_ge(f_sin, 1)
                for half in range(2):
                    nc.tensor.matmul(bank(2 + half)[0:HID], w_hy2[:], HH1[0:HID, half * 512:(half + 1) * 512],
                                     start=True, stop=True).then_inc(f_mm, 1)
                spectrum(0, 3)
                pe.wait_ge(f_sin, 2)
                for t in range(2 * KT):
                    par, tc = t // KT, t % KT
                    if t >= 2:
                        pe.wait_ge(filt_ready, t - 1)
                    for k in range(2):
                        nc.tensor.matmul(bank(2 * (t % 2) + k),
                                         HH2[0:HID, par + 2 * tc * P:par + 2 * (tc + 1) * P - 1:2],
                                         W3H[0:HID, k * HW:(k + 1) * HW], start=True, stop=True).then_inc(h3_mm, 1)

            hyena_filters()

            def transform():
                pe.wait_ge(filt_ready, 2 * KT)
                for kt in range(KT):
                    for q in range(8):
                        if kt or q >= 4:
                            spectrum(kt, q)

            def inverse():
                pe.wait_ge(tables_in, 48)

                def part(c, par, kts, first, last):
                    for fn in range(2):
                        for kt in kts:
                            ins = nc.tensor.matmul(
                                bank(2 * (c % 4) + par), YF[:, kt, 2 * fn + par, c * P:(c + 1) * P],
                                IDFT[:, fn, par, kt * HALF:(kt + 1) * HALF],
                                start=first and fn == 0 and kt == kts[0], stop=last and fn == 1 and kt == kts[-1])
                    return ins

                pe.wait_ge(yf_dve, 2 * (KT - 1))
                pe.wait_ge(yf_pool, 2 * (KT - 1))
                for c in range(HC):
                    for par in range(2):
                        q = (2 * c + par + 4) % 8
                        pe.wait_ge(uk_ready, 8 * (KT - 1) + q + 1)
                        part(c, par, list(range(KT - 1)), True, False)
                pe.wait_ge(yf_dve, 2 * KT)
                pe.wait_ge(yf_pool, 2 * KT)
                for c in range(HC):
                    for par in range(2):
                        part(c, par, [KT - 1], False, True).then_inc(idft_mm, 1)

            transform()
            inverse()

            def projection_out(l, first, mixed):
                for i in range(TT):
                    for half in range(2):
                        n = 2 * i + half
                        if i == 0:
                            slab_in(first + half)
                        if n >= 4:
                            pe.wait_ge(h_ready, 2 * TT * l + n - 3)
                        for j in range(KC):
                            ins = nc.tensor.matmul(bank(n % 4), mixed[:, j, i * P:(i + 1) * P],
                                                   slab(first + half, KC, 512)[:, j],
                                                   start=j == 0, stop=j == KC - 1)
                        ins.then_inc(out_mm, 1)

            pe.wait_ge(hmix_ready, 2 * HC)
            projection_out(0, L0_OUT, MIX)

            def router(l):
                n = 2 * l + 1
                pe.wait_ge(small_in, SMALL0 + 64 * l)
                pe.wait_ge(h_ready, 2 * TT * (l + 1))

                def logits(i):
                    pe.wait_ge(u_ready, norm_base[n] + i + 1)
                    pe.wait_ge(u_act, norm_base[n] + i + 1)
                    if i >= 2:
                        pe.wait_ge(lg_ready, l * TT + i - 1)
                    lg = bank(2 + 4 * (i % 2))[:, 0:NG + NE]
                    for j in range(KC):
                        nc.tensor.matmul(lg, VTT[:, i % 2, j * P:(j + 1) * P], w_router[:, j], start=j == 0, stop=False)
                    nc.tensor.matmul(lg, cst[0:1, K_ONE:K_ONE + P], b_router[0:1], start=False, stop=True)\
                        .then_inc(lg_mm, 1)

                for i in range(TT):
                    transposes(n, i, at(24576, 2, D))
                    if i:
                        logits(i - 1)
                logits(TT - 1)

            def slots(l):
                pe.wait_ge(oh_ready, l + 1)
                ones = cst[:, K_ONE:K_ONE + P]
                pe.wait_ge(lg_ready, (l + 1) * TT)
                nc.tensor.matmul(bank(0)[:, 0:TT * NE], cst[:, K_UT:K_UT + P], SUMOH, start=True, stop=False,
                                 skip_group_check=True)
                for d in range(1, TT):
                    ins = nc.tensor.matmul(bank(0)[:, d * NE:TT * NE], ones, SUMOH[:, 0:(TT - d) * NE],
                                           start=False, stop=d == TT - 1, skip_group_check=True)
                ins.then_inc(pos_mm, 1)
                for i in range(TT):
                    ins = nc.tensor.matmul(bank(1)[:, 0:NE], ones, SUMOH[:, i * NE:(i + 1) * NE],
                                           start=i == 0, stop=i == TT - 1)
                ins.then_inc(pos_mm, 1)
                pe.wait_ge(hot_ready, l + 1)
                for n in range(2 * TT):
                    ins = nc.tensor.matmul(bank(3)[:, 0:2 * NE], HOT0[:, n], RHS0[:, n].rearrange("p a b -> p (a b)"),
                                           start=n == 0, stop=n == 2 * TT - 1)
                ins.then_inc(tab_mm, 1)

            def overflow_tables(l):
                for n in range(2 * TT):
                    pe.wait_ge(ov_hot, 2 * TT * l + n + 1)
                    nc.tensor.matmul(bank(3), HOT[:, n % 2], RHS[:, n % 2].rearrange("p a b -> p (a b)"),
                                     start=n == 0, stop=n == 2 * TT - 1).then_inc(ov_tmm, 1)
                pe.wait_ge(ov_tab, l + 1)

            def up(b, w, x):
                for c in range(FC):
                    for j in range(KC):
                        ins = nc.tensor.matmul(bank(b)[:, c * P:(c + 1) * P], w[:, j, c::FC], x[:, j],
                                               start=j == 0, stop=j == KC - 1)
                return ins

            def experts(l):
                e0 = l * (NE // 2)

                def turn(b, i):
                    pe.wait_ge(x_full[b], (i + e0 + 1) * 16)
                    for j in range(KC):
                        ins = nc.tensor.transpose(bank(j // 4)[:, (j % 4) * P:(j % 4 + 1) * P],
                                                  XG[:, b, j * P:(j + 1) * P], ident)
                        if j % 4 == 3:
                            ins.then_inc(x_T[b], 1)

                def expert(b, i, first, last):
                    x = XT[:, b].rearrange("p (j t) -> p j t", j=KC)
                    pe.wait_ge(xt_ready[b], (i + e0 + 1) * 2)
                    for m, done in ((0, up_mm), (1, gate_mm)):
                        pe.wait_ge(w_full[b][m], (i + e0 + 1) * 16)
                        up(2 + m, w_slot(b, m, KC, FE), x).then_inc(done[b], 1)
                    if not last:
                        turn(1 - b, i + b)
                    pe.wait_ge(ht_ready[b], i + e0 + 1)
                    pe.wait_ge(w_full[b][2], (i + e0 + 1) * 16)
                    if b:
                        pe.wait_ge(y_ready[0], (i + e0 + 1) * 2)
                    elif not first:
                        pe.wait_ge(y_ready[1], (i + e0) * 2)
                    w = w_slot(b, 2, FC, D)
                    for half in range(2):
                        for j in range(FC):
                            ins = nc.tensor.matmul(bank(5 + half), HT[:, j * P:(j + 1) * P],
                                                   w[:, j, half * 512:(half + 1) * 512],
                                                   start=j == 0, stop=j == FC - 1)
                        ins.then_inc(y_mm[b], 1)

                pe.wait_ge(tab_ready, l + 1)
                turn(0, 0)
                for b in range(2):
                    expert(b, 0, l == 0, False)
                with pe.Fori(0, NE // 2 - 2) as i:
                    for b in range(2):
                        expert(b, i + 1, False, False)
                for b in range(2):
                    expert(b, NE // 2 - 1, False, b == 1)

            def overflow(l):
                flag = pe.value_load(ANY[0:1, 0:1])
                with pe.If(flag > 0):
                    overflow_tables(l)
                    with pe.Fori(0, NOV) as n:
                        act_flag = pe.value_load(ACTIVE[0:1, bass.ds(n + NE, 1)])
                        with pe.If(act_flag > 0):
                            pe.wait_ge(ov_x[l], (n + 1) * 16)
                            for j in range(KC):
                                ins = nc.tensor.transpose(bank(j // 4)[:, (j % 4) * P:(j % 4 + 1) * P],
                                                          XG[:, 0, j * P:(j + 1) * P], ident)
                            ins.then_inc(ov_xT, 1)
                            pe.wait_ge(ov_xt, n + (l * NOV + 1))
                            for m, done in ((0, ov_up), (1, ov_gate)):
                                pe.wait_ge(ov_w[m], (n + (l * NOV + 1)) * 16)
                                up(2 + m, w_slot(0, m, KC, FE), XT[:, 0].rearrange("p (j t) -> p j t", j=KC))\
                                    .then_inc(done, 1)
                            pe.wait_ge(ov_ht, n + (l * NOV + 1))
                            pe.wait_ge(ov_w[2], (n + (l * NOV + 1)) * 16)
                            for half in range(2):
                                for j in range(FC):
                                    ins = nc.tensor.matmul(bank(5 + half), HT[:, j * P:(j + 1) * P],
                                                           w_slot(0, 2, FC, D)[:, j, half * 512:(half + 1) * 512],
                                                           start=j == 0, stop=j == FC - 1)
                            ins.then_inc(ov_ymm, 1)
                            pe.wait_ge(ov_ymm, n + (l * NOV + 1))
                            pe.sem_inc(waited, 1)
                        with pe.Else():
                            for s in (ov_xT, ov_up, ov_gate, ov_ymm):
                                pe.sem_inc(s, 1)
                with pe.Else():
                    pe.sem_inc(ov_tmm, 2 * TT)
                    pe.sem_inc(ov_xT, NOV)
                    pe.sem_inc(ov_up, NOV)
                    pe.sem_inc(ov_gate, NOV)
                    pe.sem_inc(ov_ymm, NOV)
                pe.sem_inc(ov_left, 1)

            def shortconv():
                pe.wait_ge(ov_left, 5)
                gate_rows(1)
                for i in range(TT):
                    transposes(2, i, at(28672, 2, D))
                pe.wait_ge(mod_gate, 8)
                pe.wait_ge(u_ready, norm_base[2] + TT)
                pe.wait_ge(u_act, norm_base[2] + TT)
                for c in range(KC):
                    slab_in(L1_IN + c, 3)
                    w = slab(L1_IN + c, 3, KC, P)
                    for k in range(3):
                        if c:
                            if k < 2:
                                pe.wait_ge(bg_ready, 2 * (c - 1) + k + 1)
                            else:
                                pe.wait_ge(od_conv, c)
                        for half in range(2):
                            for j in range(KC):
                                ins = nc.tensor.matmul(bank(2 * k + half), w[:, k, j], u_part(half, j),
                                                       start=j == 0, stop=j == KC - 1)
                            ins.then_inc(od_mm, 1)
                pe.wait_ge(od_conv, KC)
                projection_out(1, L1_OUT, GTM)

            for l in range(DEPTH):
                if l:
                    shortconv()
                router(l)
                slots(l)
                experts(l)
                overflow(l)

        @block.vector
        def _(dve):
            count = [0]

            def step(ins):
                count[0] += 1
                ins.then_inc(dve_step, 1)
                return count[0]

            def settle(n=None):
                dve.wait_ge(dve_step, count[0] if n is None else n)

            def link(ins):
                step(ins)
                settle()

            V = nc.vector

            def norm(n, src, xn, target, gain, shift):
                dve.wait_ge(sq_done, norm_base[n + 1])
                m = NORMS[n]
                V.tensor_scalar(rstd[:, 0:m], ss[:, 0:m], 1.0 / D, EPS, ALU.mult, ALU.add).then_inc(ms_ready, 1)
                dve.wait_ge(root_ready, n + 1)
                link(V.reciprocal(rstd[:, 0:m], rstd[:, 0:m]))

                def columns(i):
                    dve.wait_ge(xn_T, norm_base[n] + i + 1)
                    if n in (1, 3) and i >= 2:
                        dve.wait_ge(lg_mm, (n // 2) * TT + i - 1)
                    for j in range(KC // 2):
                        ins = V.tensor_scalar(target(i, j), bank(4 * (i % 2))[:, j * P:(j + 1) * P],
                                              gain(i, j), shift(i, j), ALU.mult, ALU.add)
                    ins.then_inc(u_ready, 1)
                    if n in (1, 3) and i:
                        logits(n // 2, i - 1)

                for i in range(m):
                    if i >= 2:
                        dve.wait_ge(xn_T, norm_base[n] + i - 1)
                        if n in (1, 3):
                            dve.wait_ge(hn_out[i % 2], 16 * ((n // 2) * (TT // 2) + i // 2))
                    V.tensor_scalar(xn[:, i % 2].rearrange("t (c p) -> t p c", p=P),
                                    src[:, i].rearrange("t (p c) -> t p c", c=KC),
                                    rstd[:, i:i + 1], None, ALU.mult).then_inc(xn_ready, 1)
                    if i:
                        columns(i - 1)
                columns(m - 1)
                if n in (1, 3):
                    logits(n // 2, m - 1)

            def logits(l, i):
                dve.wait_ge(lg_mm, l * TT + i + 1)
                V.tensor_copy(LG[:, i], bank(2 + 4 * (i % 2))[:, 0:NG + NE]).then_inc(lg_ready, 1)

            def modulation():
                for n in range(NMOD):
                    dve.wait_ge(mod_mm, n + 1)
                    V.tensor_copy(MROW[0:2, n // 2, (n % 2) * 512:(n % 2 + 1) * 512], bank(n % 2)[0:2])\
                        .then_inc(mod_row, 1)
                dve.wait_ge(rows_T, 1)
                link(V.tensor_copy(cols[:], bank(5)[:, 0:N_ROWS]))
                V.tensor_scalar(neg_ba[:], cols[:, R_BA:R_HY], -1.0, None, ALU.mult).then_inc(cols_ready, 1)
                dve.wait_ge(vec_T, 1)
                step(V.tensor_copy(vec_cols[:], bank(6)[:, 0:KC * N_VEC].rearrange("p (a b) -> p a b", b=N_VEC)))
                dve.wait_ge(mod_T, 2)
                settle()
                for s in range(2):
                    for r, dst in ((0, mod[:, 0, s]), (1, mod_ctx[:, s])):
                        ps_col = bank(2)[:, s * KC * 2:(s + 1) * KC * 2].rearrange("p (j r) -> p j r", r=2)[:, :, r]
                        step(V.tensor_tensor(dst, ps_col, vec_cols[:, :, s], ALU.add))
                settle()
                gain(0, mod[:, 0, 1], V_NMIX)
                gain(2 * DEPTH, mod_ctx[:, 1], V_NMIX)
                settle()
                dve.sem_inc(mod_ready, 1)

            def gain(n, scale, v):
                step(V.scalar_tensor_tensor(out=gain_x[:, n], in0=scale, scalar=1.0, in1=vec_cols[:, :, v],
                                            op0=ALU.add, op1=ALU.mult))

            def late_modulation():
                def columns_in(g):
                    l, s = SECTIONS[g]
                    dve.wait_ge(m_cols, g + 1)
                    V.tensor_tensor(mod[:, l, s], bank(7)[:, g * KC:(g + 1) * KC], vec_cols[:, :, 6 * l + s], ALU.add)\
                        .then_inc(m_ready, 1)

                dve.wait_ge(xn_ready, TT + CT)
                dve.wait_ge(silu_ready, 1)
                for g in range(NSEC):
                    for half in range(2):
                        m = 2 * g + half
                        dve.wait_ge(m_full[m % 3], 16 * (m // 3 + 1))
                        w = M_SLABS[m % 3]
                        acc = ACC[:, g % 2, half * 512:(half + 1) * 512]
                        link(V.tensor_scalar(acc, w[:, 0], silu_c[:, 0, 0:1], None, ALU.mult))
                        for j in range(1, KC):
                            ins = V.scalar_tensor_tensor(out=acc, in0=w[:, j], scalar=silu_c[:, j, 0:1], in1=acc,
                                                         op0=ALU.mult, op1=ALU.add)
                            if j < KC - 1:
                                link(ins)
                        ins.then_inc(m_used, 1)
                        if g and not half:
                            columns_in(g - 1)
                columns_in(NSEC - 1)
                dve.wait_ge(m_ready, NSEC)
                dve.wait_ge(m_used, 2 * NSEC)
                for l in range(DEPTH):
                    if l:
                        gain(2 * l, mod[:, l, 1], V_NMIX + l)
                    gain(2 * l + 1, mod[:, l, 4], V_NFFN + l)
                settle()

            def gate_rows(l):
                for g in range(2):
                    for half in range(2):
                        dve.wait_ge(mod_bc, 4 * l + 2 * g + half + 1)
                        V.tensor_copy(gates[:, g, half * 512:(half + 1) * 512], bank((2, 3, 6, 7)[2 * g + half]))\
                            .then_inc(mod_gate, 1)
                dve.wait_ge(mod_gate, 4 * (l + 1))

            dve.wait_ge(s_cst, 16)
            for k in range(2):
                step(V.tensor_scalar(row_number[:, k], cst[:, K_TV:K_TV + TT], float(k) - FAR, None, ALU.add))
            modulation()
            norm(0, X0, at(41984, 2, D),
                 lambda i, j: U[:, j, i * P:(i + 1) * P] if i < TT else UC[:, j, (i - TT) * P:(i - TT + 1) * P],
                 lambda i, j: gain_x[:, 0 if i < TT else 2 * DEPTH, j:j + 1],
                 lambda i, j: mod[:, 0, 0, j:j + 1] if i < TT else mod_ctx[:, 0, j:j + 1])

            def gla_head(h):
                for q in range(3):
                    n = 512 if q < 2 else CTX
                    cs = slice(q * 512, q * 512 + n)
                    dve.wait_ge(gx_mm, 3 * h + q + 1)
                    V.tensor_scalar(T1[:, cs], bank(5 + q)[:, 0:n], cols[:, R_BA + h:R_BA + h + 1], 0.0,
                                    ALU.add, ALU.min).then_inc(gx_read, 1)
                for q in range(3):
                    n = 512 if q < 2 else CTX
                    cs = slice(q * 512, q * 512 + n)
                    dve.wait_ge(gx_read, 6 * h + 3 + q)
                    V.scalar_tensor_tensor(out=BB[:, cs], in0=T1[:, cs], scalar=2.0, in1=bank(5 + q)[:, 0:n],
                                           op0=ALU.mult, op1=ALU.subtract).then_inc(gx_read, 1)
                dve.wait_ge(ln_ready, h + 1)
                link(V.tensor_tensor(T1, T1, BB, ALU.subtract))
                step(V.tensor_tensor_scan(BB[0:DK], SCAN1[0:DK], T1[0:DK], 0.0, ALU.mult, ALU.add))
                link(V.tensor_tensor_scan(BB[DK:P, TOK - 1::-1], SCAN1[DK:P], T1[DK:P, TOK - 1::-1], 0.0,
                                          ALU.mult, ALU.add))
                bv = BB.rearrange("p (c t) -> p c t", t=CH)
                tv = T1.rearrange("p (c t) -> p c t", t=CH)
                shape = [DK, NCH + NCC, CH]
                V.tensor_tensor(tv[0:DK], bv[0:DK, :, CH - 1:CH].to_broadcast(shape), bv[0:DK], ALU.subtract)\
                    .then_inc(cum_ready, 1)
                V.tensor_tensor(tv[DK:P], bv[DK:P, :, 0:1].to_broadcast(shape), bv[DK:P], ALU.subtract)\
                    .then_inc(cum_ready, 1)
                dve.wait_ge(er_ready, 3 * h + 1)
                dve.wait_ge(dup_pool, 2 * (h + 1))
                V.tensor_tensor(T1, K, T1, ALU.mult).then_inc(kr_ready, 1)
                dve.wait_ge(eb_ready, 2 * h + 1)
                V.tensor_tensor(KD, K[:, 0:SEQ], KD, ALU.mult).then_inc(kr_ready, 1)
                dve.wait_ge(eb_ready, 2 * h + 2)
                dve.wait_ge(dup_act, 2 * (h + 1))
                V.tensor_tensor(Q, Q, BB[:, 0:SEQ], ALU.mult).then_inc(kr_ready, 1)
                dve.wait_ge(kr_ready, 3 * (h + 1))
                dve.sem_inc(qd_ready, 1)

                dve.wait_ge(ds_mm, h + 1)
                dve.wait_ge(er_ready, 3 * (h + 1))

                def ds(c, r):
                    return ds_place(c)[r]

                fw, bw = slice(0, DK), slice(DK, P)
                order = {0: [NCH + n for n in range(NCC)] + list(range(NCH)),
                         1: [NCH + NCC - 1 - n for n in range(NCC)] + list(range(NCH - 1, -1, -1))}
                last = [0, 0]
                for n in range(NCC + NCH - 1):
                    for d, r in ((0, fw), (1, bw)):
                        c = order[d][n]
                        nxt = order[d][n + 1]
                        dst = (SCTX if n < NCC - 1 else ST[:, nxt])[r]
                        if n == 0:
                            last[d] = step(V.tensor_copy(dst, ds(c, r)))
                            continue
                        src = (SCTX if n < NCC else ST[:, c])[r]
                        settle(last[d])
                        last[d] = step(V.scalar_tensor_tensor(out=dst, in0=src, scalar=decay[r, c:c + 1],
                                                              in1=ds(c, r), op0=ALU.mult, op1=ALU.add))
                settle()
                dve.sem_inc(state_ready, 1)
                for i in range(TT):
                    dve.wait_ge(a_mm, TT * h + i + 1)
                    if h or i >= 2:
                        dve.wait_ge(o_mm, TT * h + i - 1)
                    V.copy_predicated(out=AT[:, i % 2],
                                      mask=cst[:, K_MASK:K_END].bitcast(I32).rearrange("p (a b) -> p a b", a=2),
                                      data=ps[:, (5, 1)[i % 2]:(5, 1)[i % 2] + 2, 0:P]).then_inc(at_ready, 1)
                dve.wait_ge(o_copied, TT * (h + 1))
                sq = BB[:, 0:SEQ].rearrange("p (a b) -> p a b", b=DV)
                link(V.tensor_tensor(sq, OT, OT, ALU.mult))
                link(V.tensor_reduce(ss[:, 0:TT], sq, AX.X, ALU.add))
                V.tensor_scalar(rstd[:, 0:TT], ss[:, 0:TT], 1.0 / DV, EPS, ALU.mult, ALU.add).then_inc(oss_ready, 1)
                dve.wait_ge(oroot_ready, h + 1)
                link(V.reciprocal(rstd[:, 0:TT], rstd[:, 0:TT]))
                V.tensor_tensor(OT, OT, rstd[:, 0:TT].unsqueeze(2).to_broadcast([P, TT, DV]), ALU.mult)\
                    .then_inc(on_ready, 1)
                for half in range(2):
                    dve.wait_ge(o_T, 2 * h + half + 1)
                    cs = slice(half * 512, (half + 1) * 512)
                    V.scalar_tensor_tensor(out=MIX[:, h, cs], in0=bank(3 + half), scalar=cols[:, R_GAIN:R_GAIN + 1],
                                           in1=SG[:, cs], op0=ALU.mult, op1=ALU.mult).then_inc(omix_ready, 1)

            late_modulation()
            dve.wait_ge(u_ready, TT + CT)
            step(V.memset(AT, 0.0))
            link(V.memset(SCAN1, 1.0))
            link(V.memset(SCAN1.rearrange("p (c t) -> p c t", t=CH)[:, :, 0:1], 0.0))
            for h in range(HEADS):
                gla_head(h)

            def conv(dst, src, w0, bias):
                if bias is None:
                    link(V.tensor_scalar(dst, src, w0(1), None, ALU.mult))
                else:
                    link(V.tensor_scalar(dst, src, w0(1), bias, ALU.mult, ALU.add))
                link(V.scalar_tensor_tensor(out=dst[:, 1:], in0=src[:, 0:SEQ - 1], scalar=w0(0), in1=dst[:, 1:],
                                            op0=ALU.mult, op1=ALU.add))
                return V.scalar_tensor_tensor(out=dst[:, 0:SEQ - 1], in0=src[:, 1:], scalar=w0(2),
                                              in1=dst[:, 0:SEQ - 1], op0=ALU.mult, op1=ALU.add)

            for c in range(HC):
                for k, dst in ((0, MIX[:, HC + c]), (1, X1C), (2, VC_)):
                    dve.wait_ge(hy_mm, 6 * c + 2 * k + 2)
                    src = ps[:, 2 * k:2 * k + 2, :].rearrange("p a b -> p (a b)")
                    r = R_CB + 4 * k + c
                    conv(dst, src, lambda w: cols[:, R_CW + 12 * w + 4 * k + c:R_CW + 12 * w + 4 * k + c + 1],
                         cols[:, r:r + 1]).then_inc(conv_done, 1)
                dve.wait_ge(conv_done, 3 * (c + 1))
                V.tensor_tensor(VX[:, c], VC_, X1C, ALU.mult).then_inc(vx_ready, 1)
            gate_rows(0)

            def sine_argument(first, b, f):
                for half in range(2):
                    dve.wait_ge(f_mm, first + half + 1)
                    step(V.tensor_scalar(ARG[0:HID, half * 512:(half + 1) * 512], bank(first + half)[0:HID],
                                         cols[0:HID, b:b + 1], cols[0:HID, f:f + 1], ALU.add, ALU.mult))
                settle()
                ar, tu = ARG[0:HID], TURNS[0:HID]
                link(V.tensor_scalar(tu, ar, 1.0 / (2 * np.pi), MAGIC, ALU.mult, ALU.add))
                link(V.tensor_scalar(tu, tu, MAGIC, None, ALU.subtract))
                link(V.scalar_tensor_tensor(out=ar, in0=tu, scalar=-TWO_PI_HI, in1=ar, op0=ALU.mult, op1=ALU.add))
                link(V.scalar_tensor_tensor(out=ar, in0=tu, scalar=-TWO_PI_LO, in1=ar, op0=ALU.mult, op1=ALU.add))
                V.tensor_scalar(ar, ar, PI_F, -PI_F, ALU.min, ALU.max).then_inc(f_arg, 1)

            sine_argument(0, R_HY, R_HY + 1)
            dve.wait_ge(f_sin, 1)
            sine_argument(2, R_HY + 2, R_HY + 3)
            dve.wait_ge(tables_in, 32)
            for t in range(2 * KT):
                dve.wait_ge(h3_copied, t + 1)
                b = 2 * (t % 2)
                step(V.tensor_tensor(HSUM[:, t], bank(b), FTMP[:, 0], ALU.add))
                link(V.tensor_tensor(HDIF[:, t], bank(b), FTMP[:, 0], ALU.subtract))
                step(V.tensor_tensor(HSUM[:, t], HSUM[:, t], WIN[:, t], ALU.mult))
                link(V.tensor_tensor(HDIF[:, t], HDIF[:, t], WIN[:, t], ALU.mult))
                dve.sem_inc(filt_ready, 1)
            for kt in range(KT):
                dve.wait_ge(uk_ready, 8 * (kt + 1))
                ua, ub, uc, ud, ka, kb, kc, kd = [UK[:, q] for q in range(8)]
                t0, t1 = CTMP[:, 0], CTMP[:, 1]
                for row_, terms, signs in ((0, ((ua, ka), (ub, kb), (uc, kc), (ud, kd)), (1, -1, -1)),
                                           (2, ((ua, kc), (ub, kd), (uc, ka), (ud, kb)), (1, 1, 1))):
                    step(V.tensor_tensor(t0, terms[0][0], terms[0][1], ALU.mult))
                    for q in range(3):
                        x, y = terms[q + 1]
                        link(V.tensor_tensor(t1, x, y, ALU.mult))
                        op = ALU.add if signs[q] > 0 else ALU.subtract
                        if q == 2:
                            V.tensor_tensor(YF[:, kt, row_], t0, t1, op).then_inc(yf_dve, 1)
                            dve.wait_ge(yf_dve, 2 * kt + row_ // 2 + 1)
                        else:
                            link(V.tensor_tensor(t0, t0, t1, op))
            for c in range(HC):
                for par in range(2):
                    n = 2 * c + par
                    dve.wait_ge(idft_mm, n + 1)
                    sl = slice(par, SEQ - 1 + par, 2)
                    tmp = CTMP[:, n % 2]
                    if c:
                        dve.wait_ge(hmix_ready, n - 1)
                    link(V.scalar_tensor_tensor(out=tmp, in0=VX[:, c, sl],
                                                scalar=cols[:, R_SKIP + c:R_SKIP + c + 1], in1=bank(n),
                                                op0=ALU.mult, op1=ALU.add))
                    V.tensor_tensor(MIX[:, HC + c, sl], tmp, MIX[:, HC + c, sl], ALU.mult).then_inc(hmix_ready, 1)

            def residual(l, tmp):
                for n in range(2 * TT):
                    dve.wait_ge(out_mm, 2 * TT * l + n + 1)
                    cs = slice((n % 2) * 512, (n % 2 + 1) * 512)
                    link(V.tensor_tensor(tmp[:, n % 2], bank(n % 4), gates[:, 0, cs], ALU.mult))
                    V.tensor_tensor(H[:, n // 2, cs], H[:, n // 2, cs], tmp[:, n % 2], ALU.add).then_inc(h_ready, 1)

            dve.wait_ge(tables_in, 64)
            residual(0, CTMP)

            def first_of_largest(dst, values, top, iota, n, scratch):
                shape = [P, TT, n]
                link(V.tensor_tensor(scratch, values, top.unsqueeze(2).to_broadcast(shape), ALU.is_equal))
                link(V.scalar_tensor_tensor(out=scratch, in0=scratch, scalar=-64.0,
                                            in1=iota.unsqueeze(1).to_broadcast(shape), op0=ALU.mult, op1=ALU.add))
                link(V.tensor_reduce(SC[:, 15], scratch, AX.X, ALU.min))
                link(V.tensor_tensor(dst, scratch, SC[:, 15].unsqueeze(2).to_broadcast(shape), ALU.is_equal))

            def routing(l):
                dve.wait_ge(lg_ready, (l + 1) * TT)
                lg4, lge = LG[:, :, 0:NG], LG[:, :, NG:]
                e64 = cst[:, K_E64:K_E64 + NE]
                link(V.tensor_reduce(SC[:, 0], lg4, AX.X, ALU.max))
                V.tensor_tensor(GRP[:, 1], lg4, SC[:, 0].unsqueeze(2).to_broadcast([P, TT, NG]), ALU.subtract)\
                    .then_inc(gexp_in, 1)
                first_of_largest(GRP[:, 0], lg4, SC[:, 0], e64[:, 0:NG], NG, GRP[:, 2])
                link(V.tensor_scalar(GRP[:, 3], GRP[:, 0], BIG, -BIG, ALU.mult, ALU.add))
                link(V.tensor_tensor(LEX.rearrange("p t (g e) -> p t g e", g=NG),
                                     lge.rearrange("p t (g e) -> p t g e", g=NG),
                                     GRP[:, 3].unsqueeze(3).to_broadcast([P, TT, NG, EPG]), ALU.add))
                link(V.tensor_reduce(SC[:, 1], LEX, AX.X, ALU.max))
                first_of_largest(ONE_HOT[0], LEX, SC[:, 1], e64, NE, MSK)
                link(V.scalar_tensor_tensor(out=LEX, in0=ONE_HOT[0], scalar=-3.0 * BIG, in1=LEX,
                                            op0=ALU.mult, op1=ALU.add))
                link(V.tensor_reduce(SC[:, 2], LEX, AX.X, ALU.max))
                V.tensor_tensor(SC[:, 4], SC[:, 2], SC[:, 1], ALU.subtract).then_inc(gexp_in, 1)
                first_of_largest(ONE_HOT[1], LEX, SC[:, 2], e64, NE, MSK)
                link(V.tensor_tensor(SUMOH.rearrange("p (t e) -> p t e", e=NE), ONE_HOT[0], ONE_HOT[1], ALU.add))
                dve.sem_inc(oh_ready, 1)
                dve.wait_ge(gexp_out, 2 * (l + 1))
                link(V.tensor_reduce(SC[:, 3], GRP[:, 1], AX.X, ALU.add))
                link(V.tensor_scalar(SC[:, 5], SC[:, 4], 1.0, None, ALU.add))
                link(V.tensor_tensor(SC[:, 5], SC[:, 5], SC[:, 3], ALU.mult))
                link(V.reciprocal(SC[:, 6], SC[:, 5]))
                link(V.tensor_tensor(SC[:, 7], SC[:, 6], SC[:, 4], ALU.mult))
                dve.wait_ge(pos_mm, 2 * l + 1)
                link(V.tensor_copy(POSM, bank(0)[:, 0:TT * NE].rearrange("p (t e) -> p t e", e=NE)))
                both = [P, 2, TT, NE]
                hots = HOTS_OF.rearrange("p (k t e) -> p k t e", k=2, t=TT)
                link(V.tensor_tensor(POS2.rearrange("p (k t e) -> p k t e", k=2, t=TT), hots,
                                     POSM.unsqueeze(1).to_broadcast(both), ALU.mult))
                place, tile, slot = [SC[:, q:q + 2].rearrange("p k t -> p (k t)") for q in (8, 10, 12)]
                link(V.tensor_reduce(place, POS2.rearrange("p (n e) -> p n e", e=NE), AX.X, ALU.add))
                link(V.tensor_scalar(tile, place, 1.0 / P, None, ALU.mult))
                over = RHS0.rearrange("p n m e -> p (n m e)")[:, 0:2 * TT * (NJ - 1)].rearrange(
                    "p (n j) -> p n j", j=NJ - 1)
                shape = [P, 2 * TT, NJ - 1]
                link(V.tensor_tensor(over, tile.unsqueeze(2).to_broadcast(shape),
                                     cst[:, K_J + 1:K_J + NJ].unsqueeze(1).to_broadcast(shape), ALU.is_ge))
                link(V.tensor_reduce(tile, over, AX.X, ALU.add))
                link(V.scalar_tensor_tensor(out=slot, in0=tile, scalar=-float(P), in1=place,
                                            op0=ALU.mult, op1=ALU.add))
                dve.wait_ge(pos_mm, 2 * l + 2)
                for j in range(NJ):
                    step(V.tensor_scalar(ACTIVE_F[:, j], bank(1)[:, 0:NE], float(P * j), None, ALU.is_gt))
                settle()
                link(V.tensor_reduce(ANY_F[:, 0:1], ACTIVE_F[:, 1], AX.X, ALU.max))
                step(V.tensor_copy(ANY[:, 0:1], ANY_F[:, 0:1]))
                link(V.tensor_copy(ACTIVE, ACTIVE_F.rearrange("p a b -> p (a b)")))
                shape = [P, 2 * TT, P]
                step(V.tensor_tensor(HOT0, cst[:, K_IOTA:K_IOTA + P].unsqueeze(1).to_broadcast(shape),
                                     slot.unsqueeze(2).to_broadcast(shape), ALU.is_equal))
                link(V.tensor_scalar(JEQ0, tile, 0.0, None, ALU.is_equal))
                rows = row_number[:].rearrange("p k t -> p (k t)")
                gate = SC[:, 6:8].rearrange("p k t -> p (k t)")
                step(V.tensor_tensor(FIRST[:, 0], rows, JEQ0, ALU.mult))
                link(V.tensor_tensor(FIRST[:, 1], gate, JEQ0, ALU.mult))
                for m in range(2):
                    step(V.tensor_tensor(RHS0[:, :, m], HOTS_OF.rearrange("p (n e) -> p n e", e=NE),
                                         FIRST[:, m].unsqueeze(2).to_broadcast([P, 2 * TT, NE]), ALU.mult))
                settle()
                dve.sem_inc(hot_ready, 1)
                dve.wait_ge(tab_mm, l + 1)
                tables_out(NE)
                dve.sem_inc(tab_ready, 1)

            def tables_out(n):
                step(V.tensor_copy(GATE_OF[:, 0:n], bank(3)[:, n:2 * n]))
                link(V.tensor_scalar(SLOT_F[:, 0:n], bank(3)[:, 0:n], FAR, None, ALU.add))
                link(V.tensor_copy(SLOT_ROW[:, 0:n], SLOT_F[:, 0:n]))
                link(V.tensor_scalar(SLOT_TOK[:, 0:n], SLOT_ROW[:, 0:n], 1, None, ALU.logical_shift_right))

            def overflow_tables(l):
                for b in range(2):
                    dve.wait_ge(y_out[b], 16 * (NE // 2) * (l + 1))
                for n in range(2 * TT):
                    i, k = n // 2, n % 2
                    if n >= 2:
                        dve.wait_ge(ov_tmm, 2 * TT * l + n - 1)
                    step(V.tensor_scalar(HOT[:, k], cst[:, K_IOTA:K_IOTA + P], SC[:, 12 + k, i:i + 1], None,
                                         ALU.is_equal))
                    step(V.tensor_scalar(JEQ[:, k], cst[:, K_J:K_J + NJ], SC[:, 10 + k, i:i + 1], None, ALU.is_equal))
                    step(V.tensor_scalar(OV[:, k, 0], ONE_HOT[k][:, i], row_number[:, k, i:i + 1], None, ALU.mult))
                    link(V.tensor_scalar(OV[:, k, 1], ONE_HOT[k][:, i], SC[:, 6 + k, i:i + 1], None, ALU.mult))
                    shape = [P, NJ, NE]
                    for m in range(2):
                        step(V.tensor_tensor(RHS[:, k, m].rearrange("p (a b) -> p a b", b=NE),
                                             JEQ[:, k].unsqueeze(2).to_broadcast(shape),
                                             OV[:, k, m].unsqueeze(1).to_broadcast(shape), ALU.mult))
                    settle()
                    dve.sem_inc(ov_hot, 1)
                dve.wait_ge(ov_tmm, 2 * TT * (l + 1))
                tables_out(NJ * NE)
                dve.sem_inc(ov_tab, 1)

            def columns_of_x(l, b, done, halves):
                for j in range(KC):
                    ins = V.tensor_scalar(XT[:, b, j * P:(j + 1) * P],
                                          bank(j // 4)[:, (j % 4) * P:(j % 4 + 1) * P],
                                          gain_x[:, 2 * l + 1, j:j + 1], mod[:, l, 3, j:j + 1], ALU.mult, ALU.add)
                    if j % 4 == 3 and halves or j == KC - 1:
                        ins.then_inc(done, 1)

            def experts(l):
                e0 = l * (NE // 2)

                def x_cols(b, i):
                    dve.wait_ge(x_T[b], (i + e0 + 1) * 2)
                    columns_of_x(l, b, xt_ready[b], True)

                def expert(b, i, first, last):
                    dve.wait_ge(sl_ready[b], i + e0 + 1)
                    dve.wait_ge(gate_mm[b], i + e0 + 1)
                    V.tensor_tensor(HT, SL, bank(3), ALU.mult).then_inc(ht_ready[b], 1)
                    if not last:
                        x_cols(1 - b, i + b)
                    if not first:
                        dve.wait_ge(y_out[b], (i + e0) * 16)
                    for half in range(2):
                        cs = slice(half * 512, (half + 1) * 512)
                        dve.wait_ge(y_mm[b], (i + e0) * 2 + half + 1)
                        V.scalar_tensor_tensor(out=YS[:, b, cs], in0=bank(5 + half),
                                               scalar=GATE_OF[:, bass.ds(i * 2 + b, 1)], in1=gates[:, 1, cs],
                                               op0=ALU.mult, op1=ALU.mult).then_inc(y_ready[b], 1)

                x_cols(0, 0)
                for b in range(2):
                    expert(b, 0, l == 0, False)
                with dve.Fori(0, NE // 2 - 2) as i:
                    for b in range(2):
                        expert(b, i + 1, False, False)
                for b in range(2):
                    expert(b, NE // 2 - 1, False, b == 1)

            def overflow(l):
                dve.wait_ge(tab_ready, l + 1)
                flag = dve.value_load(ANY[0:1, 0:1])
                steps = count[0]
                with dve.If(flag > 0):
                    overflow_tables(l)
                    with dve.Fori(0, NOV) as n:
                        act_flag = dve.value_load(ACTIVE[0:1, bass.ds(n + NE, 1)])
                        with dve.If(act_flag > 0):
                            dve.wait_ge(ov_xT, n + (l * NOV + 1))
                            columns_of_x(l, 0, ov_xt, False)
                            dve.wait_ge(ov_sl, n + (l * NOV + 1))
                            dve.wait_ge(ov_gate, n + (l * NOV + 1))
                            V.tensor_tensor(HT, SL, bank(3), ALU.mult).then_inc(ov_ht, 1)
                            dve.wait_ge(ov_ymm, n + (l * NOV + 1))
                            for half in range(2):
                                cs = slice(half * 512, (half + 1) * 512)
                                ins = V.scalar_tensor_tensor(
                                    out=YS[:, 0, cs], in0=bank(5 + half),
                                    scalar=GATE_OF[:, bass.ds(n + NE, 1)], in1=gates[:, 1, cs],
                                    op0=ALU.mult, op1=ALU.mult)
                            ins.then_inc(ov_y, 1)
                            dve.wait_ge(ov_y, n + (l * NOV + 1))
                            dve.sem_inc(waited, 1)
                        with dve.Else():
                            for s in (ov_xt, ov_ht, ov_y):
                                dve.sem_inc(s, 1)
                with dve.Else():
                    dve.sem_inc(dve_step, count[0] - steps)
                    dve.sem_inc(ov_hot, 2 * TT)
                    dve.sem_inc(ov_tab, 1)
                    dve.sem_inc(ov_xt, NOV)
                    dve.sem_inc(ov_ht, NOV)
                    dve.sem_inc(ov_y, NOV)
                dve.sem_inc(ov_left, 1)

            def router_norm(l):
                norm(2 * l + 1, H, at(24576, 2, D), lambda i, j: VTT[:, i % 2, j * P:(j + 1) * P],
                     lambda i, j: gain_x[:, 2 * l + 1, j:j + 1], lambda i, j: mod[:, l, 3, j:j + 1])

            def final():
                dve.wait_ge(sq_done, norm_base[5])
                V.tensor_scalar(rstd[:, 0:TT], ss[:, 0:TT], 1.0 / D, EPS, ALU.mult, ALU.add).then_inc(ms_ready, 1)
                dve.wait_ge(root_ready, 5)
                link(V.reciprocal(rstd[:, 0:TT], rstd[:, 0:TT]))
                dve.wait_ge(small_in, SMALL0 + 64 * (DEPTH - 1) + 16)
                for i in range(TT):
                    V.scalar_tensor_tensor(out=H[:, i], in0=H[:, i], scalar=rstd[:, i:i + 1], in1=GF,
                                           op0=ALU.mult, op1=ALU.mult).then_inc(o_ready, 1)

            def combine(l):
                for i in range(TT):
                    dve.wait_ge(cy_full[i % NCY], 16 * (l * TT // NCY + i // NCY + 1))
                    link(V.tensor_tensor(H[:, i], H[:, i], CY[:, i % NCY, 0], ALU.add))
                    V.tensor_tensor(H[:, i], H[:, i], CY[:, i % NCY, 1], ALU.add).then_inc(cy_used, 1)

            def shortconv():
                for c in range(KC):
                    cx = CX[:, c % 2]
                    dve.wait_ge(bg_ready, 2 * c + 2)
                    dve.wait_ge(od_mm, 6 * c + 6)
                    link(V.tensor_tensor(cx, CONVT[:, c % 2], ps[:, 4:6, :].rearrange("p a b -> p (a b)"), ALU.mult))
                    dst = GTM[:, c]
                    link(conv(dst, cx, lambda w: cols[:, R_OD + 8 * w + c:R_OD + 8 * w + c + 1], None))
                    V.tensor_tensor(dst, dst, BGT[:, c % 2], ALU.mult).then_inc(od_conv, 1)

            for l in range(DEPTH):
                if l:
                    gate_rows(1)
                    norm(2, H, at(28672, 2, D), lambda i, j: U[:, j, i * P:(i + 1) * P],
                         lambda i, j: gain_x[:, 2, j:j + 1], lambda i, j: mod[:, 1, 0, j:j + 1])
                    shortconv()
                    residual(1, at(28672, 4, 512))
                router_norm(l)
                routing(l)
                experts(l)
                overflow(l)
                combine(l)
            final()


_INS = ['x', 'c', 'ctx', 'c_ctx', 'mod_w', 'mod_b', 'norm_mix', 'norm_ffn', 'norm_final', 'ev_w_in', 'ev_w_out',
        'gla_wa_f', 'gla_ba_f', 'gla_wa_b', 'gla_ba_b', 'gla_norm', 'hy_conv_w', 'hy_conv_b', 'hy_w1', 'hy_b1',
        'hy_f1', 'hy_w2', 'hy_b2', 'hy_f2', 'hy_w3', 'hy_skip', 'od_w_in', 'od_conv_w', 'od_w_out', 'rt_w_grp',
        'rt_b_grp', 'rt_w_exp', 'rt_b_exp', 'ex_w1', 'ex_w3', 'ex_w2']


def kernel(**inputs):
    import concourse.bacc as _bacc
    from concourse.bass_utils import run_bass_kernel_spmd as _run

    nc = _bacc.Bacc("TRN2", target_bir_lowering=False, num_devices=1)
    arrays, aps = {}, {}
    for name, value in [(n, inputs[n]) for n in _INS] + list(constants().items()):
        arr = np.ascontiguousarray(value)
        arrays[f"in_{name}_dram"] = arr
        aps[name] = nc.dram_tensor(f"in_{name}_dram", arr.shape, F32, kind="ExternalInput").ap()
    out = nc.dram_tensor("out_0_dram", (1, SEQ, D), F32, kind="ExternalOutput").ap()
    build(nc, aps, out)
    r = _run(nc, [arrays], core_ids=[0])
    return r.results[0]["out_0_dram"]
```
